# Optimizing a Trainium2 kernel written in Bass

```python
import math
import jax, jax.numpy as jnp
from jax import lax
import numpy as np

D_MODEL = 2048
BATCH = 1
SEQ = 256
DEPTH = 1

DIFF_HEADS = 8
DIFF_D = 64
NSA_HEADS = 8
NSA_KV = 2
NSA_GROUP = NSA_HEADS // NSA_KV
NSA_DK = 128
NSA_DV = 128
CMP_LEN = 32
CMP_STRIDE = 16
CMP_HIDDEN = 256
SLC_LEN = 64
SLC_TOPK = 16
WINDOW = 512
N_BUCKETS = 32
MAX_DISTANCE = 128
D_FF = 5632
CONV_W = 3
Q_BLOCK = 128
EPS = 1e-6
NEG = -1e30
FORCE = 1e30
TINY = 1e-30

DIFF_QK = DIFF_HEADS * 2 * DIFF_D
DIFF_V = DIFF_HEADS * 2 * DIFF_D
NSA_Q = NSA_HEADS * NSA_DK
NSA_K = NSA_KV * NSA_DK
NSA_V = NSA_KV * NSA_DV
N_GATES = NSA_HEADS * 3
SPLIT_SIZES = (DIFF_QK, DIFF_QK, DIFF_V, NSA_Q, NSA_K, NSA_V, NSA_K, NSA_V, NSA_K, NSA_V, N_GATES)
IN_COLS = 2 * DIFF_QK + DIFF_V + NSA_Q + 3 * (NSA_K + NSA_V) + N_GATES
MIX_WIDTH = DIFF_HEADS * 2 * DIFF_D + NSA_HEADS * NSA_DV


def rms_norm(x, g):
    xf = x.astype(jnp.float32)
    y = xf * lax.rsqrt(jnp.mean(xf * xf, axis=-1, keepdims=True) + EPS)
    return (y * g.astype(jnp.float32)).astype(x.dtype)

def rel_bucket(delta):
    n = jnp.maximum(delta, 0)
    max_exact = N_BUCKETS // 2
    nf = jnp.maximum(n, 1).astype(jnp.float32)
    large = max_exact + (jnp.log(nf / max_exact) / math.log(MAX_DISTANCE / max_exact)
                         * (N_BUCKETS - max_exact)).astype(jnp.int32)
    large = jnp.minimum(large, N_BUCKETS - 1)
    return jnp.where(n < max_exact, n, large)

def masked_softmax(s, mask):
    s = jnp.where(mask, s, NEG)
    m = jnp.max(s, axis=-1, keepdims=True)
    p = jnp.exp(s - m) * mask
    return p / jnp.maximum(jnp.sum(p, axis=-1, keepdims=True), TINY)

def selection_map(nb, nc):
    r = SLC_LEN // CMP_STRIDE
    j = np.arange(nb)[:, None, None]
    m = np.arange(r)[None, :, None]
    n = np.arange(CMP_LEN // CMP_STRIDE)[None, None, :]
    c = r * j - m - n
    jj = np.broadcast_to(j, c.shape)
    valid = (c >= 0) & (c < nc)
    out = np.zeros((nb, nc), np.float32)
    np.add.at(out, (jj[valid], c[valid]), 1.0)
    return out

def compress(k, pos_emb, w1, w2):
    B, S, G, d = k.shape
    nc = (S - CMP_LEN) // CMP_STRIDE + 1
    idx = jnp.arange(nc)[:, None] * CMP_STRIDE + jnp.arange(CMP_LEN)[None, :]
    blocks = k[:, idx] + pos_emb[:, None, :]
    blocks = jnp.transpose(blocks, (0, 3, 1, 2, 4)).reshape(B, G, nc, CMP_LEN * d)
    return jax.nn.gelu(blocks @ w1, approximate=True) @ w2

def diff_attention(q, k, v, lam, lam_init, subln, bias_tab):
    B, H, S, _, d = q.shape
    nblk = S // Q_BLOCK
    kpos = jnp.arange(S)
    scale = d ** -0.5

    def block(i):
        s0 = i * Q_BLOCK
        qb = lax.dynamic_slice_in_dim(q, s0, Q_BLOCK, axis=2)
        qpos = s0 + jnp.arange(Q_BLOCK)
        delta = qpos[:, None] - kpos[None, :]
        bias = jnp.transpose(bias_tab[rel_bucket(delta)], (2, 0, 1))
        logits = jnp.einsum('bhqmd,bhkmd->bhmqk', qb, k).astype(jnp.float32) * scale + bias[None, :, None]
        p = masked_softmax(logits, (delta >= 0)[None, None, None])
        a = p[:, :, 0] - lam * p[:, :, 1]
        return jnp.einsum('bhqk,bhke->bhqe', a.astype(v.dtype), v)

    o = lax.map(block, jnp.arange(nblk))
    o = jnp.transpose(o, (1, 2, 0, 3, 4)).reshape(B, H, S, 2 * d)
    return rms_norm(o, subln) * (1.0 - lam_init)

def nsa_attention(q, k_cmp, v_cmp, k_slc, v_slc, k_win, v_win, gates, bias_nsa):
    B, G, Hg, S, dk = q.shape
    nc = k_cmp.shape[2]
    nb = S // SLC_LEN
    topk = min(SLC_TOPK, nb)
    nsel = topk * SLC_LEN
    scale = dk ** -0.5
    sel_map = jnp.asarray(selection_map(nb, nc))
    cmp_end = jnp.arange(nc) * CMP_STRIDE + (CMP_LEN - 1)
    ks_blk = k_slc.reshape(B, G, nb, SLC_LEN, dk)
    vs_blk = v_slc.reshape(B, G, nb, SLC_LEN, -1)
    pad = ((0, 0), (0, 0), (WINDOW, 0), (0, 0))
    kw_pad = jnp.pad(k_win, pad)
    vw_pad = jnp.pad(v_win, pad)
    table_g = jnp.transpose(bias_nsa, (1, 0, 2))
    bi = jnp.arange(B)[:, None, None, None]
    gi = jnp.arange(G)[None, :, None, None]
    blk = jnp.arange(nb)

    def block(i):
        s0 = i * Q_BLOCK
        qb = lax.dynamic_slice_in_dim(q, s0, Q_BLOCK, axis=3)
        gb = lax.dynamic_slice_in_dim(gates, s0, Q_BLOCK, axis=3)
        qpos = s0 + jnp.arange(Q_BLOCK)
        lc = jnp.einsum('bghqd,bgcd->bghqc', qb, k_cmp).astype(jnp.float32) * scale
        pc = masked_softmax(lc, cmp_end[None, :] <= qpos[:, None])
        o_cmp = jnp.einsum('bghqc,bgcd->bghqd', pc.astype(v_cmp.dtype), v_cmp)
        imp = jnp.einsum('bgqc,jc->bgqj', jnp.sum(pc, axis=2), sel_map)
        cur = (qpos // SLC_LEN)[:, None]
        forced = (blk[None] == 0) | (blk[None] == cur) | (blk[None] == cur - 1)
        imp = jnp.where(forced, FORCE, jnp.where(blk[None] <= cur, imp, NEG))
        _, idx = lax.top_k(imp, topk)
        k_sel = ks_blk[bi, gi, idx].reshape(B, G, Q_BLOCK, nsel, dk)
        v_sel = vs_blk[bi, gi, idx].reshape(B, G, Q_BLOCK, nsel, -1)
        kpos_sel = (idx[..., None] * SLC_LEN + jnp.arange(SLC_LEN)).reshape(B, G, Q_BLOCK, nsel)
        d_sel = qpos[:, None] - kpos_sel
        b_sel = jnp.transpose(table_g[gi, rel_bucket(d_sel)], (0, 1, 4, 2, 3))
        ls = jnp.einsum('bghqd,bgqkd->bghqk', qb, k_sel).astype(jnp.float32) * scale + b_sel
        ps = masked_softmax(ls, (d_sel >= 0)[:, :, None])
        o_slc = jnp.einsum('bghqk,bgqkd->bghqd', ps.astype(v_sel.dtype), v_sel)
        kwb = lax.dynamic_slice_in_dim(kw_pad, s0, Q_BLOCK + WINDOW, axis=2)
        vwb = lax.dynamic_slice_in_dim(vw_pad, s0, Q_BLOCK + WINDOW, axis=2)
        kpos_w = s0 - WINDOW + jnp.arange(Q_BLOCK + WINDOW)
        d_w = qpos[:, None] - kpos_w[None, :]
        wmask = (d_w >= 0) & (d_w < WINDOW) & (kpos_w[None, :] >= 0)
        b_w = jnp.transpose(bias_nsa[rel_bucket(d_w)], (2, 3, 0, 1))
        lw = jnp.einsum('bghqd,bgkd->bghqk', qb, kwb).astype(jnp.float32) * scale + b_w
        pw = masked_softmax(lw, wmask)
        o_win = jnp.einsum('bghqk,bgkd->bghqd', pw.astype(vwb.dtype), vwb)
        return gb[..., 0:1] * o_cmp + gb[..., 1:2] * o_slc + gb[..., 2:3] * o_win

    o = lax.map(block, jnp.arange(S // Q_BLOCK))
    return jnp.transpose(o, (1, 2, 3, 0, 4, 5)).reshape(B, G, Hg, S, -1)

def causal_dwconv(u, w, b):
    S = u.shape[1]
    up = jnp.pad(u, ((0, 0), (CONV_W - 1, 0), (0, 0)))
    y = b
    for j in range(CONV_W):
        y = y + w[j] * up[:, j:j + S]
    return y

def first_inputs(seed: int = 0) -> dict:
    key = jax.random.key(seed)
    ks = jax.random.split(key, 24)
    f32 = jnp.float32

    def nrm(k, shape, scale):
        return jax.random.normal(k, shape, f32) * scale

    def gain(k, shape):
        return 1.0 + 0.05 * jax.random.normal(k, shape, f32)

    return {
        'x': nrm(ks[0], (BATCH, SEQ, D_MODEL), 1.0),
        'pre_mix_norm': gain(ks[1], (DEPTH, D_MODEL)),
        'w_in': nrm(ks[2], (DEPTH, D_MODEL, IN_COLS), D_MODEL ** -0.5),
        'lambda_q1': nrm(ks[3], (DEPTH, DIFF_D), 0.1),
        'lambda_k1': nrm(ks[4], (DEPTH, DIFF_D), 0.1),
        'lambda_q2': nrm(ks[5], (DEPTH, DIFF_D), 0.1),
        'lambda_k2': nrm(ks[6], (DEPTH, DIFF_D), 0.1),
        'diff_subln': gain(ks[7], (DEPTH, 2 * DIFF_D)),
        'cmp_pos_k': nrm(ks[8], (DEPTH, CMP_LEN, NSA_DK), 0.1),
        'cmp_pos_v': nrm(ks[9], (DEPTH, CMP_LEN, NSA_DV), 0.1),
        'cmp_k_w1': nrm(ks[10], (DEPTH, CMP_LEN * NSA_DK, CMP_HIDDEN), (CMP_LEN * NSA_DK) ** -0.5),
        'cmp_k_w2': nrm(ks[11], (DEPTH, CMP_HIDDEN, NSA_DK), CMP_HIDDEN ** -0.5),
        'cmp_v_w1': nrm(ks[12], (DEPTH, CMP_LEN * NSA_DV, CMP_HIDDEN), (CMP_LEN * NSA_DV) ** -0.5),
        'cmp_v_w2': nrm(ks[13], (DEPTH, CMP_HIDDEN, NSA_DV), CMP_HIDDEN ** -0.5),
        'rel_bias': nrm(ks[14], (N_BUCKETS, DIFF_HEADS + NSA_HEADS), 0.5),
        'w_out': nrm(ks[15], (DEPTH, MIX_WIDTH, D_MODEL), MIX_WIDTH ** -0.5),
        'post_mix_norm': gain(ks[16], (DEPTH, D_MODEL)),
        'pre_ffn_norm': gain(ks[17], (DEPTH, D_MODEL)),
        'w_up': nrm(ks[18], (DEPTH, D_MODEL, 2 * D_FF), D_MODEL ** -0.5),
        'conv_w': nrm(ks[19], (DEPTH, CONV_W, 2 * D_FF), CONV_W ** -0.5),
        'conv_b': nrm(ks[20], (DEPTH, 2 * D_FF), 0.01),
        'w_down': nrm(ks[21], (DEPTH, D_FF, D_MODEL), D_FF ** -0.5),
        'post_ffn_norm': gain(ks[22], (DEPTH, D_MODEL)),
    }

def first_block(x, pre_mix_norm, w_in, lambda_q1, lambda_k1, lambda_q2, lambda_k2, diff_subln,
              cmp_pos_k, cmp_pos_v, cmp_k_w1, cmp_k_w2, cmp_v_w1, cmp_v_w2, rel_bias, w_out,
              post_mix_norm, pre_ffn_norm, w_up, conv_w, conv_b, w_down, post_ffn_norm):
    B, S, _ = x.shape
    f32 = jnp.float32
    offsets = np.cumsum(SPLIT_SIZES)[:-1].tolist()
    bias_diff = rel_bias[:, :DIFF_HEADS]
    bias_nsa = rel_bias[:, DIFF_HEADS:].reshape(N_BUCKETS, NSA_KV, NSA_GROUP)
    for l in range(DEPTH):
        h = rms_norm(x, pre_mix_norm[l])
        proj = h @ w_in[l]
        (dq, dk, dv, nq, kc, vc, ksl, vsl, kwn, vwn, g) = jnp.split(proj, offsets, axis=-1)
        q_d = dq.reshape(B, S, DIFF_HEADS, 2, DIFF_D).transpose(0, 2, 1, 3, 4)
        k_d = dk.reshape(B, S, DIFF_HEADS, 2, DIFF_D).transpose(0, 2, 1, 3, 4)
        v_d = dv.reshape(B, S, DIFF_HEADS, 2 * DIFF_D).transpose(0, 2, 1, 3)
        lam_init = 0.8 - 0.6 * math.exp(-0.3 * l)
        lam = (jnp.exp(jnp.sum(lambda_q1[l].astype(f32) * lambda_k1[l].astype(f32)))
               - jnp.exp(jnp.sum(lambda_q2[l].astype(f32) * lambda_k2[l].astype(f32))) + lam_init)
        o_diff = diff_attention(q_d, k_d, v_d, lam, lam_init, diff_subln[l], bias_diff)
        q_n = nq.reshape(B, S, NSA_KV, NSA_GROUP, NSA_DK).transpose(0, 2, 3, 1, 4)
        k_c = compress(kc.reshape(B, S, NSA_KV, NSA_DK), cmp_pos_k[l], cmp_k_w1[l], cmp_k_w2[l])
        v_c = compress(vc.reshape(B, S, NSA_KV, NSA_DV), cmp_pos_v[l], cmp_v_w1[l], cmp_v_w2[l])
        k_s = ksl.reshape(B, S, NSA_KV, NSA_DK).transpose(0, 2, 1, 3)
        v_s = vsl.reshape(B, S, NSA_KV, NSA_DV).transpose(0, 2, 1, 3)
        k_w = kwn.reshape(B, S, NSA_KV, NSA_DK).transpose(0, 2, 1, 3)
        v_w = vwn.reshape(B, S, NSA_KV, NSA_DV).transpose(0, 2, 1, 3)
        gates = jax.nn.sigmoid(g.reshape(B, S, NSA_KV, NSA_GROUP, 3)).transpose(0, 2, 3, 1, 4)
        o_nsa = nsa_attention(q_n, k_c, v_c, k_s, v_s, k_w, v_w, gates, bias_nsa)
        mix = jnp.concatenate([o_diff.transpose(0, 2, 1, 3).reshape(B, S, -1),
                               o_nsa.transpose(0, 3, 1, 2, 4).reshape(B, S, -1)], axis=-1)
        x = x + rms_norm(mix @ w_out[l], post_mix_norm[l])
        h = rms_norm(x, pre_ffn_norm[l])
        u = causal_dwconv(h @ w_up[l], conv_w[l], conv_b[l])
        gate, up = jnp.split(u, 2, axis=-1)
        y = (jax.nn.gelu(gate, approximate=True) * up) @ w_down[l]
        x = x + rms_norm(y, post_ffn_norm[l])
    return x


ATTN_WIDTH = D_MODEL // 2
HEAD_DIM = 64
N_Q_HEADS = ATTN_WIDTH // HEAD_DIM
N_KV_HEADS = 2
GROUP = N_Q_HEADS // N_KV_HEADS
KV_WIDTH = N_KV_HEADS * HEAD_DIM
WINDOW_2 = 128
BLOCK = 128
RNN_WIDTH = D_MODEL - ATTN_WIDTH
RNN_HEAD_DIM = 128
N_RNN_HEADS = RNN_WIDTH // RNN_HEAD_DIM
CHUNK = 64
MIX_WIDTH_2 = ATTN_WIDTH + RNN_WIDTH
D_FF_2 = 4 * D_MODEL
IN_WIDTH = ATTN_WIDTH + 2 * KV_WIDTH + 4 * RNN_WIDTH
SPLITS = tuple(int(s) for s in np.cumsum([ATTN_WIDTH, KV_WIDTH, KV_WIDTH,
                                           RNN_WIDTH, RNN_WIDTH, RNN_WIDTH]))


def rmsnorm(x, gain):
    xf = x.astype(jnp.float32)
    y = xf * lax.rsqrt(jnp.mean(xf * xf, axis=-1, keepdims=True) + EPS)
    return (y * gain.astype(jnp.float32)).astype(x.dtype)

def alibi_slopes(n_heads):
    return jnp.exp2(-8.0 * jnp.arange(1, n_heads + 1, dtype=jnp.float32) / n_heads)

def sliding_window_attention(q, k, v, sinks):
    B, S, _ = q.shape
    nb = S // BLOCK
    qb = q.reshape(B, nb, BLOCK, N_KV_HEADS, GROUP, HEAD_DIM)
    kb = k.reshape(B, nb, BLOCK, N_KV_HEADS, HEAD_DIM)
    vb = v.reshape(B, nb, BLOCK, N_KV_HEADS, HEAD_DIM)
    pad = ((0, 0), (1, 0), (0, 0), (0, 0), (0, 0))
    kcat = jnp.concatenate([jnp.pad(kb, pad)[:, :-1], kb], axis=2)
    vcat = jnp.concatenate([jnp.pad(vb, pad)[:, :-1], vb], axis=2)
    scores = jnp.einsum('bnqhgd,bnkhd->bnhgqk', qb, kcat,
                        preferred_element_type=jnp.float32) * (HEAD_DIM ** -0.5)
    q_pos = jnp.arange(BLOCK) + BLOCK
    k_pos = jnp.arange(2 * BLOCK)
    dist = (q_pos[:, None] - k_pos[None, :]).astype(jnp.float32)
    band = (dist >= 0) & (dist < WINDOW_2)
    abs_k = jnp.arange(nb)[:, None] * BLOCK - BLOCK + k_pos[None, :]
    valid = band[None] & (abs_k >= 0)[:, None, :]
    slopes = alibi_slopes(N_Q_HEADS).reshape(N_KV_HEADS, GROUP, 1, 1)
    scores = scores - slopes * dist
    scores = jnp.where(valid[None, :, None, None], scores, -jnp.inf)
    sink = sinks.astype(jnp.float32).reshape(N_KV_HEADS, GROUP, 1, 1)
    m = jnp.maximum(jnp.max(scores, axis=-1, keepdims=True), sink)
    p = jnp.exp(scores - m)
    probs = p / (jnp.sum(p, axis=-1, keepdims=True) + jnp.exp(sink - m))
    out = jnp.einsum('bnhgqk,bnkhd->bnqhgd', probs.astype(v.dtype), vcat)
    return out.reshape(B, S, ATTN_WIDTH)

def hgrn2_chunkwise(q, f_logit, i, g, lb, norm_gain):
    B, S, _ = q.shape
    nc = S // CHUNK
    f32 = jnp.float32
    f = lb + (1.0 - lb) * jax.nn.sigmoid(f_logit.astype(f32))
    log_f = jnp.log(f)
    key = 1.0 - f
    qf = jax.nn.silu(q.astype(f32))
    vf = i.astype(f32)

    def to_chunks(t):
        return t.reshape(B, nc, CHUNK, N_RNN_HEADS, RNN_HEAD_DIM).transpose(1, 0, 3, 2, 4)

    causal = jnp.tril(jnp.ones((CHUNK, CHUNK), dtype=bool))

    def step(state, inp):
        qc, kc, vc, lfc = inp
        b = jnp.cumsum(lfc, axis=-2)
        o_inter = jnp.einsum('bhtk,bhkv->bhtv', qc * jnp.exp(b), state)
        diff = b[:, :, :, None, :] - b[:, :, None, :, :]
        decay = jnp.exp(jnp.where(causal[:, :, None], diff, -jnp.inf))
        att = jnp.einsum('bhtk,bhsk,bhtsk->bhts', qc, kc, decay)
        o_intra = jnp.einsum('bhts,bhsv->bhtv', att, vc)
        b_last = b[:, :, -1:, :]
        new_state = (jnp.exp(b_last[:, :, 0, :])[..., None] * state
                     + jnp.einsum('bhsk,bhsv->bhkv', kc * jnp.exp(b_last - b), vc))
        return new_state, o_inter + o_intra

    s0 = jnp.zeros((B, N_RNN_HEADS, RNN_HEAD_DIM, RNN_HEAD_DIM), f32)
    _, o = lax.scan(step, s0, (to_chunks(qf), to_chunks(key), to_chunks(vf), to_chunks(log_f)))
    o = o.transpose(1, 0, 3, 2, 4).reshape(B, S, N_RNN_HEADS, RNN_HEAD_DIM)
    o = o * lax.rsqrt(jnp.mean(o * o, axis=-1, keepdims=True) + EPS) * norm_gain.astype(f32)
    gate = jax.nn.silu(g.astype(f32)).reshape(B, S, N_RNN_HEADS, RNN_HEAD_DIM)
    return (o * gate).reshape(B, S, RNN_WIDTH).astype(q.dtype)

def second_inputs(seed: int = 0) -> dict:
    key = jax.random.key(seed)
    ks = jax.random.split(key, 14)
    f32 = jnp.float32

    def gain(k, shape):
        return 1.0 + 0.05 * jax.random.normal(k, shape, f32)

    return {
        "x": jax.random.normal(ks[0], (BATCH, SEQ, D_MODEL), f32),
        "w_in": jax.random.normal(ks[1], (DEPTH, D_MODEL, IN_WIDTH), f32) * D_MODEL ** -0.5,
        "attn_sinks": 0.5 * jax.random.normal(ks[2], (DEPTH, N_Q_HEADS), f32),
        "attn_out_gain": gain(ks[3], (DEPTH, ATTN_WIDTH)),
        "rnn_lb_logits": 0.1 * jax.random.normal(ks[4], (DEPTH + 1, RNN_WIDTH), f32),
        "rnn_norm_gain": gain(ks[5], (DEPTH, RNN_HEAD_DIM)),
        "w_out": jax.random.normal(ks[6], (DEPTH, MIX_WIDTH_2, D_MODEL), f32) * MIX_WIDTH_2 ** -0.5,
        "mix_pre_gain": gain(ks[7], (DEPTH, D_MODEL)),
        "mix_post_gain": gain(ks[8], (DEPTH, D_MODEL)),
        "mlp_pre_gain": gain(ks[9], (DEPTH, D_MODEL)),
        "mlp_post_gain": gain(ks[10], (DEPTH, D_MODEL)),
        "w_up": jax.random.normal(ks[11], (DEPTH, D_MODEL, D_FF_2), f32) * D_MODEL ** -0.5,
        "w_down": jax.random.normal(ks[12], (DEPTH, D_FF_2, D_MODEL), f32) * D_FF_2 ** -0.5,
    }

def second_block(x, w_in, attn_sinks, attn_out_gain, rnn_lb_logits, rnn_norm_gain, w_out,
              mix_pre_gain, mix_post_gain, mlp_pre_gain, mlp_post_gain, w_up, w_down):
    lb_all = jnp.cumsum(jax.nn.softmax(rnn_lb_logits.astype(jnp.float32), axis=0), axis=0)
    for layer in range(DEPTH):
        h = rmsnorm(x, mix_pre_gain[layer])
        proj = jnp.einsum('bsd,de->bse', h, w_in[layer])
        q_a, k_a, v_a, q_r, f_r, i_r, g_r = jnp.split(proj, SPLITS, axis=-1)
        attn = sliding_window_attention(q_a, k_a, v_a, attn_sinks[layer])
        attn = rmsnorm(attn, attn_out_gain[layer])
        rnn = hgrn2_chunkwise(q_r, f_r, i_r, g_r, lb_all[layer], rnn_norm_gain[layer])
        mixed = jnp.einsum('bse,ed->bsd', jnp.concatenate([attn, rnn], axis=-1), w_out[layer])
        x = x + rmsnorm(mixed, mix_post_gain[layer])
        h = rmsnorm(x, mlp_pre_gain[layer])
        u = jax.nn.relu(jnp.einsum('bsd,df->bsf', h, w_up[layer]))
        y = jnp.einsum('bsf,fd->bsd', u * u, w_down[layer])
        x = x + rmsnorm(y, mlp_post_gain[layer])
    return x


def setup_inputs(seed=0):
    out = dict(first_inputs(seed))
    for name, value in second_inputs(seed + 1).items():
        if name != "x":
            out[name + "_2"] = value
    return out


def reference(
    x, pre_mix_norm, w_in, lambda_q1, lambda_k1, lambda_q2, lambda_k2, diff_subln, cmp_pos_k,
    cmp_pos_v, cmp_k_w1, cmp_k_w2, cmp_v_w1, cmp_v_w2, rel_bias, w_out, post_mix_norm,
    pre_ffn_norm, w_up, conv_w, conv_b, w_down, post_ffn_norm, w_in_2, attn_sinks_2,
    attn_out_gain_2, rnn_lb_logits_2, rnn_norm_gain_2, w_out_2, mix_pre_gain_2, mix_post_gain_2,
    mlp_pre_gain_2, mlp_post_gain_2, w_up_2, w_down_2,
):
    x = first_block(
        x, pre_mix_norm, w_in, lambda_q1, lambda_k1, lambda_q2, lambda_k2, diff_subln,
        cmp_pos_k, cmp_pos_v, cmp_k_w1, cmp_k_w2, cmp_v_w1, cmp_v_w2, rel_bias, w_out,
        post_mix_norm, pre_ffn_norm, w_up, conv_w, conv_b, w_down, post_ffn_norm,
    )
    return second_block(
        x, w_in_2, attn_sinks_2, attn_out_gain_2, rnn_lb_logits_2, rnn_norm_gain_2, w_out_2,
        mix_pre_gain_2, mix_post_gain_2, mlp_pre_gain_2, mlp_post_gain_2, w_up_2, w_down_2,
    )


_drawn_inputs = setup_inputs


def setup_inputs(seed=0):
    import zlib

    import numpy as np

    out = dict(_drawn_inputs(seed))
    spreads = {}
    factors = {'lambda_q2': 8.0,
     'cmp_pos_k': 8.0,
     'conv_b': 5.884,
     'rnn_lb_logits_2': 8.0,
     'rnn_norm_gain_2': 3.908}
    for name, (base, spread) in spreads.items():
        noise = np.random.default_rng([zlib.crc32(name.encode()), seed]).standard_normal(out[name].shape)
        drawn = base * np.exp(spread * noise) if base else spread * noise
        out[name] = __import__('jax').numpy.asarray(drawn.astype(out[name].dtype))
    for name, factor in factors.items():
        out[name] = (out[name] * factor).astype(out[name].dtype)
    return out
```

```python
import math

import numpy as np

import concourse.bass as bass
from concourse import mybir
from contextlib import ExitStack

F32 = mybir.dt.float32
F32R = mybir.dt.float32r
ALU = mybir.AluOpType
ACT = mybir.ActivationFunctionType
AX = mybir.AxisListType

P = 128
D = 2048
S = 256
TT = S // P
KC = D // P
EPS = 1e-6
NEG = -1e30
TINY = 1e-30

HD = 8
HN = 8
NKV = 2
GATES = HN * 3
NB_BUCKETS = 32
CMP_LEN, CMP_STRIDE, HID = 32, 16, 256
NC = (S - CMP_LEN) // CMP_STRIDE + 1
LAM_INIT = 0.8 - 0.6 * math.exp(0.0)
C_DQ, C_DK, C_DV, C_NQ = 0, 1024, 2048, 3072
C_KC, C_VC, C_KS, C_VS, C_KW, C_VW, C_G = 4096, 4352, 4608, 4864, 5120, 5376, 5632
IN1 = C_G + GATES
F1 = 5632
F2 = 8192
HA, HR = 16, 8
C_QA, C_KA, C_VA, C_QR, C_FR, C_IR, C_GR = 0, 1024, 1152, 1280, 2304, 3328, 4352
IN2 = 5376
SK = 384
LEVELS = (64, 32, 16, 8, 4, 2, 1)

STAGES = 8
SPLITS = 4
TILE = 1024
NW = 512
TC = TILE // NW
FW = 256
FC = TILE // FW
FT = 2 * KC // FC


class Gemm:

    def __init__(self, kind, first, blocks, tiles, acc=0):
        self.kind, self.first, self.blocks, self.tiles, self.acc = kind, first, blocks, tiles, acc


def plan():
    out, n, acc, up = {}, 0, 0, 0
    order = [("in1", "tok", 12, 8), ("cmp", "raw", 1, 16), ("out1", "tok", 4, 8),
             ("up1a", "feat", 12, FT), ("down1a", "tok", 4, 12), ("up1b", "feat", 10, FT), ("down1b", "tok", 4, 10),
             ("in2", "tok", 11, 8), ("out2", "tok", 4, 8),
             ("up2a", "feat", 8, FT), ("down2a", "tok", 4, 16), ("up2b", "feat", 8, FT), ("down2b", "tok", 4, 16)]
    for name, kind, blocks, tiles in order:
        out[name] = Gemm(kind, n, blocks, tiles, up if kind == "feat" else acc)
        assert n % STAGES == 0
        n += blocks * tiles
        if kind == "tok":
            acc += blocks
        if kind == "feat":
            up += blocks
    return out


def buckets(d):
    half = NB_BUCKETS // 2
    if d < half:
        return d
    return min(half + int(math.log(d / half) / math.log(128 / half) * half), NB_BUCKETS - 1)


def shape_constants():
    i = np.arange(P)
    c = {}
    c["ident"] = np.eye(P, dtype=np.float32)
    c["flip"] = np.eye(P, dtype=np.float32)[::-1].copy()
    onehot = np.zeros((NB_BUCKETS, SK), np.float32)
    for m in range(S):
        onehot[buckets(S - 1 - m), m] = 1.0
    c["onehot"] = onehot
    far = np.full((P, SK), 1e34, np.float32)
    for q in range(P):
        for lo, hi, off in ((0, 128, 0), (128, 256, 256), (256, 384, 256)):
            for col in range(lo, hi):
                d = off + q - col if lo != 0 else q - col
                if 0 <= d < P:
                    far[q, col] = d
    c["far"] = far
    ends = np.zeros((P, TT, NC), np.float32)
    for t in range(TT):
        for n in range(NC):
            ends[:, t, n] = (n * CMP_STRIDE + CMP_LEN - 1 <= t * P + i)
    c["cmp_keep"] = ends
    c["cmp_drop"] = ((1.0 - ends) * NEG).astype(np.float32)
    sums = np.zeros((P, 9, P), np.float32)
    keep = np.zeros((P, 8, P), np.float32)
    u, t = i[:, None], i[None, :]
    for n, ln in enumerate(LEVELS):
        mid = t // (2 * ln) * (2 * ln) + ln
        sums[:, n, :] = np.where(t >= mid, (u >= mid) & (u <= t), (u > t) & (u < mid))
        same = u // (2 * ln) == t // (2 * ln)
        keep[:, n, :] = same & (u % (2 * ln) < ln) & (t % (2 * ln) >= ln)
    sums[:, 7, :] = u > t
    sums[:, 8, :] = u <= t
    keep[:, 7, :] = u == t
    c["sums"] = sums
    c["keep"] = keep
    return c


def layout(a):
    return a


def build(nc, w, out, scratch):
    G = plan()
    ctx = ExitStack()
    sems = {}

    def ev(name):
        if name not in sems:
            sems[name] = ctx.enter_context(nc.semaphore(name))
        return sems[name]

    with ctx:
        def sb(name, shape, dt=F32, on=ctx):
            return on.enter_context(nc.sbuf_tensor(name, shape, dt))

        stage = sb("stage", [P, STAGES, TILE])
        whi = sb("whi", [P, SPLITS, TILE], F32R)
        wlo = sb("wlo", [P, SPLITS, TILE], F32R)
        x = sb("x", [P, TT, D])
        ident = sb("ident", [P, P])
        grow = sb("grow", [P, D])
        cols = sb("cols", [P, 96])
        posT = sb("posT", [P, 2, CMP_LEN])
        convT = sb("convT", [P, 4, 2 * F1 // P])
        small = sb("small", [P, 24])
        hstat = sb("hstat", [P, 3, 16])
        lbs = sb("lbs", [P, 48])
        half = sb("half", [P, 1])
        stat = sb("stat", [P, 2, 16])
        here = ExitStack()
        actT = sb("actT", [P, KC, 2 * S], F32R, here)
        here.close()
        mixer1 = ExitStack()
        QT = sb("QT", [P, 32, S], F32, mixer1)
        proj = sb("proj", [P, TT, IN1], F32, mixer1)
        bias = sb("bias", [P, 16, SK], F32, mixer1)
        work = sb("work", [P, 3072], F32, mixer1)
        gates = sb("gates", [P, TT, GATES], F32, mixer1)
        mixer1.close()
        scores = work[:, 0:4 * SK].rearrange("p (a m k) -> p a m k", a=2, m=2)
        probs = work[:, 4 * SK:6 * SK].rearrange("p (a k) -> p a k", a=2)
        probsT = work[:, 6 * SK:8 * SK].rearrange("p (a k) -> p a k", a=2)
        flat = proj[:, :, :].rearrange("p t n -> p (t n)")
        hankel = flat[:, 4096:8192].rearrange("p (h j) -> p h j", h=16)
        vecs = flat[:, 8192:8192 + 6 * P].rearrange("p (r j) -> p r j", r=6)
        lamv = work[:, 0:256].rearrange("p (a c) -> p a c", a=4)
        tab = work[0:NB_BUCKETS, 512:528]
        hot = work[0:NB_BUCKETS, 1024:1024 + SK]
        flip = work[:, 1536:1664]
        urow = work[0:16, 2048:2048 + SK]
        blocks = grow[:, 0:2 * CMP_LEN * NKV * NC].rearrange("p (v l g c) -> p v l g c", v=2, l=CMP_LEN, g=NKV)
        w2 = proj[:, 0, C_KC:C_KC + 512].rearrange("p (v a n) -> p v a n", v=2, a=2)
        hid = proj[:, 1, C_KC:C_KC + 4 * 2 * NC].rearrange("p (v a c) -> p v a c", v=2, a=2)
        kcT = proj[:, 1, C_KC + 128:C_KC + 128 + 2 * NC]
        vc = proj[0:NC, 1, C_KC + 192:C_KC + 192 + NKV * P].rearrange("p (g d) -> p g d", g=NKV)
        pcs = proj[:, 0, C_DK:C_DK + HN * TT * NC].rearrange("p (h t c) -> p h t c", h=HN, t=TT)
        keepc = proj[:, 0, C_DK + 256:C_DK + 256 + 2 * TT * NC].rearrange("p (a t c) -> p a t c", a=2, t=TT)
        cst = proj[:, 0, C_DK + 384:C_DK + 384 + 3 * HN * TT].rearrange("p (a h t) -> p a h t", a=3, h=HN)
        pcT = work[0:NC, 0:2048].rearrange("p (n q) -> p n q", n=HN * TT)
        mixer2 = ExitStack()
        QT2 = sb("QT2", [P, 32, S], F32, mixer2)
        proj2 = sb("proj2", [P, TT, IN2], F32, mixer2)
        far = sb("far", [P, SK], F32, mixer2)
        scores2 = sb("scores2", [P, 2, SK], F32, mixer2)
        probsT2 = sb("probsT2", [P, 2, SK], F32, mixer2)
        sinks = sb("sinks", [P, 2, HA], F32, mixer2)
        sums = sb("sums", [P, 9, P], F32, mixer2)
        keep = sb("keep", [P, 8, P], F32, mixer2)
        logf = sb("logf", [P, TT, HR, P], F32, mixer2)
        fackf = sb("fackf", [P, 2, 8, P], F32, mixer2)
        kcross = sb("kcross", [P, P], F32, mixer2)
        attT = sb("attT", [P, P], F32, mixer2)
        crossT = sb("crossT", [P, P], F32, mixer2)
        mixer2.close()
        kdup = QT2[:, 10:12, :].rearrange("p t (v u d) -> p t v u d", v=NKV, u=2)
        fac = fackf[:, 0, :, :]
        kf = fackf[:, 1, :, :]
        attm = proj2[:, 0, C_QR:C_QR + 1024].rearrange("p (l t) -> p l t", l=8)
        qf = proj2[:, 1, C_QR:C_QR + 1024].rearrange("p (l t) -> p l t", l=8)
        sig_q = logf[:, :, :, :].rearrange("p t h k -> p (t h k)").rearrange("p (h s) -> p h s", h=HR)
        lnf = fackf[:, :, :, :].rearrange("p a l t -> p (a l t)").rearrange("p (h s) -> p h s", h=HR)
        sig_g = fackf[:, :, :, :].rearrange("p a l t -> p a (l t)")
        ffn = ExitStack()
        sb("actT_place", [P, KC, 2 * S], F32R, ffn)
        yacc = sb("yacc", [P, TT, D], F32, ffn)
        both = ExitStack()
        gT1 = sb("gT1", [P, 24, 2 * S], F32R, both)
        pre = sb("pre", [P, 4, S + 2], F32, both)
        both.close()
        gT2 = sb("gT2", [P, 32, 2 * S], F32R, ffn)
        ffn.close()
        lowsum = grow[:, 0:4 * S].rearrange("p (a s) -> p a s", a=4)
        post = grow[:, 4 * S:8 * S].rearrange("p (a s) -> p a s", a=4)

        PS = ctx.enter_context(nc.psum_tensor("PS", [P, 8, 512], F32))

        ln = {"dve": 0, "act": 0, "pool": 0}

        def then(eng, name, ins):
            ln[name] += 1
            ins.then_inc(ev("self_" + name), 1)
            eng.wait_ge(ev("self_" + name), ln[name])

        GAIN = {"n1": 0, "n2": 16, "n3": 32, "n4": 48, "attn": 64, "subln": 72, "rnn": 73, "one": 74}
        C_LB = 76

        def gain_of(turn, c):
            if turn == "mix1":
                at = GAIN["subln"] if c < HD else GAIN["one"]
            elif turn == "mix2":
                at = GAIN["attn"] + c if c < 8 else GAIN["rnn"]
            else:
                at = GAIN[turn] + c
            return cols[:, at:at + 1]

        def src_of(turn, t, c):
            if turn == "mix1":
                at = C_DQ + c * P if c < HD else C_NQ + (c - HD) * P
                return proj[:, t, at:at + P]
            if turn == "mix2":
                at = C_QA + c * P if c < 8 else C_IR + (c - 8) * P
                return proj2[:, t, at:at + P]
            return yacc[:, t, c * P:(c + 1) * P]

        WT = {"in1": (w["w_in"][0], 0), "out1": (w["w_out"][0], 0),
              "down1a": (w["w_down"][0], 0), "down1b": (w["w_down"][0], 24),
              "in2": (w["w_in_2"][0], 0), "out2": (w["w_out_2"][0], 0),
              "down2a": (w["w_down_2"][0], 0), "down2b": (w["w_down_2"][0], 32)}
        UP = {"up1a": (w["w_up"][0], 0, F1, 256), "up1b": (w["w_up"][0], 12 * 256, F1, 256),
              "up2a": (w["w_up_2"][0], 0, 256, 512), "up2b": (w["w_up_2"][0], 8 * 512, 256, 512)}
        PAIRS = {"in1": 5, "out1": 2, "down1a": 2, "down1b": 0, "in2": 5, "out2": 2, "down2a": 2, "down2b": 2}
        WIDTH = {("in1", 11): GATES, ("in2", 10): 256}

        def width(name, b):
            return WIDTH.get((name, b), NW)

        def used(n):
            return n + SPLITS

        def tok_order(eng, name, tile, take):
            g, pairs = G[name], PAIRS[name]
            T = g.tiles

            def one(i, b, base, prev):
                for j in range(T):
                    tile(i, b, j, base + j)
                    if j == SPLITS - 1 and prev is not None and take is not None:
                        take(*prev)
            if pairs:
                for b in range(2):
                    one(0, b, g.first + b * T, (0, 0) if b else None)
                with eng.Fori(1, pairs) as i:
                    for b in range(2):
                        one(i, b, i * (2 * T) + (g.first + b * T), (i, 0) if b else (i - 1, 1))
            for b in range(2 * pairs, g.blocks):
                one(None, b, g.first + b * T, (None, b - 1) if b else None)
            if take is not None:
                take(None, g.blocks - 1)

        def place(name, i, b):
            if i is None:
                return b * NW, b, b % 2, width(name, b)
            return i * (2 * NW) + b * NW, i * 2 + b, b, NW

        def span(start, size):
            return slice(start, start + size) if isinstance(start, int) else bass.ds(start, size)

        def turn_at(name, i, s):
            g = G[name]
            k = (g.first + s) // STAGES + 1
            return 16 * k if i is None else i * (2 * g.tiles // STAGES * 16) + 16 * k

        block = ctx.enter_context(nc.Block())

        @block.sync
        def _(sp):
            def tile_in(slot, n, src, dst):
                sp.wait_ge(ev("lo_done"), n + 1)
                sp.dma_start(dst, src).then_inc(ev(f"landed{slot}"), 16)

            def tok_block(name, i, b, base):
                m, k0 = WT[name]
                col, _, _, wd = place(name, i, b)
                for j in range(G[name].tiles):
                    k = k0 + TC * j
                    slot = (b * G[name].tiles + j) % STAGES
                    tile_in(slot, base + j, m[k * P:(k + TC) * P, span(col, wd)].rearrange("(c p) n -> p c n", p=P),
                            stage[:, slot, 0:TC * wd].rearrange("p (c n) -> p c n", c=TC))

            def tok(name):
                g = G[name]
                if PAIRS[name]:
                    with sp.Fori(0, PAIRS[name]) as i:
                        for b in range(2):
                            tok_block(name, i, b, i * (2 * g.tiles) + (g.first + b * g.tiles))
                for b in range(2 * PAIRS[name], g.blocks):
                    tok_block(name, None, b, g.first + b * g.tiles)

            def feat(name):
                m, c0, other, step = UP[name]
                with sp.Fori(0, G[name].blocks) as i:
                    for j in range(FT):
                        q, kh = j // (FT // 2), j % (FT // 2)
                        src = m[kh * FC * P:(kh + 1) * FC * P, bass.ds(i * step + (c0 + q * other), FW)]
                        tile_in(j, i * FT + (G[name].first + j), src.rearrange("(c p) n -> p c n", p=P),
                                stage[:, j, :].rearrange("p (c n) -> p c n", c=FC))

            tok("in1")
            for j in range(G["cmp"].tiles):
                m = (w["cmp_k_w1"], w["cmp_v_w1"])[j // 8][0]
                r = (j % 8) * FC * P
                tile_in(j % STAGES, G["cmp"].first + j, m[r:r + FC * P, :].rearrange("(c p) n -> p c n", p=P),
                        stage[:, j % STAGES, :].rearrange("p (c n) -> p c n", c=FC))
            tok("out1")
            feat("up1a")
            tok("down1a")
            feat("up1b")
            tok("down1b")
            tok("in2")
            tok("out2")
            feat("up2a")
            tok("down2a")
            feat("up2b")
            tok("down2b")
            for t in range(TT):
                sp.wait_ge(ev("resid"), 3 * TT + t + 1)
                sp.dma_start(out[0, t * P:(t + 1) * P, :], x[:, t, :]).then_inc(ev("stored"), 16)
            sp.wait_ge(ev("stored"), 16 * TT)

        @block.gpsimd
        def _(pool):
            pool.dma_start(x[:, :, :], w["x"][0].rearrange("(t p) n -> p t n", p=P)).then_inc(ev("x_in"), 16)
            pool.dma_start(tab, w["rel_bias"]).then_inc(ev("tab_in"), 16)
            pool.dma_start(hot, w["onehot"]).then_inc(ev("tab_in"), 16)
            pool.dma_start(ident[:, :], w["ident"]).then_inc(ev("ident_in"), 16)
            pool.dma_start(flip, w["flip"]).then_inc(ev("ident_in"), 16)
            for r0, nm, k in ((0, "pre_mix_norm", 16), (16, "pre_ffn_norm", 16), (32, "mix_pre_gain_2", 16),
                              (48, "mlp_pre_gain_2", 16), (64, "attn_out_gain_2", 8), (72, "diff_subln", 1),
                              (73, "rnn_norm_gain_2", 1)):
                pool.dma_start(vecs[r0:r0 + k, 0, :], w[nm][0].rearrange("(r f) -> r f", f=P)).then_inc(ev("vecs_in"), 16)
            pool.dma_start(vecs[74:90, 0, :], w["rnn_lb_logits_2"].rearrange("l (r f) -> (l r) f", f=P)).then_inc(ev("vecs_in"), 16)
            pool.dma_start(vecs[0:CMP_LEN, 1, :], w["cmp_pos_k"][0]).then_inc(ev("vecs_in"), 16)
            pool.dma_start(vecs[CMP_LEN:2 * CMP_LEN, 1, :], w["cmp_pos_v"][0]).then_inc(ev("vecs_in"), 16)
            for j in range(3):
                pool.dma_start(vecs[0:88, 2 + j, :], w["conv_w"][0, j].rearrange("(r f) -> r f", f=P)).then_inc(ev("vecs_in"), 16)
            pool.dma_start(vecs[0:88, 5, :], w["conv_b"][0].rearrange("(r f) -> r f", f=P)).then_inc(ev("vecs_in"), 16)
            for j, nm in enumerate(("lambda_q1", "lambda_q2", "lambda_k1", "lambda_k2")):
                pool.dma_start(lamv[:, j, :], w[nm][0:1, :].broadcast_to((P, 64))).then_inc(ev("lam_in"), 16)
            pool.memset(half[:, :], -0.5).then_inc(ev("half_set"), 1)
            pool.wait_ge(ev("urow"), 2)
            pool.dma_start(scratch, urow).then_inc(ev("scratch_out"), 16)
            pool.wait_ge(ev("scratch_out"), 16)
            pool.dma_start(hankel, bass.AP(scratch.tensor, 0, [[1, P], [SK, 16], [1, S]])).then_inc(ev("hankel_in"), 16)
            pool.wait_ge(ev("half_set"), 1)

            def inv_sqrt(n, dst, src, k):
                pool.wait_ge(ev("var"), n)
                pool.tensor_tensor(dst, src, half[:, 0:1].broadcast_to((P, k)), ALU.pow).then_inc(ev("rstd"), 1)

            inv_sqrt(1, small[:, 4:6], small[:, 2:4], 2)
            pool.wait_ge(ev("qt_a"), 8)
            pool.wait_ge(ev("qt_d"), 8)
            for j, nm in enumerate(("cmp_k_w2", "cmp_v_w2")):
                pool.dma_start(w2[:, j, :, :], w[nm][0].rearrange("(a p) n -> p a n", p=P)).then_inc(ev("w2_in"), 16)
            pool.dma_start(keepc[:, 0, :, :], w["cmp_keep"]).then_inc(ev("keep_in"), 16)
            pool.dma_start(keepc[:, 1, :, :], w["cmp_drop"]).then_inc(ev("keep_in"), 16)
            pool.wait_ge(ev("cols"), 1)
            for v in range(2):
                for g in range(NKV):
                    for a in range(2):
                        src = QT[:, 24 + 2 * v + g, 16 * a:16 * a + 16 * NC].rearrange("p (c b) -> p b c", b=16)
                        add = posT[:, v, 16 * a:16 * a + 16].rearrange("p (b o) -> p b o", o=1).broadcast_to((P, 16, NC))
                        pool.tensor_tensor(blocks[:, v, 16 * a:16 * a + 16, g, :], src, add, ALU.add).then_inc(ev("blocks_done"), 1)
            pool.wait_ge(ev("hid_mm"), 2)
            pool.dma_start(grow[:, :], w["post_mix_norm"][0:1, :].broadcast_to((P, D))).then_inc(ev("grow_in"), 16)
            inv_sqrt(2, hstat[:, 2, :], hstat[:, 1, :], 16)
            inv_sqrt(3, small[:, 4:6], small[:, 2:4], 2)
            inv_sqrt(4, small[:, 4:6], small[:, 2:4], 2)
            pool.wait_ge(ev("g_lo"), 1 + 22)
            pool.dma_start(grow[:, :], w["post_ffn_norm"][0:1, :].broadcast_to((P, D))).then_inc(ev("grow_in"), 16)
            inv_sqrt(5, small[:, 4:6], small[:, 2:4], 2)
            pool.wait_ge(ev("resid"), 4)
            pool.dma_start(grow[:, :], w["mix_post_gain_2"][0:1, :].broadcast_to((P, D))).then_inc(ev("grow_in"), 16)
            pool.dma_start(far[:, :], w["far"]).then_inc(ev("mix2_in"), 16)
            pool.dma_start(sinks[:, 0, :], w["attn_sinks_2"][0:1, :].broadcast_to((P, HA))).then_inc(ev("mix2_in"), 16)
            pool.dma_start(sums[:, :, :], w["sums"]).then_inc(ev("mix2_in"), 16)
            pool.dma_start(keep[:, :, :], w["keep"]).then_inc(ev("mix2_in"), 16)
            inv_sqrt(6, small[:, 4:6], small[:, 2:4], 2)
            pool.wait_ge(ev("key_done"), 1)
            for n in range(HR * TT):
                h, t = n // TT, n % TT
                key = QT2[:, 24 + h, t * P:(t + 1) * P]
                pool.wait_ge(ev("fac"), n + 1)
                if t == 0:
                    if h >= 1:
                        pool.wait_ge(ev("cross_mm"), h)
                    pool.tensor_tensor(kcross[:, :], fac[:, 7, :], key, ALU.mult).then_inc(ev("kcross_done"), 1)
                if n >= 1:
                    pool.wait_ge(ev("att_mm"), n)
                many = key.rearrange("p (o t) -> p o t", o=1).broadcast_to((P, 7, P))
                pool.tensor_tensor(kf[:, 0:7, :], fac[:, 0:7, :], many, ALU.mult).then_inc(ev("kf"), 1)
            inv_sqrt(7, small[:, 4:6], small[:, 2:4], 2)
            inv_sqrt(8, hstat[:, 2, :], hstat[:, 1, :], 16)
            inv_sqrt(9, small[:, 4:6], small[:, 2:4], 2)
            inv_sqrt(10, small[:, 4:6], small[:, 2:4], 2)
            pool.wait_ge(ev("g_lo"), 1 + 22 + 16)
            pool.dma_start(grow[:, :], w["mlp_post_gain_2"][0:1, :].broadcast_to((P, D))).then_inc(ev("grow_in"), 16)
            inv_sqrt(11, small[:, 4:6], small[:, 2:4], 2)

        NBR = HD + 2 * HN
        TURN2 = [0, 1, 2, 3, 4, 8, 9, 10, 11, 12, 13, 14, 15]

        @block.scalar
        def _(act):
            squares = [PS[:, 4 * t:4 * t + 4, :].rearrange("p b n -> p (b n)") for t in range(TT)]

            def tok(name, dst):
                g = G[name]

                def tile(i, b, j, n):
                    s = b * g.tiles + j
                    wd = TC * (width(name, b) if i is None else NW)
                    act.wait_ge(ev("tile_used"), used(n - SPLITS + 1))
                    act.wait_ge(ev(f"landed{s % STAGES}"), turn_at(name, i, s))
                    nc.scalar.activation(whi[:, s % SPLITS, 0:wd], stage[:, s % STAGES, 0:wd], ACT.Copy)\
                        .then_inc(ev("hi_done"), 1)

                def take(i, b):
                    col, nb, bank, wd = place(name, i, b)
                    act.wait_ge(ev("tile_used"), used((nb + 1) * g.tiles + g.first))
                    act.wait_ge(ev("begun"), 1)
                    for t in range(TT):
                        last = nc.scalar.activation(dst[:, t, span(col, wd)], PS[:, 2 * bank + t, 0:wd], ACT.Copy)
                    last.then_inc(ev("acc_free"), 1)
                tok_order(act, name, tile, take if dst is not None else None)
                if dst is not None:
                    act.wait_ge(ev("acc_free"), 2 + g.acc + g.blocks)

            def sum_squares(src, junk=None):
                for t in range(TT):
                    last = nc.scalar.activation(squares[t] if junk is None else junk[:, t, :], src[:, t, :], ACT.Square, accum_out=small[:, t:t + 1])
                last.then_inc(ev("ssq"), 1)

            def split_turned(turn):
                for c in range(KC):
                    act.wait_ge(ev("turned_" + turn), c // 2 + 1)
                    nc.scalar.activation(actT[:, c, 0:S], PS[:, c // 2, (c % 2) * S:(c % 2 + 1) * S], ACT.Copy,
                                         scale=gain_of(turn, c)).then_inc(ev("acthi_" + turn), 1)

            def feat(name, conv):
                g = G[name]
                gT = gT1 if conv else gT2

                def tiles(i, js):
                    for j in js:
                        act.wait_ge(ev("tile_used"), used(i * FT + (g.first + j - SPLITS + 1)))
                        act.wait_ge(ev(f"landed{j}"), i * 16 + (g.first // STAGES + 1) * 16)
                        nc.scalar.activation(whi[:, j % SPLITS, :], stage[:, j, :], ACT.Copy).then_inc(ev("hi_done"), 1)

                def low_sums(i, s):
                    act.wait_ge(ev("tile_used"), used(i * FT + (g.first + FT)))
                    nc.scalar.activation(lowsum, PS[:, 4 * s:4 * s + 4, S:2 * S], ACT.Copy).then_inc(ev("low_out"), 1)

                def first_tap(i):
                    act.wait_ge(ev("g_lo"), i + (g.acc + 1))
                    act.wait_ge(ev("pre_done"), i + (g.acc + 3))
                    act.wait_ge(ev("begun"), 1)
                    for a in range(4):
                        f = i * 2 + (2 * (g.acc if name == "up1b" else 0) + a % 2 + F1 // P * (a // 2))
                        nc.scalar.activation(post[:, a, :], pre[:, a, 2:2 + S], ACT.Identity,
                                             scale=convT[:, 2, span(f, 1)], bias=convT[:, 3, span(f, 1)])\
                            .then_inc(ev("tap"), 1)

                def high_parts(i):
                    if conv:
                        act.wait_ge(ev("conv_done"), i + (g.acc + 1))
                        nc.scalar.activation(lowsum[:, 0:2, :], post[:, 0:2, :], ACT.Gelu_apprx_tanh).then_inc(ev("gelu"), 1)
                    k = 2 if conv else 4
                    act.wait_ge(ev("prod"), i + (g.acc + 1))
                    act.wait_ge(ev("begun"), 1)
                    nc.scalar.activation(gT[:, span(i * k, k), 0:S], post[:, 0:k, :], ACT.Copy).then_inc(ev("g_hi"), 1)

                def one(i, s, prev):
                    tiles(i, (0, 1, 2, 3))
                    if prev is not None:
                        low_sums(prev, 1 - s)
                        if conv:
                            first_tap(prev)
                    tiles(i, (4, 5))
                    if prev is not None:
                        high_parts(prev)
                    tiles(i, (6, 7))
                one(0, 0, None)
                one(1, 1, 0)
                with act.Fori(1, g.blocks // 2) as r:
                    one(r * 2, 0, r * 2 - 1)
                    one(r * 2 + 1, 1, r * 2)
                low_sums(g.blocks - 1, 1)
                if conv:
                    first_tap(g.blocks - 1)
                high_parts(g.blocks - 1)

            act.sem_inc(ev("begun"), 1)
            act.wait_ge(ev("x_in"), 16)
            sum_squares(x, yacc)
            split_turned("n1")
            act.wait_ge(ev("lam_dot"), 1)
            nc.scalar.activation(small[:, 10:12], small[:, 8:10], ACT.Exp)
            nc.scalar.activation(lbs[:, 16:32], lbs[:, 0:16], ACT.Exp).then_inc(ev("early_exp"), 1)
            tok("in1", proj)
            for n in range(0, 16, 2):
                act.wait_ge(ev("qt_mm"), n + 1)
                root = 64 ** -0.5 if n < 4 else P ** -0.5 if 8 <= n < 12 else 1.0
                nc.scalar.activation(QT[:, 2 * n:2 * n + 2, :].rearrange("p c s -> p (c s)"), PS[:, n % 8, :], ACT.Copy,
                                     scale=root).then_inc(ev("qt_a"), 1)
            nc.scalar.activation(gates[:, :, :], proj[:, :, C_G:C_G + GATES], ACT.Sigmoid).then_inc(ev("gates_done"), 1)
            for v in range(2):
                act.wait_ge(ev("hid_mm"), v + 1)
                nc.scalar.activation(hid[:, v, :, :], PS[:, 2 * v:2 * v + 2, 0:2 * NC], ACT.Gelu_apprx_tanh).then_inc(ev("hid_done"), 1)
            act.wait_ge(ev("tile_used"), used(G["cmp"].first + G["cmp"].tiles))
            act.sem_inc(ev("hi_done"), G["cmp"].tiles)
            act.wait_ge(ev("cmp_shift"), 1)
            nc.scalar.activation(pcs, pcs, ACT.Exp).then_inc(ev("cmp_exp"), 1)
            for n in range(4):
                act.wait_ge(ev("pct_mm"), n + 1)
                nc.scalar.activation(pcT[:, 4 * n:4 * n + 4, :].rearrange("p a b -> p (a b)"), PS[0:NC, n, :], ACT.Copy)\
                    .then_inc(ev("pct_out"), 1)
            for s in range(NBR + 2):
                if s < NBR:
                    act.wait_ge(ev("max1"), s + 1)
                    for m in range(2 if s < HD else 1):
                        for q, (lo, hi) in enumerate(((0, P), (P, SK))):
                            last = nc.scalar.activation(scores[:, s % 2, m, lo:hi], scores[:, s % 2, m, lo:hi], ACT.Exp,
                                                        bias=stat[:, s % 2, 2 * m + q:2 * m + q + 1],
                                                        accum_out=stat[:, s % 2, 4 + 2 * m + q:5 + 2 * m + q])
                    last.then_inc(ev("exp1"), 1)
                if s >= 2:
                    act.wait_ge(ev("pt_mm1"), s - 1)
                    if s >= 4:
                        act.wait_ge(ev("pv_mm1"), s - 3)
                    nc.scalar.activation(probsT[:, s % 2, :], PS[:, 4 + s % 2, 0:SK], ACT.Copy).then_inc(ev("pt_out1"), 1)
            act.wait_ge(ev("o_out1"), NBR)
            for n in range(HD * TT):
                h, t = n // TT, n % TT
                last = nc.scalar.activation(work[:, n * P:(n + 1) * P], proj[:, t, C_DQ + h * P:C_DQ + (h + 1) * P], ACT.Square,
                                            accum_out=hstat[:, 0, n:n + 1])
            last.then_inc(ev("hssq"), 1)
            split_turned("mix1")
            tok("out1", yacc)
            sum_squares(yacc)
            act.wait_ge(ev("resid"), 2)
            sum_squares(x)
            split_turned("n2")
            feat("up1a", True)
            tok("down1a", yacc)
            feat("up1b", True)
            tok("down1b", None)
            act.wait_ge(ev("acc_free"), 2 + G["down1b"].acc + 4)
            sum_squares(yacc)
            act.wait_ge(ev("resid"), 4)
            sum_squares(x)
            split_turned("n3")
            tok("in2", proj2)
            for m, n in enumerate(TURN2):
                if m % 2 == 0:
                    act.wait_ge(ev("qt2_mm"), m + 1)
                    nc.scalar.activation(QT2[:, 2 * n:2 * n + 2, :].rearrange("p c s -> p (c s)"), PS[:, m % 8, :], ACT.Copy,
                                         scale=64 ** -0.5 if n < 4 else 1.0).then_inc(ev("qt2_a"), 1)
            act.wait_ge(ev("qt2_a"), 7)
            act.wait_ge(ev("qt2_d"), 6)
            nc.scalar.activation(sig_q, QT2[:, 16:24, :], ACT.Sigmoid).then_inc(ev("sig"), 1)
            nc.scalar.activation(QT2[:, 24:32, :], QT2[:, 24:32, :], ACT.Sigmoid).then_inc(ev("sig"), 1)
            nc.scalar.activation(sig_g, proj2[:, :, C_GR:C_GR + 1024], ACT.Sigmoid).then_inc(ev("sig"), 1)
            act.wait_ge(ev("f_done"), 1)
            nc.scalar.activation(lnf, QT2[:, 24:32, :], ACT.Ln).then_inc(ev("ln_done"), 1)
            for n in range(4):
                act.wait_ge(ev("logf_mm"), n + 1)
                nc.scalar.activation(logf[:, n // 2, 4 * (n % 2):4 * (n % 2) + 4, :].rearrange("p a b -> p (a b)"),
                                     PS[:, n, :], ACT.Copy).then_inc(ev("logf_out"), 1)
            for s in range(HA + 2):
                if s < HA:
                    act.wait_ge(ev("max2"), s + 1)
                    for q, (lo, hi) in enumerate(((0, P), (P, SK))):
                        nc.scalar.activation(scores2[:, s % 2, lo:hi], scores2[:, s % 2, lo:hi], ACT.Exp,
                                             bias=stat[:, s % 2, q:q + 1], accum_out=stat[:, s % 2, 4 + q:5 + q])
                    nc.scalar.activation(stat[:, s % 2, 6:8], stat[:, s % 2, 0:2], ACT.Exp,
                                         bias=sinks[:, 0, s:s + 1]).then_inc(ev("exp2"), 1)
                if s >= 2:
                    act.wait_ge(ev("pt_mm2"), s - 1)
                    if s >= 4:
                        act.wait_ge(ev("pv_mm2"), s - 3)
                    nc.scalar.activation(probsT2[:, s % 2, :], PS[:, 2 + s % 2, 0:SK], ACT.Copy).then_inc(ev("pt_out2"), 1)
            def cross_out(h):
                act.wait_ge(ev("cross_mm"), h + 1)
                if h >= 1:
                    act.wait_ge(ev("o_mm"), 2 * h)
                nc.scalar.activation(crossT[:, :], PS[:, 4, 0:P], ACT.Copy).then_inc(ev("cross_out"), 1)

            def o_out(n):
                h, t = n // TT, n % TT
                act.wait_ge(ev("o_mm"), n + 1)
                nc.scalar.activation(proj2[:, t, C_FR + h * P:C_FR + (h + 1) * P], PS[:, 5, 0:P], ACT.Copy)
                nc.scalar.activation(PS[:, 5, P:2 * P], PS[:, 5, 0:P], ACT.Square, accum_out=hstat[:, 0, n:n + 1])\
                    .then_inc(ev("o_out"), 1)

            NR = HR * TT
            for n in range(NR + 2):
                if n < NR:
                    act.wait_ge(ev("exps_mm"), n + 1)
                    if n >= 1:
                        act.wait_ge(ev("qf"), n)
                        act.wait_ge(ev("kf"), n)
                    nc.scalar.activation(fac.rearrange("p a b -> p (a b)"), PS[:, 0:2, :].rearrange("p a b -> p (a b)"),
                                         ACT.Exp).then_inc(ev("fac"), 1)
                if 1 <= n <= NR and (n - 1) % TT == 1:
                    cross_out((n - 1) // TT)
                if n >= 2:
                    o_out(n - 2)
            act.wait_ge(ev("o_out2"), HA)
            act.wait_ge(ev("o_out"), NR)
            for t in range(TT):
                last = nc.scalar.activation(squares[t][:, 0:1024], proj2[:, t, C_QA:C_QA + 1024],
                                            ACT.Square, accum_out=small[:, t:t + 1])
            last.then_inc(ev("ssq"), 1)
            split_turned("mix2")
            tok("out2", yacc)
            sum_squares(yacc)
            act.wait_ge(ev("resid"), 6)
            sum_squares(x)
            split_turned("n4")
            feat("up2a", False)
            tok("down2a", yacc)
            feat("up2b", False)
            tok("down2b", None)
            act.wait_ge(ev("acc_free"), 2 + G["down2b"].acc + 4)
            sum_squares(yacc)

        @block.vector
        def _(dve):
            def tok(name, add):
                g = G[name]

                def tile(i, b, j, n):
                    s = b * g.tiles + j
                    wd = TC * (width(name, b) if i is None else NW)
                    dve.wait_ge(ev("hi_done"), n + 1)
                    nc.vector.tensor_tensor(wlo[:, s % SPLITS, 0:wd], stage[:, s % STAGES, 0:wd],
                                            whi[:, s % SPLITS, 0:wd].bitcast(F32), ALU.subtract).then_inc(ev("lo_done"), 1)

                def take(i, b):
                    col, nb, bank, wd = place(name, i, b)
                    dve.wait_ge(ev("tile_used"), used((nb + 1) * g.tiles + g.first))
                    for t in range(TT):
                        last = nc.vector.tensor_tensor(yacc[:, t, span(col, wd)], PS[:, 2 * bank + t, 0:wd],
                                                       yacc[:, t, span(col, wd)], ALU.add)
                    last.then_inc(ev("acc_free"), 1)
                tok_order(dve, name, tile, take if add else None)

            def feat(name, conv):
                g = G[name]
                gT = gT1 if conv else gT2

                def tiles(i, js):
                    for j in js:
                        dve.wait_ge(ev("hi_done"), i * FT + (g.first + j + 1))
                        nc.vector.tensor_tensor(wlo[:, j % SPLITS, :], stage[:, j, :], whi[:, j % SPLITS, :].bitcast(F32),
                                                ALU.subtract).then_inc(ev("lo_done"), 1)

                def join(i, s):
                    dve.wait_ge(ev("low_out"), i + (g.acc + 1))
                    to = pre[:, :, 2:2 + S] if conv else lowsum
                    nc.vector.tensor_tensor(to, PS[:, 4 * s:4 * s + 4, 0:S], lowsum, ALU.add).then_inc(ev("pre_done"), 1)

                def taps(i):
                    for tap, name_ in ((1, "tap_mid"), (0, "conv_done")):
                        if tap:
                            dve.wait_ge(ev("tap"), i * 4 + 4 * (g.acc + 1))
                        else:
                            dve.wait_ge(ev("tap_mid"), i + (g.acc + 1))
                        for a in range(4):
                            f = i * 2 + (2 * (g.acc if name == "up1b" else 0) + a % 2 + F1 // P * (a // 2))
                            last = nc.vector.scalar_tensor_tensor(post[:, a, :], pre[:, a, tap:tap + S],
                                                                  convT[:, tap, span(f, 1)], post[:, a, :],
                                                                  ALU.mult, ALU.add)
                        last.then_inc(ev(name_), 1)

                def product(i):
                    if conv:
                        dve.wait_ge(ev("gelu"), i + (g.acc + 1))
                        nc.vector.tensor_tensor(post[:, 0:2, :], lowsum[:, 0:2, :], post[:, 2:4, :], ALU.mult)\
                            .then_inc(ev("prod"), 1)
                    else:
                        dve.wait_ge(ev("pre_done"), i + (g.acc + 3))
                        nc.vector.scalar_tensor_tensor(post[:, :, :], lowsum, 0.0, lowsum, ALU.max, ALU.mult)\
                            .then_inc(ev("prod"), 1)

                def low_parts(i):
                    k = 2 if conv else 4
                    dve.wait_ge(ev("g_hi"), i + (g.acc + 1))
                    nc.vector.tensor_tensor(gT[:, span(i * k, k), S:2 * S], post[:, 0:k, :],
                                            gT[:, span(i * k, k), 0:S].bitcast(F32), ALU.subtract).then_inc(ev("g_lo"), 1)

                def one(i, s, prev):
                    tiles(i, (0, 1, 2, 3))
                    if prev is not None:
                        join(prev, 1 - s)
                        if conv:
                            taps(prev)
                    tiles(i, (4, 5))
                    if prev is not None:
                        product(prev)
                        low_parts(prev)
                    tiles(i, (6, 7))
                one(0, 0, None)
                one(1, 1, 0)
                with dve.Fori(1, g.blocks // 2) as r:
                    one(r * 2, 0, r * 2 - 1)
                    one(r * 2 + 1, 1, r * 2)
                join(g.blocks - 1, 1)
                if conv:
                    taps(g.blocks - 1)
                product(g.blocks - 1)
                low_parts(g.blocks - 1)

            def mean_square(k, src, dst, count, ready, n):
                dve.wait_ge(ev(ready), n)
                nc.vector.tensor_scalar(dst, src, 1.0 / count, EPS, ALU.mult, ALU.add).then_inc(ev("var"), 1)

            def normed_x(k, n):
                mean_square(k, small[:, 0:2], small[:, 2:4], D, "ssq", k)
                dve.wait_ge(ev("rstd"), n)
                for t in range(TT):
                    nc.vector.tensor_scalar(yacc[:, t, :], x[:, t, :], small[:, 4 + t:5 + t], None, ALU.mult)\
                        .then_inc(ev("normed"), 1)

            def split_turned(turn):
                for c in range(KC):
                    dve.wait_ge(ev("acthi_" + turn), c // 2 * 2 + 2)
                    nc.vector.scalar_tensor_tensor(actT[:, c, S:2 * S], PS[:, c // 2, (c % 2) * S:(c % 2 + 1) * S],
                                                   gain_of(turn, c), actT[:, c, 0:S].bitcast(F32),
                                                   ALU.mult, ALU.subtract).then_inc(ev("actlo_" + turn), 1)

            def residual(k, n, gain):
                mean_square(k, small[:, 0:2], small[:, 2:4], D, "ssq", k)
                dve.wait_ge(ev("grow_in"), 16 * gain)
                dve.wait_ge(ev("rstd"), n)
                for t in range(TT):
                    then(dve, "dve", nc.vector.scalar_tensor_tensor(yacc[:, t, :], yacc[:, t, :], small[:, 4 + t:5 + t],
                                                                    grow[:, :], ALU.mult, ALU.mult))
                    nc.vector.tensor_tensor(x[:, t, :], x[:, t, :], yacc[:, t, :], ALU.add).then_inc(ev("resid"), 1)

            def me(ins):
                then(dve, "dve", ins)

            dve.sem_inc(ev("lo_done"), STAGES)
            dve.sem_inc(ev("acc_free"), 2)
            dve.sem_inc(ev("pre_done"), 2)
            dve.sem_inc(ev("g_lo"), 1)
            dve.wait_ge(ev("urow_mm"), 1)
            nc.vector.memset(urow[:, S:SK], NEG).then_inc(ev("urow"), 1)
            nc.vector.tensor_copy(urow[:, 0:S], PS[0:16, 5, 0:S]).then_inc(ev("urow"), 1)
            dve.wait_ge(ev("vecs_mm"), 1)
            me(nc.vector.tensor_copy(cols[:, 0:74], PS[:, 7, 0:74]))
            me(nc.vector.tensor_scalar(cols[:, 72:73], cols[:, 72:73], 1.0 - LAM_INIT, None, ALU.mult))
            me(nc.vector.memset(cols[:, 74:75], 1.0))
            me(nc.vector.tensor_copy(cols[:, C_LB:C_LB + 16], PS[:, 7, 74:90]))
            nc.vector.tensor_copy(convT[:, :, :], PS[:, 6, :].rearrange("p (j f) -> p j f", j=4)[:, :, 0:88])
            nc.vector.tensor_copy(posT[:, :, :], PS[:, 7, 128:192].rearrange("p (v l) -> p v l", v=2)).then_inc(ev("cols"), 1)
            dve.wait_ge(ev("lam_in"), 64)
            me(nc.vector.tensor_tensor(lamv[:, 0:2, :], lamv[:, 0:2, :], lamv[:, 2:4, :], ALU.mult))
            me(nc.vector.tensor_tensor(lbs[:, 32:40], cols[:, C_LB:C_LB + 8], cols[:, C_LB + 8:C_LB + 16], ALU.max))
            nc.vector.tensor_tensor(lbs[:, 0:8], cols[:, C_LB:C_LB + 8], lbs[:, 32:40], ALU.subtract)
            nc.vector.tensor_tensor(lbs[:, 8:16], cols[:, C_LB + 8:C_LB + 16], lbs[:, 32:40], ALU.subtract)
            nc.vector.tensor_reduce(small[:, 8:10], lamv[:, 0:2, :], AX.X, ALU.add).then_inc(ev("lam_dot"), 1)
            mean_square(1, small[:, 0:2], small[:, 2:4], D, "ssq", 1)
            for n in range(8):
                dve.wait_ge(ev("bias_mm"), n + 1)
                rows = PS[:, n, :].rearrange("p (h j) -> p h j", h=2)
                nc.vector.tensor_copy(bias[:, 2 * n:2 * n + 2, P:SK], rows)
                nc.vector.tensor_copy(bias[:, 2 * n:2 * n + 2, 0:P], rows[:, :, P:2 * P]).then_inc(ev("bias_done"), 1)
            dve.wait_ge(ev("rstd"), 1)
            for t in range(TT):
                nc.vector.tensor_scalar(yacc[:, t, :], x[:, t, :], small[:, 4 + t:5 + t], None, ALU.mult)\
                    .then_inc(ev("normed"), 1)
            split_turned("n1")
            dve.wait_ge(ev("early_exp"), 1)
            me(nc.vector.tensor_tensor(small[:, 12:13], small[:, 11:12], small[:, 10:11], ALU.subtract))
            me(nc.vector.tensor_scalar(small[:, 12:13], small[:, 12:13], LAM_INIT, None, ALU.subtract))
            me(nc.vector.tensor_tensor(lbs[:, 32:40], lbs[:, 16:24], lbs[:, 24:32], ALU.add))
            me(nc.vector.reciprocal(lbs[:, 32:40], lbs[:, 32:40]))
            me(nc.vector.tensor_tensor(lbs[:, 32:40], lbs[:, 16:24], lbs[:, 32:40], ALU.mult))
            me(nc.vector.tensor_scalar(lbs[:, 40:48], lbs[:, 32:40], -1.0, 1.0, ALU.mult, ALU.add))
            tok("in1", False)
            for n in range(1, 16, 2):
                dve.wait_ge(ev("qt_mm"), n + 1)
                root = 64 ** -0.5 if n < 4 else P ** -0.5 if 8 <= n < 12 else 1.0
                nc.vector.tensor_scalar(QT[:, 2 * n:2 * n + 2, :].rearrange("p c s -> p (c s)"), PS[:, n % 8, :], root, None,
                                        ALU.mult).then_inc(ev("qt_d"), 1)
            for j in range(G["cmp"].tiles):
                dve.wait_ge(ev("tile_used"), used(G["cmp"].first + j + 1))
                dve.sem_inc(ev("lo_done"), 1)
            dve.wait_ge(ev("kc_mm"), 1)
            nc.vector.tensor_copy(kcT, PS[:, 4, 0:2 * NC])
            nc.vector.tensor_copy(vc, PS[0:NC, 5, 0:NKV * P].rearrange("p (g d) -> p g d", g=NKV)).then_inc(ev("kc_out"), 1)
            dve.wait_ge(ev("keep_in"), 32)
            dve.wait_ge(ev("gates_done"), 1)
            dve.wait_ge(ev("cmp_mm"), 1)
            every = PS[:, 6, 0:256].rearrange("p (h t c) -> p h t c", h=HN, t=TT)[:, :, :, 0:NC]
            for t in range(TT):
                keep_t = keepc[:, 0, t, :].rearrange("p (o c) -> p o c", o=1).broadcast_to((P, HN, NC))
                last = nc.vector.tensor_tensor(pcs[:, :, t, :], every[:, :, t, :], keep_t, ALU.mult)
            me(last)
            for t in range(TT):
                drop_t = keepc[:, 1, t, :].rearrange("p (o c) -> p o c", o=1).broadcast_to((P, HN, NC))
                last = nc.vector.tensor_tensor(pcs[:, :, t, :], pcs[:, :, t, :], drop_t, ALU.add)
            me(last)
            flat_h = cst.rearrange("p a h t -> p a (h t)")
            flat_p = pcs.rearrange("p h t c -> p (h t) c")

            def wide(k):
                return flat_h[:, k, :].rearrange("p (n o) -> p n o", o=1).broadcast_to((P, HN * TT, NC))
            me(nc.vector.tensor_reduce(flat_h[:, 0, :], flat_p, AX.X, ALU.max))
            nc.vector.tensor_tensor(flat_p, flat_p, wide(0), ALU.subtract).then_inc(ev("cmp_shift"), 1)
            dve.wait_ge(ev("cmp_exp"), 1)
            for t in range(TT):
                keep_t = keepc[:, 0, t, :].rearrange("p (o c) -> p o c", o=1).broadcast_to((P, HN, NC))
                last = nc.vector.tensor_tensor(pcs[:, :, t, :], pcs[:, :, t, :], keep_t, ALU.mult)
            me(last)
            me(nc.vector.tensor_reduce(flat_h[:, 1, :], flat_p, AX.X, ALU.add))
            me(nc.vector.tensor_scalar(flat_h[:, 1, :], flat_h[:, 1, :], TINY, None, ALU.max))
            me(nc.vector.reciprocal(flat_h[:, 1, :], flat_h[:, 1, :]))
            gate0 = gates[:, :, :].rearrange("p t (h b) -> p h t b", b=3)[:, :, :, 0]
            me(nc.vector.tensor_tensor(cst[:, 2, :, :], cst[:, 1, :, :], gate0, ALU.mult))
            nc.vector.tensor_tensor(flat_p, flat_p, wide(2), ALU.mult).then_inc(ev("cmp_probs"), 1)
            for h in range(HN):
                dve.wait_ge(ev("cmp_pv"), h // 2 + 1)
                o = PS[:, 4 + h // 2, (h % 2) * S:(h % 2 + 1) * S].rearrange("p (t d) -> p t d", t=TT)
                last = nc.vector.tensor_copy(proj[:, :, C_NQ + h * P:C_NQ + (h + 1) * P], o)
            last.then_inc(ev("cmp_out"), 1)

            def front(s):
                dve.wait_ge(ev("log_mm1"), s + 1)
                if s >= 2:
                    dve.wait_ge(ev("pt_mm1"), s - 1)
                head = s if s < HD else HD + (s - HD) // 2
                maps = 2 if s < HD else 1
                b = bias[:, head:head + 1, :].broadcast_to((P, maps, SK))
                me(nc.vector.tensor_tensor(scores[:, s % 2, 0:maps, :], PS[:, 2 * (s % 2):2 * (s % 2) + maps, 0:SK], b, ALU.add))
                nm = stat[:, s % 2, 0:4].rearrange("p (m q) -> p m q", q=2)
                nc.vector.tensor_reduce(nm[:, 0:maps, 0], scores[:, s % 2, 0:maps, 0:P], AX.X, ALU.max, negate=True)
                nc.vector.tensor_reduce(nm[:, 0:maps, 1], scores[:, s % 2, 0:maps, P:SK], AX.X, ALU.max, negate=True)\
                    .then_inc(ev("max1"), 1)

            def weigh(s):
                dve.wait_ge(ev("exp1"), s + 1)
                st = stat[:, s % 2, :]
                k = 4 if s < HD else 2
                me(nc.vector.reciprocal(st[:, 8:8 + k], st[:, 4:4 + k]))
                if s < HD:
                    me(nc.vector.tensor_scalar(st[:, 10:12], st[:, 10:12], small[:, 12:13], None, ALU.mult))
                    if s >= 2:
                        dve.wait_ge(ev("pt_mm1"), s - 1)
                    for q, (lo, hi) in enumerate(((0, P), (P, SK))):
                        last = nc.vector.tensor_scalar(probs[:, s % 2, lo:hi], scores[:, s % 2, 0, lo:hi], st[:, 8 + q:9 + q],
                                                       None, ALU.mult)
                    me(last)
                    for q, (lo, hi) in enumerate(((0, P), (P, SK))):
                        last = nc.vector.scalar_tensor_tensor(probs[:, s % 2, lo:hi], scores[:, s % 2, 1, lo:hi],
                                                              st[:, 10 + q:11 + q], probs[:, s % 2, lo:hi],
                                                              ALU.mult, ALU.add)
                    last.then_inc(ev("probs1"), 1)
                else:
                    r = s - HD
                    g = gates[:, :, :].rearrange("p t (h b) -> p h t b", b=3)[:, r // 2, :, 1 + r % 2]
                    nc.vector.tensor_tensor(weights[:, s % 4, :], st[:, 8:10], g, ALU.mult).then_inc(ev("probs1"), 1)

            def take_out(s):
                dve.wait_ge(ev("pv_mm1"), s + 1)
                o = PS[:, 6 + s % 2, 0:S].rearrange("p (t d) -> p t d", t=TT)
                if s < HD:
                    nc.vector.tensor_copy(proj[:, :, C_DQ + s * P:C_DQ + (s + 1) * P], o).then_inc(ev("o_out1"), 1)
                    return
                h = (s - HD) // 2
                for t in range(TT):
                    at = proj[:, t, C_NQ + h * P:C_NQ + (h + 1) * P]
                    last = nc.vector.scalar_tensor_tensor(at, o[:, t, :], weights[:, s % 4, t:t + 1], at, ALU.mult, ALU.add)
                last.then_inc(ev("o_out1"), 1)
                dve.wait_ge(ev("o_out1"), s + 1)
            weights = small[:, 16:24].rearrange("p (s t) -> p s t", s=4)
            for s in range(NBR + 3):
                if s < NBR:
                    front(s)
                if 1 <= s <= NBR:
                    weigh(s - 1)
                if s >= 3:
                    take_out(s - 3)
            mean_square(0, hstat[:, 0, :], hstat[:, 1, :], P, "hssq", 1)
            dve.wait_ge(ev("rstd"), 2)
            r = hstat[:, 2, :].rearrange("p (h t o) -> p h t o", t=TT, o=1)
            for t in range(TT):
                o = proj[:, t, C_DQ:C_DQ + HD * P].rearrange("p (h d) -> p h d", h=HD)
                nc.vector.tensor_tensor(o, o, r[:, :, t, :].broadcast_to((P, HD, P)), ALU.mult).then_inc(ev("mixed1"), 1)
            split_turned("mix1")
            tok("out1", False)
            residual(2, 3, 1)
            me(nc.vector.memset(pre[:, :, 0:2], 0.0))
            normed_x(3, 4)
            split_turned("n2")
            feat("up1a", True)
            tok("down1a", False)
            feat("up1b", True)
            dve.wait_ge(ev("acc_free"), 2 + G["down1b"].acc)
            tok("down1b", True)
            residual(4, 5, 2)
            normed_x(5, 6)
            split_turned("n3")
            tok("in2", False)
            dve.wait_ge(ev("acc_free"), 2 + G["in2"].acc + G["in2"].blocks)
            for v in range(NKV):
                src = proj2[:, :, C_KA + v * 64:C_KA + (v + 1) * 64]
                for u in range(2):
                    last = nc.vector.tensor_copy(kdup[:, :, v, u, :], src)
            last.then_inc(ev("kdup"), 1)
            for m, n in enumerate(TURN2):
                if m % 2:
                    dve.wait_ge(ev("qt2_mm"), m + 1)
                    nc.vector.tensor_scalar(QT2[:, 2 * n:2 * n + 2, :].rearrange("p c s -> p (c s)"), PS[:, m % 8, :],
                                            64 ** -0.5 if n < 4 else 1.0, None, ALU.mult).then_inc(ev("qt2_d"), 1)
            dve.wait_ge(ev("sig"), 1)
            me(nc.vector.tensor_tensor(QT2[:, 16:24, :], QT2[:, 16:24, :], sig_q, ALU.mult))
            dve.wait_ge(ev("sig"), 2)
            for h in range(HR):
                f = QT2[:, 24 + h, :]
                nc.vector.tensor_scalar(f, f, lbs[:, 40 + h:41 + h], lbs[:, 32 + h:33 + h], ALU.mult, ALU.add)
            dve.wait_ge(ev("sig"), 3)
            gr = proj2[:, :, C_GR:C_GR + 1024]
            nc.vector.tensor_tensor(gr, gr, sig_g, ALU.mult).then_inc(ev("f_done"), 1)
            dve.wait_ge(ev("ln_done"), 1)
            nc.vector.tensor_scalar(QT2[:, 24:32, :], QT2[:, 24:32, :], -1.0, 1.0, ALU.mult, ALU.add).then_inc(ev("key_done"), 1)
            dve.wait_ge(ev("mix2_in"), 64)
            me(nc.vector.tensor_scalar(sinks[:, 1, :], sinks[:, 0, :], -1.0, None, ALU.mult))

            def front2(s):
                dve.wait_ge(ev("log_mm2"), s + 1)
                if s >= 2:
                    dve.wait_ge(ev("pt_mm2"), s - 1)
                slope = -(2.0 ** (-8.0 * (s + 1) / HA))
                me(nc.vector.scalar_tensor_tensor(scores2[:, s % 2, :], far[:, :], slope, PS[:, s % 2, 0:SK], ALU.mult, ALU.add))
                st = stat[:, s % 2, :]
                nc.vector.tensor_reduce(st[:, 0:1], scores2[:, s % 2, 0:P], AX.X, ALU.max, negate=True)
                me(nc.vector.tensor_reduce(st[:, 1:2], scores2[:, s % 2, P:SK], AX.X, ALU.max, negate=True))
                nc.vector.tensor_scalar(st[:, 0:2], st[:, 0:2], sinks[:, 1, s:s + 1], None, ALU.min).then_inc(ev("max2"), 1)

            def weigh2(s):
                dve.wait_ge(ev("exp2"), s + 1)
                st = stat[:, s % 2, :]
                me(nc.vector.tensor_tensor(st[:, 4:6], st[:, 4:6], st[:, 6:8], ALU.add))
                me(nc.vector.reciprocal(wsum[:, s % 4, :], st[:, 4:6]))

            def take_out2(s):
                dve.wait_ge(ev("pv_mm2"), s + 1)
                for t in range(TT):
                    last = nc.vector.tensor_scalar(proj2[:, t, C_QA + s * 64:C_QA + (s + 1) * 64],
                                                   PS[:, 6 + s % 2, t * 64:(t + 1) * 64], wsum[:, s % 4, t:t + 1], None, ALU.mult)
                last.then_inc(ev("o_out2"), 1)
            wsum = lbs[:, 0:8].rearrange("p (s t) -> p s t", s=4)
            for s in range(HA + 3):
                if s < HA:
                    front2(s)
                if 1 <= s <= HA:
                    weigh2(s - 1)
                if s >= 3:
                    take_out2(s - 3)
            NR = HR * TT
            for n in range(NR + 1):
                if n < NR:
                    h, t = n // TT, n % TT
                    dve.wait_ge(ev("fac"), n + 1)
                    if n >= 1:
                        dve.wait_ge(ev("att_mm"), n)
                    q = QT2[:, 16 + h, t * P:(t + 1) * P].rearrange("p (o t) -> p o t", o=1).broadcast_to((P, 8, P))
                    nc.vector.tensor_tensor(qf, fac, q, ALU.mult).then_inc(ev("qf"), 1)
                if n >= 1:
                    dve.wait_ge(ev("att_mm"), n)
                    me(nc.vector.tensor_tensor(attm, PS[:, 2:4, :].rearrange("p a (l t) -> p (a l) t", t=P), keep[:, :, :], ALU.mult))
                    if n >= 2:
                        dve.wait_ge(ev("o_mm"), n - 1)
                    nc.vector.tensor_reduce(attT[:, :], attm.rearrange("p l t -> p t l"), AX.X, ALU.add).then_inc(ev("att_out"), 1)
            mean_square(0, small[:, 0:2], small[:, 2:4], 1024, "ssq", 6)
            dve.wait_ge(ev("o_out"), NR)
            mean_square(0, hstat[:, 0, :], hstat[:, 1, :], P, "o_out", NR)
            dve.wait_ge(ev("rstd"), 7)
            for t in range(TT):
                o = proj2[:, t, C_QA:C_QA + 1024]
                nc.vector.tensor_scalar(o, o, small[:, 4 + t:5 + t], None, ALU.mult).then_inc(ev("mixed2"), 1)
            dve.wait_ge(ev("rstd"), 8)
            r = hstat[:, 2, :].rearrange("p (h t o) -> p h t o", t=TT, o=1)
            for t in range(TT):
                g = proj2[:, t, C_GR:C_GR + 1024].rearrange("p (h d) -> p h d", h=HR)
                me(nc.vector.tensor_tensor(g, g, r[:, :, t, :].broadcast_to((P, HR, P)), ALU.mult))
                nc.vector.tensor_tensor(proj2[:, t, C_IR:C_IR + 1024], proj2[:, t, C_FR:C_FR + 1024],
                                        proj2[:, t, C_GR:C_GR + 1024], ALU.mult).then_inc(ev("mixed2"), 1)
            split_turned("mix2")
            tok("out2", False)
            residual(7, 9, 3)
            normed_x(8, 10)
            split_turned("n4")
            feat("up2a", False)
            tok("down2a", False)
            feat("up2b", False)
            dve.wait_ge(ev("acc_free"), 2 + G["down2b"].acc)
            tok("down2b", True)
            residual(9, 11, 4)

        @block.tensor
        def _(pe):
            def tok(name, lhs, first=0):
                g, pairs = G[name], PAIRS[name]
                T = g.tiles

                def one(i, b, base):
                    _, nb, bank, wd = place(name, i, b)
                    pe.wait_ge(ev("acc_free"), nb + (g.acc + 1))
                    for j in range(T):
                        s = (b * T + j) % SPLITS
                        pe.wait_ge(ev("lo_done"), base + (j + 1 + STAGES))
                        for c in range(TC):
                            k = TC * j + c
                            h, l = whi[:, s, c * wd:(c + 1) * wd], wlo[:, s, c * wd:(c + 1) * wd]
                            for t in range(TT):
                                o = PS[:, 2 * bank + t, 0:wd]
                                ah, al = lhs[:, k, t * P:(t + 1) * P], lhs[:, k, S + t * P:S + (t + 1) * P]
                                nc.tensor.matmul(o, ah, h, start=k == 0, stop=False)
                                nc.tensor.matmul(o, ah, l, start=False, stop=False)
                                last = nc.tensor.matmul(o, al, h, start=False, stop=k == TC * T - 1)
                        last.then_inc(ev("tile_used"), 1)
                if pairs:
                    with pe.Fori(0, pairs) as i:
                        for b in range(2):
                            one(i, b, i * (2 * T) + (g.first + b * T))
                for b in range(2 * pairs, g.blocks):
                    one(None, b, g.first + b * T)

            def feat(name):
                g = G[name]
                with pe.Fori(0, g.blocks // 2) as r:
                    for s in range(2):
                        i = r * 2 + s
                        pe.wait_ge(ev("pre_done"), i + (g.acc + 1))
                        for j in range(FT):
                            pe.wait_ge(ev("lo_done"), i * FT + (g.first + j + 1 + STAGES))
                            for c in range(FC):
                                k = j % (FT // 2) * FC + c
                                for f in range(2):
                                    o = PS[:, 4 * s + 2 * (j // (FT // 2)) + f, :]
                                    at = slice(c * FW + f * P, c * FW + (f + 1) * P)
                                    nc.tensor.matmul(o, whi[:, j % SPLITS, at], actT[:, k, :], start=k == 0, stop=False)
                                    last = nc.tensor.matmul(o[:, S:2 * S], wlo[:, j % SPLITS, at], actT[:, k, 0:S],
                                                            start=False, stop=k == KC - 1)
                            last.then_inc(ev("tile_used"), 1)

            def turn(name, ready, n):
                pe.wait_ge(ev(ready), n)
                for c in range(KC):
                    for t in range(TT):
                        at = (c % 2) * S + t * P
                        last = nc.tensor.transpose(PS[:, c // 2, at:at + P], src_of(name, t, c), ident[:, :])
                    if c % 2:
                        last.then_inc(ev("turned_" + name), 1)

            def acts(name):
                pe.wait_ge(ev("actlo_" + name), KC)

            pe.sem_inc(ev("tile_used"), SPLITS)
            pe.wait_ge(ev("tab_in"), 32)
            nc.tensor.matmul(PS[0:16, 5, 0:SK], tab, hot, start=True, stop=True).then_inc(ev("urow_mm"), 1)
            pe.wait_ge(ev("ident_in"), 32)
            pe.wait_ge(ev("vecs_in"), 16 * 14)
            nc.tensor.transpose(PS[:, 7, 0:90], vecs[0:90, 0, :], ident[0:90, 0:90])
            nc.tensor.transpose(PS[:, 7, 128:192], vecs[0:64, 1, :], ident[0:64, 0:64])
            for j in range(4):
                last = nc.tensor.transpose(PS[:, 6, j * P:j * P + 88], vecs[0:88, 2 + j, :], ident[0:88, 0:88])
            last.then_inc(ev("vecs_mm"), 1)
            pe.wait_ge(ev("hankel_in"), 16)
            pe.wait_ge(ev("urow"), 2)
            pe.wait_ge(ev("cols"), 1)
            pe.wait_ge(ev("ssq"), 1)
            for n in range(8):
                nc.tensor.matmul(PS[:, n, :], flip, hankel[:, 2 * n:2 * n + 2, :].rearrange("p h j -> p (h j)"),
                                 start=True, stop=True).then_inc(ev("bias_mm"), 1)
            pe.wait_ge(ev("bias_done"), 8)
            turn("n1", "normed", 2)
            acts("n1")
            tok("in1", actT)
            pe.wait_ge(ev("acc_free"), 2 + G["in1"].blocks)
            COLS = ([C_DQ + c * P for c in range(8)] + [C_DK + c * P for c in range(8)] + [C_NQ + c * P for c in range(8)]
                    + [c0 + g * P for c0 in (C_KC, C_VC, C_KS, C_KW) for g in range(NKV)])
            for n in range(16):
                if n >= 8:
                    pe.wait_ge(ev("qt_d" if n % 2 else "qt_a"), (n - 8) // 2 + 1)
                for c in range(2):
                    for t in range(TT):
                        at = COLS[2 * n + c]
                        last = nc.tensor.transpose(PS[:, n % 8, c * S + t * P:c * S + (t + 1) * P],
                                                   proj[:, t, at:at + P], ident[:, :])
                last.then_inc(ev("qt_mm"), 1)
            pe.wait_ge(ev("qt_a"), 8)
            pe.wait_ge(ev("qt_d"), 8)
            for v in range(2):
                pe.wait_ge(ev("blocks_done"), 4 * (v + 1))
                for j in range(STAGES):
                    n = G["cmp"].first + STAGES * v + j
                    pe.wait_ge(ev(f"landed{j}"), 16 * (n // STAGES + 1))
                    for l in range(FC):
                        for a in range(2):
                            k = FC * j + l
                            last = nc.tensor.matmul(PS[:, 2 * v + a, 0:2 * NC], stage[:, j, l * HID + a * P:l * HID + (a + 1) * P],
                                                    blocks[:, v, k, :, :].rearrange("p g c -> p (g c)"),
                                                    start=k == 0, stop=k == CMP_LEN - 1)
                    last.then_inc(ev("tile_used"), 1)
                pe.wait_ge(ev("tile_used"), used(n + 1))
                pe.sem_inc(ev("hid_mm"), 1)
            pe.wait_ge(ev("w2_in"), 32)
            pe.wait_ge(ev("hid_done"), 1)
            for a in range(2):
                nc.tensor.matmul(PS[:, 4, 0:2 * NC], w2[:, 0, a, :], hid[:, 0, a, :], start=a == 0, stop=a == 1)
            pe.wait_ge(ev("hid_done"), 2)
            for g in range(NKV):
                for a in range(2):
                    last = nc.tensor.matmul(PS[0:NC, 5, g * P:(g + 1) * P], hid[:, 1, a, g * NC:(g + 1) * NC], w2[:, 1, a, :],
                                            start=a == 0, stop=a == 1)
            last.then_inc(ev("kc_mm"), 1)
            pe.wait_ge(ev("kc_out"), 1)
            for n in range(HN * TT):
                h, t = n // TT, n % TT
                g = h // (HN // NKV)
                last = nc.tensor.matmul(PS[:, 6, n * 16:n * 16 + NC], QT[:, 16 + h, t * P:(t + 1) * P],
                                        kcT[:, g * NC:(g + 1) * NC], start=True, stop=True)
            last.then_inc(ev("cmp_mm"), 1)
            pe.wait_ge(ev("cmp_probs"), 1)
            for n in range(HN * TT):
                last = nc.tensor.transpose(PS[0:NC, n // 4, (n % 4) * P:(n % 4 + 1) * P], pcs[:, n // TT, n % TT, :], ident[:, :])
                if n % 4 == 3:
                    last.then_inc(ev("pct_mm"), 1)
            for n in range(HN * TT):
                h = n // TT
                pe.wait_ge(ev("pct_out"), n // 4 + 1)
                last = nc.tensor.matmul(PS[:, 4 + n // 4, (n % 4) * P:(n % 4 + 1) * P], pcT[:, n, :], vc[:, h // (HN // NKV), :],
                                        start=True, stop=True)
                if n % 4 == 3:
                    last.then_inc(ev("cmp_pv"), 1)
            pe.wait_ge(ev("cmp_out"), 1)

            def branch(s):
                if s < HD:
                    return [(QT[64 * m:64 * m + 64, s, :], QT[64 * m:64 * m + 64, 8 + s, :]) for m in range(2)], C_DV + s * P
                h, kind = (s - HD) // 2, (s - HD) % 2
                g = h // (HN // NKV)
                return [(QT[:, 16 + h, :], QT[:, 28 + 2 * kind + g, :])], (C_VS, C_VW)[kind] + g * P

            for s in range(NBR + 3):
                if s < NBR:
                    if s >= 2:
                        pe.wait_ge(ev("max1"), s - 1)
                    for m, (q, k) in enumerate(branch(s)[0]):
                        nc.tensor.matmul(PS[:, 2 * (s % 2) + m, 0:P], q[:, 0:P], k[:, 0:P], start=True, stop=True)
                        last = nc.tensor.matmul(PS[:, 2 * (s % 2) + m, P:SK], q[:, P:S], k[:, 0:S], start=True, stop=True)
                    last.then_inc(ev("log_mm1"), 1)
                if 2 <= s < NBR + 2:
                    r = s - 2
                    pe.wait_ge(ev("probs1"), r + 1)
                    if r >= 2:
                        pe.wait_ge(ev("pt_out1"), r - 1)
                    src = probs[:, r % 2, :] if r < HD else scores[:, r % 2, 0, :]
                    for b in range(3):
                        last = nc.tensor.transpose(PS[:, 4 + r % 2, b * P:(b + 1) * P], src[:, b * P:(b + 1) * P], ident[:, :])
                    last.then_inc(ev("pt_mm1"), 1)
                if s >= 3:
                    r = s - 3
                    pe.wait_ge(ev("pt_out1"), r + 1)
                    if r >= 2:
                        pe.wait_ge(ev("o_out1"), r - 1)
                    v = branch(r)[1]
                    pt, o = probsT[:, r % 2, :], PS[:, 6 + r % 2, :]
                    nc.tensor.matmul(o[:, 0:P], pt[:, 0:P], proj[:, 0, v:v + P], start=True, stop=True)
                    nc.tensor.matmul(o[:, P:2 * P], pt[:, P:2 * P], proj[:, 0, v:v + P], start=True, stop=False)
                    nc.tensor.matmul(o[:, P:2 * P], pt[:, 2 * P:3 * P], proj[:, 1, v:v + P], start=False, stop=True)\
                        .then_inc(ev("pv_mm1"), 1)
            pe.wait_ge(ev("o_out1"), NBR)
            turn("mix1", "mixed1", 2)
            acts("mix1")
            tok("out1", actT)
            turn("n2", "normed", 4)
            acts("n2")
            feat("up1a")
            pe.wait_ge(ev("g_lo"), 1 + 12)
            tok("down1a", gT1)
            pe.wait_ge(ev("acc_free"), 2 + G["down1a"].acc + 4)
            feat("up1b")
            pe.wait_ge(ev("g_lo"), 1 + 22)
            tok("down1b", gT1)
            turn("n3", "normed", 6)
            acts("n3")
            tok("in2", actT)
            pe.wait_ge(ev("acc_free"), 2 + G["in2"].acc + G["in2"].blocks)
            pe.wait_ge(ev("kdup"), 1)
            for m, n in enumerate(TURN2):
                if m >= 8:
                    pe.wait_ge(ev("qt2_d" if m % 2 else "qt2_a"), (m - 8) // 2 + 1)
                for c in range(2):
                    for t in range(TT):
                        if n == 4:
                            src = kdup[:, t, c, :, :].rearrange("p u d -> p (u d)")
                        else:
                            at = C_QA + (2 * n + c) * P if n < 4 else C_QR + (2 * n + c - 16) * P
                            src = proj2[:, t, at:at + P]
                        last = nc.tensor.transpose(PS[:, m % 8, c * S + t * P:c * S + (t + 1) * P], src, ident[:, :])
                last.then_inc(ev("qt2_mm"), 1)
            pe.wait_ge(ev("qt2_a"), 7)
            pe.wait_ge(ev("qt2_d"), 6)
            pe.wait_ge(ev("ln_done"), 1)
            pe.wait_ge(ev("f_done"), 1)
            for n in range(4):
                for k in range(4):
                    h, t = 4 * (n % 2) + k, n // 2
                    last = nc.tensor.transpose(PS[:, n, k * P:(k + 1) * P], lnf[:, h, t * P:(t + 1) * P], ident[:, :])
                last.then_inc(ev("logf_mm"), 1)
            pe.wait_ge(ev("logf_out"), 4)
            for s in range(HA + 3):
                if s < HA:
                    if s >= 2:
                        pe.wait_ge(ev("max2"), s - 1)
                    rows = slice(64 * (s % 2), 64 * (s % 2) + 64)
                    q, k = QT2[rows, s // 2, :], QT2[rows, 8 + s // (HA // NKV), :]
                    nc.tensor.matmul(PS[:, s % 2, 0:P], q[:, 0:P], k[:, 0:P], start=True, stop=True)
                    nc.tensor.matmul(PS[:, s % 2, P:SK], q[:, P:S], k[:, 0:S], start=True, stop=True).then_inc(ev("log_mm2"), 1)
                if 2 <= s < HA + 2:
                    r = s - 2
                    pe.wait_ge(ev("exp2"), r + 1)
                    if r >= 2:
                        pe.wait_ge(ev("pt_out2"), r - 1)
                    for b in range(3):
                        last = nc.tensor.transpose(PS[:, 2 + r % 2, b * P:(b + 1) * P], scores2[:, r % 2, b * P:(b + 1) * P], ident[:, :])
                    last.then_inc(ev("pt_mm2"), 1)
                if s >= 3:
                    r = s - 3
                    pe.wait_ge(ev("pt_out2"), r + 1)
                    if r >= 2:
                        pe.wait_ge(ev("o_out2"), r - 1)
                    v = C_VA + r // (HA // NKV) * 64
                    pt, o = probsT2[:, r % 2, :], PS[:, 6 + r % 2, :]
                    nc.tensor.matmul(o[:, 0:64], pt[:, 0:P], proj2[:, 0, v:v + 64], start=True, stop=True)
                    nc.tensor.matmul(o[:, 64:P], pt[:, P:2 * P], proj2[:, 0, v:v + 64], start=True, stop=False)
                    nc.tensor.matmul(o[:, 64:P], pt[:, 2 * P:3 * P], proj2[:, 1, v:v + 64], start=False, stop=True)\
                        .then_inc(ev("pv_mm2"), 1)
            NR = HR * TT
            pe.wait_ge(ev("key_done"), 1)
            for n in range(NR + 2):
                if n < NR:
                    h, t = n // TT, n % TT
                    if n >= 1:
                        pe.wait_ge(ev("fac"), n)
                    lf = logf[:, t, h, :]
                    nc.tensor.matmul(PS[:, 0, :], lf, sums[:, 0:4, :].rearrange("p l t -> p (l t)"), start=True, stop=True)
                    nc.tensor.matmul(PS[:, 1, 0:3 * P], lf, sums[:, 4:7, :].rearrange("p l t -> p (l t)"), start=True, stop=True)
                    nc.tensor.matmul(PS[:, 1, 3 * P:4 * P], lf, sums[:, 7 + t, :], start=True, stop=True).then_inc(ev("exps_mm"), 1)
                if 1 <= n <= NR:
                    r = n - 1
                    h, t = r // TT, r % TT
                    pe.wait_ge(ev("qf"), r + 1)
                    pe.wait_ge(ev("kf"), r + 1)
                    if r >= 1:
                        pe.wait_ge(ev("att_out"), r)
                    if t == 1:
                        pe.wait_ge(ev("kcross_done"), h + 1)
                        if h >= 1:
                            pe.wait_ge(ev("cross_out"), h)
                        nc.tensor.matmul(PS[:, 4, 0:P], kcross[:, :], qf[:, 7, :], start=True, stop=True).then_inc(ev("cross_mm"), 1)
                    for l in range(8):
                        lhs = kf[:, l, :] if l < 7 else QT2[:, 24 + h, t * P:(t + 1) * P]
                        rhs = qf[:, l, :] if l < 7 else QT2[:, 16 + h, t * P:(t + 1) * P]
                        last = nc.tensor.matmul(PS[:, 2 + l // 4, (l % 4) * P:(l % 4 + 1) * P], lhs, rhs, start=True, stop=True)
                    last.then_inc(ev("att_mm"), 1)
                if n >= 2:
                    r = n - 2
                    h, t = r // TT, r % TT
                    pe.wait_ge(ev("att_out"), r + 1)
                    if r >= 1:
                        pe.wait_ge(ev("o_out"), r)
                    v = C_IR + h * P
                    if t == 0:
                        nc.tensor.matmul(PS[:, 5, 0:P], attT[:, :], proj2[:, 0, v:v + P], start=True, stop=True).then_inc(ev("o_mm"), 1)
                    else:
                        nc.tensor.matmul(PS[:, 5, 0:P], attT[:, :], proj2[:, 1, v:v + P], start=True, stop=False)
                        pe.wait_ge(ev("cross_out"), h + 1)
                        nc.tensor.matmul(PS[:, 5, 0:P], crossT[:, :], proj2[:, 0, v:v + P], start=False, stop=True).then_inc(ev("o_mm"), 1)
            pe.wait_ge(ev("o_out"), NR)
            pe.wait_ge(ev("ssq"), 6)
            turn("mix2", "mixed2", 4)
            acts("mix2")
            tok("out2", actT)
            turn("n4", "normed", 8)
            acts("n4")
            feat("up2a")
            pe.wait_ge(ev("g_lo"), 1 + 22 + 8)
            tok("down2a", gT2)
            pe.wait_ge(ev("acc_free"), 2 + G["down2a"].acc + 4)
            feat("up2b")
            pe.wait_ge(ev("g_lo"), 1 + 22 + 16)
            tok("down2b", gT2)


_INS = ["x", "pre_mix_norm", "w_in", "lambda_q1", "lambda_k1", "lambda_q2", "lambda_k2", "diff_subln", "cmp_pos_k",
        "cmp_pos_v", "cmp_k_w1", "cmp_k_w2", "cmp_v_w1", "cmp_v_w2", "rel_bias", "w_out", "post_mix_norm",
        "pre_ffn_norm", "w_up", "conv_w", "conv_b", "w_down", "post_ffn_norm", "w_in_2", "attn_sinks_2",
        "attn_out_gain_2", "rnn_lb_logits_2", "rnn_norm_gain_2", "w_out_2", "mix_pre_gain_2", "mix_post_gain_2",
        "mlp_pre_gain_2", "mlp_post_gain_2", "w_up_2", "w_down_2"]


def kernel(**inputs):
    import concourse.bacc as bacc
    from concourse.bass_utils import run_bass_kernel_spmd

    nc = bacc.Bacc("TRN2", target_bir_lowering=False, num_devices=1)
    arrays, w = {}, {}
    for name in _INS:
        a = np.ascontiguousarray(inputs[name])
        arrays[f"in_{name}"] = a
        w[name] = nc.dram_tensor(f"in_{name}", a.shape, F32, kind="ExternalInput").ap()
    for name, a in shape_constants().items():
        arrays[f"const_{name}"] = a
        w[name] = nc.dram_tensor(f"const_{name}", a.shape, F32, kind="ExternalInput").ap()
    out = nc.dram_tensor("out", (1, S, D), F32, kind="ExternalOutput").ap()
    scratch = nc.dram_tensor("bias_by_distance", (16, SK), F32, kind="Internal").ap()
    build(nc, w, out, scratch)
    r = run_bass_kernel_spmd(nc, [arrays], core_ids=[0])
    return r.results[0]["out"]
```

```python
import math

import numpy as np

import concourse.bass as bass
from concourse import mybir
from contextlib import ExitStack

F32 = mybir.dt.float32
F32R = mybir.dt.float32r
ALU = mybir.AluOpType
ACT = mybir.ActivationFunctionType
AX = mybir.AxisListType

P = 128
D = 2048
S = 256
TT = S // P
KC = D // P
EPS = 1e-6
NEG = -1e30
TINY = 1e-30

HD = 8
HN = 8
NKV = 2
GATES = HN * 3
NB_BUCKETS = 32
CMP_LEN, CMP_STRIDE, HID = 32, 16, 256
NC = (S - CMP_LEN) // CMP_STRIDE + 1
LAM_INIT = 0.8 - 0.6 * math.exp(0.0)
C_DQ, C_DK, C_DV, C_NQ = 0, 1024, 2048, 3072
C_KC, C_VC, C_KS, C_VS, C_KW, C_VW, C_G = 4096, 4352, 4608, 4864, 5120, 5376, 5632
IN1 = C_G + GATES
F1 = 5632
F2 = 8192
HA, HR = 16, 8
C_QA, C_KA, C_VA, C_QR, C_FR, C_IR, C_GR = 0, 1024, 1152, 1280, 2304, 3328, 4352
IN2 = 5376
SK = 384
LEVELS = (64, 32, 16, 8, 4, 2, 1)

STAGES = 8
SPLITS = 4
TILE = 1024
NW = 512
TC = TILE // NW
FW = 256
FC = TILE // FW
FT = 2 * KC // FC


class Gemm:

    def __init__(self, kind, first, blocks, tiles, acc=0, turned=0):
        self.kind, self.first, self.blocks, self.tiles, self.acc = kind, first, blocks, tiles, acc
        self.turned = turned


def plan():
    out, n, acc, up = {}, 0, 0, 0
    order = [("in1", "tok", 12, 8), ("cmp", "raw", 1, 16), ("out1", "tok", 4, 8),
             ("up1a", "feat", 12, FT), ("down1a", "tok", 4, 12), ("up1b", "feat", 10, FT), ("down1b", "tok", 4, 10),
             ("in2", "tok", 11, 8), ("out2", "tok", 4, 8),
             ("up2a", "feat", 8, FT), ("down2a", "tok", 4, 16), ("up2b", "feat", 8, FT), ("down2b", "tok", 4, 16)]
    for name, kind, blocks, tiles in order:
        out[name] = Gemm(kind, n, blocks, tiles, up if kind == "feat" else acc, int(name in ("up1b", "down1b", "up2b", "down2b")))
        assert n % STAGES == 0
        n += blocks * tiles
        if kind == "tok":
            acc += blocks
        if kind == "feat":
            up += blocks
    return out


def buckets(d):
    half = NB_BUCKETS // 2
    if d < half:
        return d
    return min(half + int(math.log(d / half) / math.log(128 / half) * half), NB_BUCKETS - 1)


def shape_constants():
    i = np.arange(P)
    c = {}
    c["ident"] = np.eye(P, dtype=np.float32)
    c["flip"] = np.eye(P, dtype=np.float32)[::-1].copy()
    onehot = np.zeros((NB_BUCKETS, SK), np.float32)
    for m in range(S):
        onehot[buckets(S - 1 - m), m] = 1.0
    c["onehot"] = onehot
    far = np.full((P, SK), 1e34, np.float32)
    for q in range(P):
        for lo, hi, off in ((0, 128, 0), (128, 256, 256), (256, 384, 256)):
            for col in range(lo, hi):
                d = off + q - col if lo != 0 else q - col
                if 0 <= d < P:
                    far[q, col] = d
    c["far"] = far
    ends = np.zeros((P, TT, NC), np.float32)
    for t in range(TT):
        for n in range(NC):
            ends[:, t, n] = (n * CMP_STRIDE + CMP_LEN - 1 <= t * P + i)
    c["cmp_keep"] = ends
    c["cmp_drop"] = ((1.0 - ends) * NEG).astype(np.float32)
    sums = np.zeros((P, 9, P), np.float32)
    keep = np.zeros((P, 8, P), np.float32)
    u, t = i[:, None], i[None, :]
    for n, ln in enumerate(LEVELS):
        mid = t // (2 * ln) * (2 * ln) + ln
        sums[:, n, :] = np.where(t >= mid, (u >= mid) & (u <= t), (u > t) & (u < mid))
        same = u // (2 * ln) == t // (2 * ln)
        keep[:, n, :] = same & (u % (2 * ln) < ln) & (t % (2 * ln) >= ln)
    sums[:, 7, :] = u > t
    sums[:, 8, :] = u <= t
    keep[:, 7, :] = u == t
    c["sums"] = sums
    c["keep"] = keep
    return c


def layout(a):
    return a


def build(nc, w, out, scratch):
    G = plan()
    ctx = ExitStack()
    sems = {}

    def ev(name):
        if name not in sems:
            sems[name] = ctx.enter_context(nc.semaphore(name))
        return sems[name]

    with ctx:
        def sb(name, shape, dt=F32, on=ctx):
            return on.enter_context(nc.sbuf_tensor(name, shape, dt))

        stage = sb("stage", [P, STAGES, TILE])
        whi = sb("whi", [P, SPLITS, TILE], F32R)
        wlo = sb("wlo", [P, SPLITS, TILE], F32R)
        x = sb("x", [P, TT, D])
        ident = sb("ident", [P, P])
        grow = sb("grow", [P, D])
        cols = sb("cols", [P, 96])
        posT = sb("posT", [P, 2, CMP_LEN])
        convT = sb("convT", [P, 4, 2 * F1 // P])
        small = sb("small", [P, 24])
        hstat = sb("hstat", [P, 3, 16])
        lbs = sb("lbs", [P, 48])
        half = sb("half", [P, 1])
        stat = sb("stat", [P, 2, 16])
        here = ExitStack()
        actT = sb("actT", [P, KC, 2 * S], F32R, here)
        here.close()
        mixer1 = ExitStack()
        QT = sb("QT", [P, 32, S], F32, mixer1)
        proj = sb("proj", [P, TT, IN1], F32, mixer1)
        bias = sb("bias", [P, 16, SK], F32, mixer1)
        work = sb("work", [P, 3072], F32, mixer1)
        gates = sb("gates", [P, TT, GATES], F32, mixer1)
        mixer1.close()
        scores = work[:, 0:4 * SK].rearrange("p (a m k) -> p a m k", a=2, m=2)
        probs = work[:, 4 * SK:6 * SK].rearrange("p (a k) -> p a k", a=2)
        probsT = work[:, 6 * SK:8 * SK].rearrange("p (a k) -> p a k", a=2)
        flat = proj[:, :, :].rearrange("p t n -> p (t n)")
        hankel = flat[:, 4096:8192].rearrange("p (h j) -> p h j", h=16)
        vecs = flat[:, 8192:8192 + 6 * P].rearrange("p (r j) -> p r j", r=6)
        lamv = work[:, 0:256].rearrange("p (a c) -> p a c", a=4)
        tab = work[0:NB_BUCKETS, 512:528]
        hot = work[0:NB_BUCKETS, 1024:1024 + SK]
        flip = work[:, 1536:1664]
        urow = work[0:16, 2048:2048 + SK]
        blocks = grow[:, 0:2 * CMP_LEN * NKV * NC].rearrange("p (v l g c) -> p v l g c", v=2, l=CMP_LEN, g=NKV)
        w2 = proj[:, 0, C_KC:C_KC + 512].rearrange("p (v a n) -> p v a n", v=2, a=2)
        hid = proj[:, 1, C_KC:C_KC + 4 * 2 * NC].rearrange("p (v a c) -> p v a c", v=2, a=2)
        kcT = proj[:, 1, C_KC + 128:C_KC + 128 + 2 * NC]
        vc = proj[0:NC, 1, C_KC + 192:C_KC + 192 + NKV * P].rearrange("p (g d) -> p g d", g=NKV)
        pcs = proj[:, 0, C_DK:C_DK + HN * TT * NC].rearrange("p (h t c) -> p h t c", h=HN, t=TT)
        keepc = proj[:, 0, C_DK + 256:C_DK + 256 + 2 * TT * NC].rearrange("p (a t c) -> p a t c", a=2, t=TT)
        cst = proj[:, 0, C_DK + 384:C_DK + 384 + 3 * HN * TT].rearrange("p (a h t) -> p a h t", a=3, h=HN)
        pcT = probs[0:NC, :, 0:P]
        mixer2 = ExitStack()
        QT2 = sb("QT2", [P, 32, S], F32, mixer2)
        proj2 = sb("proj2", [P, TT, IN2], F32, mixer2)
        far = sb("far", [P, SK], F32, mixer2)
        scores2 = sb("scores2", [P, 2, SK], F32, mixer2)
        probsT2 = sb("probsT2", [P, 2, SK], F32, mixer2)
        sinks = sb("sinks", [P, 2, HA], F32, mixer2)
        sums = sb("sums", [P, 9, P], F32, mixer2)
        keep = sb("keep", [P, 8, P], F32, mixer2)
        logf = sb("logf", [P, TT, HR, P], F32, mixer2)
        fackf = sb("fackf", [P, 2, 8, P], F32, mixer2)
        kcross = sb("kcross", [P, P], F32, mixer2)
        attT = sb("attT", [P, P], F32, mixer2)
        crossT = sb("crossT", [P, P], F32, mixer2)
        mixer2.close()
        kdup = QT2[:, 10:12, :].rearrange("p t (v u d) -> p t v u d", v=NKV, u=2)
        fac = fackf[:, 0, :, :]
        kf = fackf[:, 1, :, :]
        attm = proj2[:, 0, C_QR:C_QR + 1024].rearrange("p (l t) -> p l t", l=8)
        qf = proj2[:, 1, C_QR:C_QR + 1024].rearrange("p (l t) -> p l t", l=8)
        sig_q = logf[:, :, :, :].rearrange("p t h k -> p (t h k)").rearrange("p (h s) -> p h s", h=HR)
        lnf = fackf[:, :, :, :].rearrange("p a l t -> p (a l t)").rearrange("p (h s) -> p h s", h=HR)
        sig_g = fackf[:, :, :, :].rearrange("p a l t -> p a (l t)")
        ffn = ExitStack()
        sb("actT_place", [P, KC, 2 * S], F32R, ffn)
        yacc = sb("yacc", [P, TT, D], F32, ffn)
        both = ExitStack()
        gT1 = sb("gT1", [P, 24, 2 * S], F32R, both)
        pre = sb("pre", [P, 4, S + 2], F32, both)
        both.close()
        gT2 = sb("gT2", [P, 32, 2 * S], F32R, ffn)
        ffn.close()
        lowsum = grow[:, 0:4 * S].rearrange("p (a s) -> p a s", a=4)
        post = grow[:, 4 * S:8 * S].rearrange("p (a s) -> p a s", a=4)

        PS = ctx.enter_context(nc.psum_tensor("PS", [P, 8, 512], F32))

        ln = {"dve": 0, "act": 0, "pool": 0}

        def then(eng, name, ins):
            ln[name] += 1
            ins.then_inc(ev("self_" + name), 1)
            eng.wait_ge(ev("self_" + name), ln[name])

        GAIN = {"n1": 0, "n2": 16, "n3": 32, "n4": 48, "attn": 64, "subln": 72, "rnn": 73, "one": 74}
        C_LB = 76

        def gain_of(turn, c):
            if turn == "mix1":
                at = GAIN["subln"] if c < HD else GAIN["one"]
            elif turn == "mix2":
                at = GAIN["attn"] + c if c < 8 else GAIN["rnn"]
            else:
                at = GAIN[turn] + c
            return cols[:, at:at + 1]

        def src_of(turn, t, c):
            if turn == "mix1":
                at = C_DQ + c * P if c < HD else C_NQ + (c - HD) * P
                return proj[:, t, at:at + P]
            if turn == "mix2":
                at = C_QA + c * P if c < 8 else C_IR + (c - 8) * P
                return proj2[:, t, at:at + P]
            return yacc[:, t, c * P:(c + 1) * P]

        WT = {"in1": (w["w_in"][0], 0), "out1": (w["w_out"][0], 0),
              "down1a": (w["w_down"][0], 0), "down1b": (w["w_down"][0], 24),
              "in2": (w["w_in_2"][0], 0), "out2": (w["w_out_2"][0], 0),
              "down2a": (w["w_down_2"][0], 0), "down2b": (w["w_down_2"][0], 32)}
        UP = {"up1a": (w["w_up"][0], 0, F1, 256), "up1b": (w["w_up"][0], 12 * 256, F1, 256),
              "up2a": (w["w_up_2"][0], 0, 256, 512), "up2b": (w["w_up_2"][0], 8 * 512, 256, 512)}
        PAIRS = {"in1": 5, "out1": 2, "down1a": 2, "down1b": 0, "in2": 5, "out2": 2, "down2a": 2, "down2b": 2}
        WIDTH = {("in1", 11): GATES, ("in2", 10): 256}

        def width(name, b):
            return WIDTH.get((name, b), NW)

        def used(n):
            return n + SPLITS

        def tok_order(eng, name, tile, take, before, defer):
            g, pairs = G[name], PAIRS[name]
            T = g.tiles

            def one(i, b, base, prev):
                for j in range(T):
                    tile(i, b, j, base + j)
                    if j == SPLITS - 1:
                        if prev is not None and take is not None:
                            take(*prev)
                        if prev is None and before is not None:
                            before()
            if pairs:
                for b in range(2):
                    one(0, b, g.first + b * T, (0, 0) if b else None)
                with eng.Fori(1, pairs) as i:
                    for b in range(2):
                        one(i, b, i * (2 * T) + (g.first + b * T), (i, 0) if b else (i - 1, 1))
            for b in range(2 * pairs, g.blocks):
                one(None, b, g.first + b * T, (None, b - 1) if b else None)
            if defer:
                return lambda: take(None, g.blocks - 1)
            if take is not None:
                take(None, g.blocks - 1)

        def place(name, i, b):
            if i is None:
                return b * NW, b, b % 2, width(name, b)
            return i * (2 * NW) + b * NW, i * 2 + b, b, NW

        def span(start, size):
            return slice(start, start + size) if isinstance(start, int) else bass.ds(start, size)

        def turn_at(name, i, s):
            g = G[name]
            k = (g.first + s) // STAGES + 1
            return 16 * k if i is None else i * (2 * g.tiles // STAGES * 16) + 16 * k

        block = ctx.enter_context(nc.Block())

        @block.sync
        def _(sp):
            def tile_in(slot, n, src, dst):
                sp.wait_ge(ev("lo_done"), n + 1)
                sp.dma_start(dst, src).then_inc(ev(f"landed{slot}"), 16)

            def tok_block(name, i, b, base):
                m, k0 = WT[name]
                col, _, _, wd = place(name, i, b)
                for j in range(G[name].tiles):
                    k = k0 + TC * j
                    slot = (b * G[name].tiles + j) % STAGES
                    tile_in(slot, base + j, m[k * P:(k + TC) * P, span(col, wd)].rearrange("(c p) n -> p c n", p=P),
                            stage[:, slot, 0:TC * wd].rearrange("p (c n) -> p c n", c=TC))

            def tok(name):
                g = G[name]
                if PAIRS[name]:
                    with sp.Fori(0, PAIRS[name]) as i:
                        for b in range(2):
                            tok_block(name, i, b, i * (2 * g.tiles) + (g.first + b * g.tiles))
                for b in range(2 * PAIRS[name], g.blocks):
                    tok_block(name, None, b, g.first + b * g.tiles)

            def feat(name):
                m, c0, other, step = UP[name]
                with sp.Fori(0, G[name].blocks) as i:
                    for j in range(FT):
                        q, kh = j // (FT // 2), j % (FT // 2)
                        src = m[kh * FC * P:(kh + 1) * FC * P, bass.ds(i * step + (c0 + q * other), FW)]
                        tile_in(j, i * FT + (G[name].first + j), src.rearrange("(c p) n -> p c n", p=P),
                                stage[:, j, :].rearrange("p (c n) -> p c n", c=FC))

            tok("in1")
            for j in range(G["cmp"].tiles):
                m = (w["cmp_k_w1"], w["cmp_v_w1"])[j // 8][0]
                r = (j % 8) * FC * P
                tile_in(j % STAGES, G["cmp"].first + j, m[r:r + FC * P, :].rearrange("(c p) n -> p c n", p=P),
                        stage[:, j % STAGES, :].rearrange("p (c n) -> p c n", c=FC))
            tok("out1")
            feat("up1a")
            tok("down1a")
            feat("up1b")
            tok("down1b")
            tok("in2")
            tok("out2")
            feat("up2a")
            tok("down2a")
            feat("up2b")
            tok("down2b")
            for t in range(TT):
                sp.wait_ge(ev("resid"), 3 * TT + t + 1)
                sp.dma_start(out[0, t * P:(t + 1) * P, :], x[:, t, :]).then_inc(ev("stored"), 16)
            sp.wait_ge(ev("stored"), 16 * TT)

        @block.gpsimd
        def _(pool):
            pool.dma_start(x[:, :, :], w["x"][0].rearrange("(t p) n -> p t n", p=P)).then_inc(ev("x_in"), 16)
            pool.dma_start(tab, w["rel_bias"]).then_inc(ev("tab_in"), 16)
            pool.dma_start(hot, w["onehot"]).then_inc(ev("tab_in"), 16)
            pool.dma_start(ident[:, :], w["ident"]).then_inc(ev("ident_in"), 16)
            pool.dma_start(flip, w["flip"]).then_inc(ev("ident_in"), 16)
            for r0, nm, k in ((0, "pre_mix_norm", 16), (16, "pre_ffn_norm", 16), (32, "mix_pre_gain_2", 16),
                              (48, "mlp_pre_gain_2", 16), (64, "attn_out_gain_2", 8), (72, "diff_subln", 1),
                              (73, "rnn_norm_gain_2", 1)):
                pool.dma_start(vecs[r0:r0 + k, 0, :], w[nm][0].rearrange("(r f) -> r f", f=P)).then_inc(ev("vecs_in"), 16)
            pool.dma_start(vecs[74:90, 0, :], w["rnn_lb_logits_2"].rearrange("l (r f) -> (l r) f", f=P)).then_inc(ev("vecs_in"), 16)
            pool.dma_start(vecs[0:CMP_LEN, 1, :], w["cmp_pos_k"][0]).then_inc(ev("vecs_in"), 16)
            pool.dma_start(vecs[CMP_LEN:2 * CMP_LEN, 1, :], w["cmp_pos_v"][0]).then_inc(ev("vecs_in"), 16)
            for j in range(3):
                pool.dma_start(vecs[0:88, 2 + j, :], w["conv_w"][0, j].rearrange("(r f) -> r f", f=P)).then_inc(ev("vecs_in"), 16)
            pool.dma_start(vecs[0:88, 5, :], w["conv_b"][0].rearrange("(r f) -> r f", f=P)).then_inc(ev("vecs_in"), 16)
            for j, nm in enumerate(("lambda_q1", "lambda_q2", "lambda_k1", "lambda_k2")):
                pool.dma_start(lamv[:, j, :], w[nm][0:1, :].broadcast_to((P, 64))).then_inc(ev("lam_in"), 16)
            pool.memset(half[:, :], -0.5).then_inc(ev("half_set"), 1)
            pool.wait_ge(ev("urow"), 2)
            pool.dma_start(scratch, urow).then_inc(ev("scratch_out"), 16)
            pool.wait_ge(ev("scratch_out"), 16)
            pool.dma_start(hankel, bass.AP(scratch.tensor, 0, [[1, P], [SK, 16], [1, S]])).then_inc(ev("hankel_in"), 16)
            pool.wait_ge(ev("half_set"), 1)

            def inv_sqrt(n, dst, src, k):
                pool.wait_ge(ev("var"), n)
                pool.tensor_tensor(dst, src, half[:, 0:1].broadcast_to((P, k)), ALU.pow).then_inc(ev("rstd"), 1)

            inv_sqrt(1, small[:, 4:6], small[:, 2:4], 2)
            pool.wait_ge(ev("qt_a"), 1)
            pool.wait_ge(ev("qt_d"), 1)
            for j, nm in enumerate(("cmp_k_w2", "cmp_v_w2")):
                pool.dma_start(w2[:, j, :, :], w[nm][0].rearrange("(a p) n -> p a n", p=P)).then_inc(ev("w2_in"), 16)
            pool.wait_ge(ev("cols"), 1)
            for v in range(2):
                for g in range(NKV):
                    for a in range(2):
                        src = QT[:, 24 + 2 * v + g, 16 * a:16 * a + 16 * NC].rearrange("p (c b) -> p b c", b=16)
                        add = posT[:, v, 16 * a:16 * a + 16].rearrange("p (b o) -> p b o", o=1).broadcast_to((P, 16, NC))
                        pool.tensor_tensor(blocks[:, v, 16 * a:16 * a + 16, g, :], src, add, ALU.add).then_inc(ev("blocks_done"), 1)
            pool.wait_ge(ev("qt_a"), 8)
            pool.wait_ge(ev("qt_d"), 8)
            pool.dma_start(keepc[:, 0, :, :], w["cmp_keep"]).then_inc(ev("keep_in"), 16)
            pool.dma_start(keepc[:, 1, :, :], w["cmp_drop"]).then_inc(ev("keep_in"), 16)
            pool.wait_ge(ev("tile_used"), used(G["cmp"].first + G["cmp"].tiles))
            pool.dma_start(grow[:, :], w["post_mix_norm"][0:1, :].broadcast_to((P, D))).then_inc(ev("grow_in"), 16)
            inv_sqrt(2, hstat[:, 2, :], hstat[:, 1, :], 16)
            inv_sqrt(3, small[:, 4:6], small[:, 2:4], 2)
            inv_sqrt(4, small[:, 4:6], small[:, 2:4], 2)
            pool.wait_ge(ev("g_lo"), 1 + 22)
            pool.dma_start(grow[:, :], w["post_ffn_norm"][0:1, :].broadcast_to((P, D))).then_inc(ev("grow_in"), 16)
            inv_sqrt(5, small[:, 4:6], small[:, 2:4], 2)
            pool.wait_ge(ev("resid"), 4)
            pool.dma_start(grow[:, :], w["mix_post_gain_2"][0:1, :].broadcast_to((P, D))).then_inc(ev("grow_in"), 16)
            pool.dma_start(far[:, :], w["far"]).then_inc(ev("mix2_in"), 16)
            pool.dma_start(sinks[:, 0, :], w["attn_sinks_2"][0:1, :].broadcast_to((P, HA))).then_inc(ev("mix2_in"), 16)
            pool.dma_start(sums[:, :, :], w["sums"]).then_inc(ev("mix2_in"), 16)
            pool.dma_start(keep[:, :, :], w["keep"]).then_inc(ev("mix2_in"), 16)
            inv_sqrt(6, small[:, 4:6], small[:, 2:4], 2)
            pool.wait_ge(ev("key_done"), 1)
            for n in range(HR * TT):
                h, t = n // TT, n % TT
                key = QT2[:, 24 + h, t * P:(t + 1) * P]
                pool.wait_ge(ev("fac"), n + 1)
                if t == 0:
                    if h >= 1:
                        pool.wait_ge(ev("cross_mm"), h)
                    pool.tensor_tensor(kcross[:, :], fac[:, 7, :], key, ALU.mult).then_inc(ev("kcross_done"), 1)
                if n >= 1:
                    pool.wait_ge(ev("att_mm"), n)
                many = key.rearrange("p (o t) -> p o t", o=1).broadcast_to((P, 7, P))
                pool.tensor_tensor(kf[:, 0:7, :], fac[:, 0:7, :], many, ALU.mult).then_inc(ev("kf"), 1)
            inv_sqrt(7, small[:, 4:6], small[:, 2:4], 2)
            inv_sqrt(8, hstat[:, 2, :], hstat[:, 1, :], 16)
            inv_sqrt(9, small[:, 4:6], small[:, 2:4], 2)
            inv_sqrt(10, small[:, 4:6], small[:, 2:4], 2)
            pool.wait_ge(ev("g_lo"), 1 + 22 + 16)
            pool.dma_start(grow[:, :], w["mlp_post_gain_2"][0:1, :].broadcast_to((P, D))).then_inc(ev("grow_in"), 16)
            inv_sqrt(11, small[:, 4:6], small[:, 2:4], 2)

        NBR = HD + 2 * HN

        def bank_of(first, r):
            return first if r <= HD else first + 2 * (r % 2)
        TURN1 = [12, 13] + list(range(12)) + [14, 15]
        TURN2 = [0, 1, 2, 3, 4, 8, 9, 10, 11, 12, 13, 14, 15]

        @block.scalar
        def _(act):
            squares = [PS[:, 4 * t:4 * t + 4, :].rearrange("p b n -> p (b n)") for t in range(TT)]

            def tok(name, dst, before=None, defer=False):
                g = G[name]

                def tile(i, b, j, n):
                    s = b * g.tiles + j
                    wd = TC * (width(name, b) if i is None else NW)
                    act.wait_ge(ev("tile_used"), used(n - SPLITS + 1))
                    act.wait_ge(ev(f"landed{s % STAGES}"), turn_at(name, i, s))
                    nc.scalar.activation(whi[:, s % SPLITS, 0:wd], stage[:, s % STAGES, 0:wd], ACT.Copy)\
                        .then_inc(ev("hi_done"), 1)

                def take(i, b):
                    col, nb, bank, wd = place(name, i, b)
                    act.wait_ge(ev("tile_used"), used((nb + 1) * g.tiles + g.first))
                    act.wait_ge(ev("begun"), 1)
                    for t in range(TT):
                        last = nc.scalar.activation(dst[:, t, span(col, wd)], PS[:, 4 * g.turned + 2 * bank + t, 0:wd], ACT.Copy)
                    last.then_inc(ev("acc_free"), 1)
                tail = tok_order(act, name, tile, take if dst is not None else None, before, defer)
                if tail is not None:
                    return tail
                if dst is not None:
                    act.wait_ge(ev("acc_free"), 2 + g.acc + g.blocks)

            def sum_squares(src, junk=None):
                for t in range(TT):
                    last = nc.scalar.activation(squares[t] if junk is None else junk[:, t, :], src[:, t, :], ACT.Square, accum_out=small[:, t:t + 1])
                last.then_inc(ev("ssq"), 1)

            def split_turned(turn):
                for c in range(KC):
                    act.wait_ge(ev("turned_" + turn), c // 2 + 1)
                    nc.scalar.activation(actT[:, c, 0:S], PS[:, c // 2, (c % 2) * S:(c % 2 + 1) * S], ACT.Copy,
                                         scale=gain_of(turn, c)).then_inc(ev("acthi_" + turn), 1)

            def feat(name, conv, before=None):
                g = G[name]
                gT = gT1 if conv else gT2

                def tiles(i, js):
                    for j in js:
                        act.wait_ge(ev("tile_used"), used(i * FT + (g.first + j - SPLITS + 1)))
                        act.wait_ge(ev(f"landed{j}"), i * 16 + (g.first // STAGES + 1) * 16)
                        nc.scalar.activation(whi[:, j % SPLITS, :], stage[:, j, :], ACT.Copy).then_inc(ev("hi_done"), 1)

                def low_sums(i, s):
                    act.wait_ge(ev("tile_used"), used(i * FT + (g.first + FT)))
                    nc.scalar.activation(lowsum, PS[:, 4 * (s ^ g.turned):4 * (s ^ g.turned) + 4, S:2 * S], ACT.Copy).then_inc(ev("low_out"), 1)

                def first_tap(i):
                    act.wait_ge(ev("g_lo"), i + (g.acc + 1))
                    act.wait_ge(ev("pre_done"), i + (g.acc + 3))
                    act.wait_ge(ev("begun"), 1)
                    for a in range(4):
                        f = i * 2 + (2 * (g.acc if name == "up1b" else 0) + a % 2 + F1 // P * (a // 2))
                        nc.scalar.activation(post[:, a, :], pre[:, a, 2:2 + S], ACT.Identity,
                                             scale=convT[:, 2, span(f, 1)], bias=convT[:, 3, span(f, 1)])\
                            .then_inc(ev("tap"), 1)

                def high_parts(i):
                    if conv:
                        act.wait_ge(ev("conv_done"), i + (g.acc + 1))
                        nc.scalar.activation(lowsum[:, 0:2, :], post[:, 0:2, :], ACT.Gelu_apprx_tanh).then_inc(ev("gelu"), 1)
                    k = 2 if conv else 4
                    act.wait_ge(ev("prod"), i + (g.acc + 1))
                    act.wait_ge(ev("begun"), 1)
                    nc.scalar.activation(gT[:, span(i * k, k), 0:S], post[:, 0:k, :], ACT.Copy).then_inc(ev("g_hi"), 1)

                def one(i, s, prev):
                    tiles(i, (0, 1, 2, 3))
                    if prev is None and before is not None:
                        before()
                    if prev is not None:
                        low_sums(prev, 1 - s)
                        if conv:
                            first_tap(prev)
                    tiles(i, (4, 5))
                    if prev is not None:
                        high_parts(prev)
                    tiles(i, (6, 7))
                one(0, 0, None)
                one(1, 1, 0)
                with act.Fori(1, g.blocks // 2) as r:
                    one(r * 2, 0, r * 2 - 1)
                    one(r * 2 + 1, 1, r * 2)

                def tail():
                    low_sums(g.blocks - 1, 1)
                    if conv:
                        first_tap(g.blocks - 1)
                    high_parts(g.blocks - 1)
                return tail

            act.sem_inc(ev("begun"), 1)
            act.wait_ge(ev("x_in"), 16)
            sum_squares(x, yacc)
            split_turned("n1")
            act.wait_ge(ev("lam_dot"), 1)
            nc.scalar.activation(small[:, 10:12], small[:, 8:10], ACT.Exp)
            nc.scalar.activation(lbs[:, 16:32], lbs[:, 0:16], ACT.Exp).then_inc(ev("early_exp"), 1)
            tok("in1", proj)
            for m in range(0, 16, 2):
                n = TURN1[m]
                act.wait_ge(ev("qt_mm"), m + 1)
                root = 64 ** -0.5 if n < 4 else P ** -0.5 if 8 <= n < 12 else 1.0
                nc.scalar.activation(QT[:, 2 * n:2 * n + 2, :].rearrange("p c s -> p (c s)"), PS[:, m % 8, :], ACT.Copy,
                                     scale=root).then_inc(ev("qt_a"), 1)
            nc.scalar.activation(gates[:, :, :], proj[:, :, C_G:C_G + GATES], ACT.Sigmoid).then_inc(ev("gates_done"), 1)

            def compress(s):
                if s in (4, 8):
                    v = s // 4 - 1
                    act.wait_ge(ev("tile_used"), used(G["cmp"].first + STAGES * (v + 1)))
                    nc.scalar.activation(hid[:, v, :, :], PS[:, 6:8, 0:2 * NC], ACT.Gelu_apprx_tanh).then_inc(ev("hid_done"), 1)
                if s == 8:
                    act.sem_inc(ev("hi_done"), G["cmp"].tiles)

            for s in range(NBR + 2):
                compress(s)
                if s < NBR:
                    act.wait_ge(ev("max1"), s + 1)
                    for m in range(2 if s < HD else 1):
                        for q, (lo, hi) in enumerate(((0, P), (P, SK))):
                            last = nc.scalar.activation(scores[:, s % 2, m, lo:hi], scores[:, s % 2, m, lo:hi], ACT.Exp,
                                                        bias=stat[:, s % 2, 2 * m + q:2 * m + q + 1],
                                                        accum_out=stat[:, s % 2, 4 + 2 * m + q:5 + 2 * m + q])
                    last.then_inc(ev("exp1"), 1)
                if s >= 2:
                    act.wait_ge(ev("pt_mm1"), s - 1)
                    if s >= 4:
                        act.wait_ge(ev("pv_mm1"), s - 3)
                    last = nc.scalar.activation(probsT[:, s % 2, :], PS[:, bank_of(4, s - 2), 0:SK], ACT.Copy)
                    if s - 2 >= HD:
                        last = nc.scalar.activation(pcT[:, s % 2, :], PS[0:NC, bank_of(4, s - 2), SK:SK + P], ACT.Copy)
                    last.then_inc(ev("pt_out1"), 1)
                if s == 9:
                    act.wait_ge(ev("cmp_shift"), 1)
                    nc.scalar.activation(pcs, pcs, ACT.Exp).then_inc(ev("cmp_exp"), 1)
            act.wait_ge(ev("o_out1"), NBR)
            for n in range(HD * TT):
                h, t = n // TT, n % TT
                last = nc.scalar.activation(work[:, n * P:(n + 1) * P], proj[:, t, C_DQ + h * P:C_DQ + (h + 1) * P], ACT.Square,
                                            accum_out=hstat[:, 0, n:n + 1])
            last.then_inc(ev("hssq"), 1)
            split_turned("mix1")
            tok("out1", yacc)
            sum_squares(yacc)
            act.wait_ge(ev("resid"), 2)
            sum_squares(x)
            split_turned("n2")
            last_up = feat("up1a", True)
            last_down = tok("down1a", yacc, before=last_up, defer=True)
            last_up = feat("up1b", True, before=last_down)
            tok("down1b", None, before=last_up)
            act.wait_ge(ev("acc_free"), 2 + G["down1b"].acc + 4)
            sum_squares(yacc)
            act.wait_ge(ev("resid"), 4)
            sum_squares(x)
            split_turned("n3")
            tok("in2", proj2)
            for m, n in enumerate(TURN2):
                if m % 2 == 0:
                    act.wait_ge(ev("qt2_mm"), m + 1)
                    nc.scalar.activation(QT2[:, 2 * n:2 * n + 2, :].rearrange("p c s -> p (c s)"), PS[:, m % 8, :], ACT.Copy,
                                         scale=64 ** -0.5 if n < 4 else 1.0).then_inc(ev("qt2_a"), 1)
            act.wait_ge(ev("qt2_a"), 7)
            act.wait_ge(ev("qt2_d"), 6)
            nc.scalar.activation(sig_q, QT2[:, 16:24, :], ACT.Sigmoid).then_inc(ev("sig"), 1)
            nc.scalar.activation(QT2[:, 24:32, :], QT2[:, 24:32, :], ACT.Sigmoid).then_inc(ev("sig"), 1)
            nc.scalar.activation(sig_g, proj2[:, :, C_GR:C_GR + 1024], ACT.Sigmoid).then_inc(ev("sig"), 1)
            act.wait_ge(ev("f_done"), 1)
            nc.scalar.activation(lnf, QT2[:, 24:32, :], ACT.Ln).then_inc(ev("ln_done"), 1)
            for n in range(4):
                act.wait_ge(ev("logf_mm"), n + 1)
                nc.scalar.activation(logf[:, n // 2, 4 * (n % 2):4 * (n % 2) + 4, :].rearrange("p a b -> p (a b)"),
                                     PS[:, n, :], ACT.Copy).then_inc(ev("logf_out"), 1)
            for s in range(HA + 2):
                if s < HA:
                    act.wait_ge(ev("max2"), s + 1)
                    for q, (lo, hi) in enumerate(((0, P), (P, SK))):
                        nc.scalar.activation(scores2[:, s % 2, lo:hi], scores2[:, s % 2, lo:hi], ACT.Exp,
                                             bias=stat[:, s % 2, q:q + 1], accum_out=stat[:, s % 2, 4 + q:5 + q])
                    nc.scalar.activation(stat[:, s % 2, 6:8], stat[:, s % 2, 0:2], ACT.Exp,
                                         bias=sinks[:, 0, s:s + 1]).then_inc(ev("exp2"), 1)
                if s >= 2:
                    act.wait_ge(ev("pt_mm2"), s - 1)
                    if s >= 4:
                        act.wait_ge(ev("pv_mm2"), s - 3)
                    nc.scalar.activation(probsT2[:, s % 2, :], PS[:, 2 + s % 2, 0:SK], ACT.Copy).then_inc(ev("pt_out2"), 1)
            def cross_out(h):
                act.wait_ge(ev("cross_mm"), h + 1)
                if h >= 1:
                    act.wait_ge(ev("o_mm"), 2 * h)
                nc.scalar.activation(crossT[:, :], PS[:, 4, 0:P], ACT.Copy).then_inc(ev("cross_out"), 1)

            def o_out(n):
                h, t = n // TT, n % TT
                act.wait_ge(ev("o_mm"), n + 1)
                nc.scalar.activation(proj2[:, t, C_FR + h * P:C_FR + (h + 1) * P], PS[:, 5, 0:P], ACT.Copy)
                nc.scalar.activation(PS[:, 5, P:2 * P], PS[:, 5, 0:P], ACT.Square, accum_out=hstat[:, 0, n:n + 1])\
                    .then_inc(ev("o_out"), 1)

            NR = HR * TT
            for n in range(NR + 2):
                if n < NR:
                    act.wait_ge(ev("exps_mm"), n + 1)
                    if n >= 1:
                        act.wait_ge(ev("qf"), n)
                        act.wait_ge(ev("kf"), n)
                    nc.scalar.activation(fac.rearrange("p a b -> p (a b)"), PS[:, 0:2, :].rearrange("p a b -> p (a b)"),
                                         ACT.Exp).then_inc(ev("fac"), 1)
                if 1 <= n <= NR and (n - 1) % TT == 1:
                    cross_out((n - 1) // TT)
                if n >= 2:
                    o_out(n - 2)
            act.wait_ge(ev("o_out2"), HA)
            act.wait_ge(ev("o_out"), NR)
            for t in range(TT):
                last = nc.scalar.activation(squares[t][:, 0:1024], proj2[:, t, C_QA:C_QA + 1024],
                                            ACT.Square, accum_out=small[:, t:t + 1])
            last.then_inc(ev("ssq"), 1)
            split_turned("mix2")
            tok("out2", yacc)
            sum_squares(yacc)
            act.wait_ge(ev("resid"), 6)
            sum_squares(x)
            split_turned("n4")
            last_up = feat("up2a", False)
            last_down = tok("down2a", yacc, before=last_up, defer=True)
            last_up = feat("up2b", False, before=last_down)
            tok("down2b", None, before=last_up)
            act.wait_ge(ev("acc_free"), 2 + G["down2b"].acc + 4)
            sum_squares(yacc)

        @block.vector
        def _(dve):
            def tok(name, add, before=None):
                g = G[name]

                def tile(i, b, j, n):
                    s = b * g.tiles + j
                    wd = TC * (width(name, b) if i is None else NW)
                    dve.wait_ge(ev("hi_done"), n + 1)
                    nc.vector.tensor_tensor(wlo[:, s % SPLITS, 0:wd], stage[:, s % STAGES, 0:wd],
                                            whi[:, s % SPLITS, 0:wd].bitcast(F32), ALU.subtract).then_inc(ev("lo_done"), 1)

                def take(i, b):
                    col, nb, bank, wd = place(name, i, b)
                    dve.wait_ge(ev("tile_used"), used((nb + 1) * g.tiles + g.first))
                    for t in range(TT):
                        last = nc.vector.tensor_tensor(yacc[:, t, span(col, wd)], PS[:, 4 * g.turned + 2 * bank + t, 0:wd],
                                                       yacc[:, t, span(col, wd)], ALU.add)
                    last.then_inc(ev("acc_free"), 1)
                tok_order(dve, name, tile, take if add else None, before, False)

            def feat(name, conv, before=None):
                g = G[name]
                gT = gT1 if conv else gT2

                def tiles(i, js):
                    for j in js:
                        dve.wait_ge(ev("hi_done"), i * FT + (g.first + j + 1))
                        nc.vector.tensor_tensor(wlo[:, j % SPLITS, :], stage[:, j, :], whi[:, j % SPLITS, :].bitcast(F32),
                                                ALU.subtract).then_inc(ev("lo_done"), 1)

                def join(i, s):
                    dve.wait_ge(ev("low_out"), i + (g.acc + 1))
                    to = pre[:, :, 2:2 + S] if conv else lowsum
                    nc.vector.tensor_tensor(to, PS[:, 4 * (s ^ g.turned):4 * (s ^ g.turned) + 4, 0:S], lowsum, ALU.add).then_inc(ev("pre_done"), 1)

                def taps(i):
                    for tap, name_ in ((1, "tap_mid"), (0, "conv_done")):
                        if tap:
                            dve.wait_ge(ev("tap"), i * 4 + 4 * (g.acc + 1))
                        else:
                            dve.wait_ge(ev("tap_mid"), i + (g.acc + 1))
                        for a in range(4):
                            f = i * 2 + (2 * (g.acc if name == "up1b" else 0) + a % 2 + F1 // P * (a // 2))
                            last = nc.vector.scalar_tensor_tensor(post[:, a, :], pre[:, a, tap:tap + S],
                                                                  convT[:, tap, span(f, 1)], post[:, a, :],
                                                                  ALU.mult, ALU.add)
                        last.then_inc(ev(name_), 1)

                def product(i):
                    if conv:
                        dve.wait_ge(ev("gelu"), i + (g.acc + 1))
                        nc.vector.tensor_tensor(post[:, 0:2, :], lowsum[:, 0:2, :], post[:, 2:4, :], ALU.mult)\
                            .then_inc(ev("prod"), 1)
                    else:
                        dve.wait_ge(ev("pre_done"), i + (g.acc + 3))
                        nc.vector.scalar_tensor_tensor(post[:, :, :], lowsum, 0.0, lowsum, ALU.max, ALU.mult)\
                            .then_inc(ev("prod"), 1)

                def low_parts(i):
                    k = 2 if conv else 4
                    dve.wait_ge(ev("g_hi"), i + (g.acc + 1))
                    nc.vector.tensor_tensor(gT[:, span(i * k, k), S:2 * S], post[:, 0:k, :],
                                            gT[:, span(i * k, k), 0:S].bitcast(F32), ALU.subtract).then_inc(ev("g_lo"), 1)

                def one(i, s, prev):
                    tiles(i, (0, 1, 2, 3))
                    if prev is None and before is not None:
                        before()
                    if prev is not None:
                        join(prev, 1 - s)
                        if conv:
                            taps(prev)
                    tiles(i, (4, 5))
                    if prev is not None:
                        product(prev)
                        low_parts(prev)
                    tiles(i, (6, 7))
                one(0, 0, None)
                one(1, 1, 0)
                with dve.Fori(1, g.blocks // 2) as r:
                    one(r * 2, 0, r * 2 - 1)
                    one(r * 2 + 1, 1, r * 2)

                def tail():
                    join(g.blocks - 1, 1)
                    if conv:
                        taps(g.blocks - 1)
                    product(g.blocks - 1)
                    low_parts(g.blocks - 1)
                return tail

            def mean_square(k, src, dst, count, ready, n):
                dve.wait_ge(ev(ready), n)
                nc.vector.tensor_scalar(dst, src, 1.0 / count, EPS, ALU.mult, ALU.add).then_inc(ev("var"), 1)

            def normed_x(k, n):
                mean_square(k, small[:, 0:2], small[:, 2:4], D, "ssq", k)
                dve.wait_ge(ev("rstd"), n)
                for t in range(TT):
                    nc.vector.tensor_scalar(yacc[:, t, :], x[:, t, :], small[:, 4 + t:5 + t], None, ALU.mult)\
                        .then_inc(ev("normed"), 1)

            def split_turned(turn):
                for c in range(KC):
                    dve.wait_ge(ev("acthi_" + turn), c // 2 * 2 + 2)
                    nc.vector.scalar_tensor_tensor(actT[:, c, S:2 * S], PS[:, c // 2, (c % 2) * S:(c % 2 + 1) * S],
                                                   gain_of(turn, c), actT[:, c, 0:S].bitcast(F32),
                                                   ALU.mult, ALU.subtract).then_inc(ev("actlo_" + turn), 1)

            def residual(k, n, gain):
                mean_square(k, small[:, 0:2], small[:, 2:4], D, "ssq", k)
                dve.wait_ge(ev("grow_in"), 16 * gain)
                dve.wait_ge(ev("rstd"), n)
                for t in range(TT):
                    then(dve, "dve", nc.vector.scalar_tensor_tensor(yacc[:, t, :], yacc[:, t, :], small[:, 4 + t:5 + t],
                                                                    grow[:, :], ALU.mult, ALU.mult))
                    nc.vector.tensor_tensor(x[:, t, :], x[:, t, :], yacc[:, t, :], ALU.add).then_inc(ev("resid"), 1)

            def me(ins):
                then(dve, "dve", ins)

            dve.sem_inc(ev("lo_done"), STAGES)
            dve.sem_inc(ev("acc_free"), 2)
            dve.sem_inc(ev("pre_done"), 2)
            dve.sem_inc(ev("g_lo"), 1)
            dve.wait_ge(ev("urow_mm"), 1)
            nc.vector.memset(urow[:, S:SK], NEG).then_inc(ev("urow"), 1)
            nc.vector.tensor_copy(urow[:, 0:S], PS[0:16, 5, 0:S]).then_inc(ev("urow"), 1)
            dve.wait_ge(ev("vecs_mm"), 1)
            me(nc.vector.tensor_copy(cols[:, 0:74], PS[:, 7, 0:74]))
            me(nc.vector.tensor_scalar(cols[:, 72:73], cols[:, 72:73], 1.0 - LAM_INIT, None, ALU.mult))
            me(nc.vector.memset(cols[:, 74:75], 1.0))
            me(nc.vector.tensor_copy(cols[:, C_LB:C_LB + 16], PS[:, 7, 74:90]))
            nc.vector.tensor_copy(convT[:, :, :], PS[:, 6, :].rearrange("p (j f) -> p j f", j=4)[:, :, 0:88])
            nc.vector.tensor_copy(posT[:, :, :], PS[:, 7, 128:192].rearrange("p (v l) -> p v l", v=2)).then_inc(ev("cols"), 1)
            dve.wait_ge(ev("lam_in"), 64)
            me(nc.vector.tensor_tensor(lamv[:, 0:2, :], lamv[:, 0:2, :], lamv[:, 2:4, :], ALU.mult))
            me(nc.vector.tensor_tensor(lbs[:, 32:40], cols[:, C_LB:C_LB + 8], cols[:, C_LB + 8:C_LB + 16], ALU.max))
            nc.vector.tensor_tensor(lbs[:, 0:8], cols[:, C_LB:C_LB + 8], lbs[:, 32:40], ALU.subtract)
            nc.vector.tensor_tensor(lbs[:, 8:16], cols[:, C_LB + 8:C_LB + 16], lbs[:, 32:40], ALU.subtract)
            nc.vector.tensor_reduce(small[:, 8:10], lamv[:, 0:2, :], AX.X, ALU.add).then_inc(ev("lam_dot"), 1)
            mean_square(1, small[:, 0:2], small[:, 2:4], D, "ssq", 1)
            for n in range(8):
                dve.wait_ge(ev("bias_mm"), n + 1)
                rows = PS[:, n, :].rearrange("p (h j) -> p h j", h=2)
                nc.vector.tensor_copy(bias[:, 2 * n:2 * n + 2, P:SK], rows)
                nc.vector.tensor_copy(bias[:, 2 * n:2 * n + 2, 0:P], rows[:, :, P:2 * P]).then_inc(ev("bias_done"), 1)
            dve.wait_ge(ev("rstd"), 1)
            for t in range(TT):
                nc.vector.tensor_scalar(yacc[:, t, :], x[:, t, :], small[:, 4 + t:5 + t], None, ALU.mult)\
                    .then_inc(ev("normed"), 1)
            split_turned("n1")
            dve.wait_ge(ev("early_exp"), 1)
            me(nc.vector.tensor_tensor(small[:, 12:13], small[:, 11:12], small[:, 10:11], ALU.subtract))
            me(nc.vector.tensor_scalar(small[:, 12:13], small[:, 12:13], LAM_INIT, None, ALU.subtract))
            me(nc.vector.tensor_tensor(lbs[:, 32:40], lbs[:, 16:24], lbs[:, 24:32], ALU.add))
            me(nc.vector.reciprocal(lbs[:, 32:40], lbs[:, 32:40]))
            me(nc.vector.tensor_tensor(lbs[:, 32:40], lbs[:, 16:24], lbs[:, 32:40], ALU.mult))
            me(nc.vector.tensor_scalar(lbs[:, 40:48], lbs[:, 32:40], -1.0, 1.0, ALU.mult, ALU.add))
            tok("in1", False)
            for m in range(1, 16, 2):
                n = TURN1[m]
                dve.wait_ge(ev("qt_mm"), m + 1)
                root = 64 ** -0.5 if n < 4 else P ** -0.5 if 8 <= n < 12 else 1.0
                nc.vector.tensor_scalar(QT[:, 2 * n:2 * n + 2, :].rearrange("p c s -> p (c s)"), PS[:, m % 8, :], root, None,
                                        ALU.mult).then_inc(ev("qt_d"), 1)
            flat_h = cst.rearrange("p a h t -> p a (h t)")
            flat_p = pcs.rearrange("p h t c -> p (h t) c")

            def wide(k):
                return flat_h[:, k, :].rearrange("p (n o) -> p n o", o=1).broadcast_to((P, HN * TT, NC))

            def masked(src, k, op):
                for t in range(TT):
                    mask = keepc[:, k, t, :].rearrange("p (o c) -> p o c", o=1).broadcast_to((P, HN, NC))
                    last = nc.vector.tensor_tensor(pcs[:, :, t, :], src[:, :, t, :], mask, op)
                me(last)

            def compressed(s):
                if s == 9:
                    dve.wait_ge(ev("kc_mm"), 1)
                    nc.vector.tensor_copy(kcT, PS[:, 7, 0:2 * NC])
                    nc.vector.tensor_copy(vc, PS[0:NC, 7, 2 * P:4 * P].rearrange("p (g d) -> p g d", g=NKV)).then_inc(ev("kc_out"), 1)

            def compressed_scores(s):
                if s == 9:
                    dve.wait_ge(ev("keep_in"), 32)
                    dve.wait_ge(ev("cmp_mm"), 1)
                    masked(PS[:, 7, 0:256].rearrange("p (h t c) -> p h t c", h=HN, t=TT)[:, :, :, 0:NC], 0, ALU.mult)
                    masked(pcs, 1, ALU.add)
                    me(nc.vector.tensor_reduce(flat_h[:, 0, :], flat_p, AX.X, ALU.max))
                    nc.vector.tensor_tensor(flat_p, flat_p, wide(0), ALU.subtract).then_inc(ev("cmp_shift"), 1)

            def compressed_probs(s):
                if s == 10:
                    dve.wait_ge(ev("cmp_exp"), 1)
                    dve.wait_ge(ev("gates_done"), 1)
                    masked(pcs, 0, ALU.mult)
                    me(nc.vector.tensor_reduce(flat_h[:, 1, :], flat_p, AX.X, ALU.add))
                    me(nc.vector.tensor_scalar(flat_h[:, 1, :], flat_h[:, 1, :], TINY, None, ALU.max))
                    me(nc.vector.reciprocal(flat_h[:, 1, :], flat_h[:, 1, :]))
                    gate0 = gates[:, :, :].rearrange("p t (h b) -> p h t b", b=3)[:, :, :, 0]
                    me(nc.vector.tensor_tensor(cst[:, 2, :, :], cst[:, 1, :, :], gate0, ALU.mult))
                    nc.vector.tensor_tensor(flat_p, flat_p, wide(2), ALU.mult).then_inc(ev("cmp_probs"), 1)

            def front(s):
                dve.wait_ge(ev("log_mm1"), s + 1)
                if s >= 2:
                    dve.wait_ge(ev("pt_mm1"), s - 1)
                head = s if s < HD else HD + (s - HD) // 2
                maps = 2 if s < HD else 1
                b = bias[:, head:head + 1, :].broadcast_to((P, maps, SK))
                me(nc.vector.tensor_tensor(scores[:, s % 2, 0:maps, :], PS[:, 2 * (s % 2):2 * (s % 2) + maps, 0:SK], b, ALU.add))
                nm = stat[:, s % 2, 0:4].rearrange("p (m q) -> p m q", q=2)
                nc.vector.tensor_reduce(nm[:, 0:maps, 0], scores[:, s % 2, 0:maps, 0:P], AX.X, ALU.max, negate=True)
                nc.vector.tensor_reduce(nm[:, 0:maps, 1], scores[:, s % 2, 0:maps, P:SK], AX.X, ALU.max, negate=True)\
                    .then_inc(ev("max1"), 1)

            def weigh(s):
                dve.wait_ge(ev("exp1"), s + 1)
                st = stat[:, s % 2, :]
                k = 4 if s < HD else 2
                me(nc.vector.reciprocal(st[:, 8:8 + k], st[:, 4:4 + k]))
                if s < HD:
                    me(nc.vector.tensor_scalar(st[:, 10:12], st[:, 10:12], small[:, 12:13], None, ALU.mult))
                    if s >= 2:
                        dve.wait_ge(ev("pt_mm1"), s - 1)
                    for q, (lo, hi) in enumerate(((0, P), (P, SK))):
                        last = nc.vector.tensor_scalar(probs[:, s % 2, lo:hi], scores[:, s % 2, 0, lo:hi], st[:, 8 + q:9 + q],
                                                       None, ALU.mult)
                    me(last)
                    for q, (lo, hi) in enumerate(((0, P), (P, SK))):
                        last = nc.vector.scalar_tensor_tensor(probs[:, s % 2, lo:hi], scores[:, s % 2, 1, lo:hi],
                                                              st[:, 10 + q:11 + q], probs[:, s % 2, lo:hi],
                                                              ALU.mult, ALU.add)
                    last.then_inc(ev("probs1"), 1)
                else:
                    r = s - HD
                    g = gates[:, :, :].rearrange("p t (h b) -> p h t b", b=3)[:, r // 2, :, 1 + r % 2]
                    nc.vector.tensor_tensor(weights[:, s % 4, :], st[:, 8:10], g, ALU.mult).then_inc(ev("probs1"), 1)

            def take_out(s):
                dve.wait_ge(ev("pv_mm1"), s + 1)
                o = PS[:, bank_of(5, s), 0:3 * P].rearrange("p (t d) -> p t d", t=3)
                if s < HD:
                    nc.vector.tensor_copy(proj[:, :, C_DQ + s * P:C_DQ + (s + 1) * P], o[:, 0:TT, :]).then_inc(ev("o_out1"), 1)
                    return
                h, mine = (s - HD) // 2, (s - HD) % 2
                at = [proj[:, t, C_NQ + h * P:C_NQ + (h + 1) * P] for t in range(TT)]
                wt = weights[:, s % 4, :]
                ln["dve"] += 1
                if mine == 0:
                    nc.vector.tensor_copy(at[0], o[:, 2, :]).then_inc(ev("self_dve"), 1)
                    nc.vector.tensor_scalar(at[1], o[:, 1, :], wt[:, 1:2], None, ALU.mult)
                else:
                    nc.vector.tensor_tensor(at[1], o[:, 2, :], at[1], ALU.add).then_inc(ev("self_dve"), 1)
                    nc.vector.scalar_tensor_tensor(at[0], o[:, 0, :], wt[:, 0:1], at[0], ALU.mult, ALU.add)
                dve.wait_ge(ev("self_dve"), ln["dve"])
                nc.vector.scalar_tensor_tensor(at[mine], o[:, mine, :], wt[:, mine:mine + 1], at[mine], ALU.mult, ALU.add)\
                    .then_inc(ev("o_out1"), 1)
                dve.wait_ge(ev("o_out1"), s + 1)
            weights = small[:, 16:24].rearrange("p (s t) -> p s t", s=4)
            for s in range(NBR + 3):
                compressed(s)
                compressed_probs(s)
                if s < NBR:
                    front(s)
                if 1 <= s <= NBR:
                    weigh(s - 1)
                if s >= 3:
                    take_out(s - 3)
                compressed_scores(s)
            mean_square(0, hstat[:, 0, :], hstat[:, 1, :], P, "hssq", 1)
            dve.wait_ge(ev("rstd"), 2)
            r = hstat[:, 2, :].rearrange("p (h t o) -> p h t o", t=TT, o=1)
            for t in range(TT):
                o = proj[:, t, C_DQ:C_DQ + HD * P].rearrange("p (h d) -> p h d", h=HD)
                nc.vector.tensor_tensor(o, o, r[:, :, t, :].broadcast_to((P, HD, P)), ALU.mult).then_inc(ev("mixed1"), 1)
            split_turned("mix1")
            tok("out1", False)
            residual(2, 3, 1)
            me(nc.vector.memset(pre[:, :, 0:2], 0.0))
            normed_x(3, 4)
            split_turned("n2")
            last_up = feat("up1a", True)
            tok("down1a", False, before=last_up)
            last_up = feat("up1b", True)
            dve.wait_ge(ev("acc_free"), 2 + G["down1b"].acc)
            tok("down1b", True, before=last_up)
            residual(4, 5, 2)
            normed_x(5, 6)
            split_turned("n3")
            tok("in2", False)
            dve.wait_ge(ev("acc_free"), 2 + G["in2"].acc + G["in2"].blocks)
            for v in range(NKV):
                src = proj2[:, :, C_KA + v * 64:C_KA + (v + 1) * 64]
                for u in range(2):
                    last = nc.vector.tensor_copy(kdup[:, :, v, u, :], src)
            last.then_inc(ev("kdup"), 1)
            for m, n in enumerate(TURN2):
                if m % 2:
                    dve.wait_ge(ev("qt2_mm"), m + 1)
                    nc.vector.tensor_scalar(QT2[:, 2 * n:2 * n + 2, :].rearrange("p c s -> p (c s)"), PS[:, m % 8, :],
                                            64 ** -0.5 if n < 4 else 1.0, None, ALU.mult).then_inc(ev("qt2_d"), 1)
            dve.wait_ge(ev("sig"), 1)
            me(nc.vector.tensor_tensor(QT2[:, 16:24, :], QT2[:, 16:24, :], sig_q, ALU.mult))
            dve.wait_ge(ev("sig"), 2)
            for h in range(HR):
                f = QT2[:, 24 + h, :]
                nc.vector.tensor_scalar(f, f, lbs[:, 40 + h:41 + h], lbs[:, 32 + h:33 + h], ALU.mult, ALU.add)
            dve.wait_ge(ev("sig"), 3)
            gr = proj2[:, :, C_GR:C_GR + 1024]
            nc.vector.tensor_tensor(gr, gr, sig_g, ALU.mult).then_inc(ev("f_done"), 1)
            dve.wait_ge(ev("ln_done"), 1)
            nc.vector.tensor_scalar(QT2[:, 24:32, :], QT2[:, 24:32, :], -1.0, 1.0, ALU.mult, ALU.add).then_inc(ev("key_done"), 1)
            dve.wait_ge(ev("mix2_in"), 64)
            me(nc.vector.tensor_scalar(sinks[:, 1, :], sinks[:, 0, :], -1.0, None, ALU.mult))

            def front2(s):
                dve.wait_ge(ev("log_mm2"), s + 1)
                if s >= 2:
                    dve.wait_ge(ev("pt_mm2"), s - 1)
                slope = -(2.0 ** (-8.0 * (s + 1) / HA))
                me(nc.vector.scalar_tensor_tensor(scores2[:, s % 2, :], far[:, :], slope, PS[:, s % 2, 0:SK], ALU.mult, ALU.add))
                st = stat[:, s % 2, :]
                nc.vector.tensor_reduce(st[:, 0:1], scores2[:, s % 2, 0:P], AX.X, ALU.max, negate=True)
                me(nc.vector.tensor_reduce(st[:, 1:2], scores2[:, s % 2, P:SK], AX.X, ALU.max, negate=True))
                nc.vector.tensor_scalar(st[:, 0:2], st[:, 0:2], sinks[:, 1, s:s + 1], None, ALU.min).then_inc(ev("max2"), 1)

            def weigh2(s):
                dve.wait_ge(ev("exp2"), s + 1)
                st = stat[:, s % 2, :]
                me(nc.vector.tensor_tensor(st[:, 4:6], st[:, 4:6], st[:, 6:8], ALU.add))
                me(nc.vector.reciprocal(wsum[:, s % 4, :], st[:, 4:6]))

            def take_out2(s):
                dve.wait_ge(ev("pv_mm2"), s + 1)
                for t in range(TT):
                    last = nc.vector.tensor_scalar(proj2[:, t, C_QA + s * 64:C_QA + (s + 1) * 64],
                                                   PS[:, 6 + s % 2, t * 64:(t + 1) * 64], wsum[:, s % 4, t:t + 1], None, ALU.mult)
                last.then_inc(ev("o_out2"), 1)
            wsum = lbs[:, 0:8].rearrange("p (s t) -> p s t", s=4)
            for s in range(HA + 3):
                if s < HA:
                    front2(s)
                if 1 <= s <= HA:
                    weigh2(s - 1)
                if s >= 3:
                    take_out2(s - 3)
            NR = HR * TT
            for n in range(NR + 1):
                if n < NR:
                    h, t = n // TT, n % TT
                    dve.wait_ge(ev("fac"), n + 1)
                    if n >= 1:
                        dve.wait_ge(ev("att_mm"), n)
                    q = QT2[:, 16 + h, t * P:(t + 1) * P].rearrange("p (o t) -> p o t", o=1).broadcast_to((P, 8, P))
                    nc.vector.tensor_tensor(qf, fac, q, ALU.mult).then_inc(ev("qf"), 1)
                if n >= 1:
                    dve.wait_ge(ev("att_mm"), n)
                    me(nc.vector.tensor_tensor(attm, PS[:, 2:4, :].rearrange("p a (l t) -> p (a l) t", t=P), keep[:, :, :], ALU.mult))
                    if n >= 2:
                        dve.wait_ge(ev("o_mm"), n - 1)
                    nc.vector.tensor_reduce(attT[:, :], attm.rearrange("p l t -> p t l"), AX.X, ALU.add).then_inc(ev("att_out"), 1)
            mean_square(0, small[:, 0:2], small[:, 2:4], 1024, "ssq", 6)
            dve.wait_ge(ev("o_out"), NR)
            mean_square(0, hstat[:, 0, :], hstat[:, 1, :], P, "o_out", NR)
            dve.wait_ge(ev("rstd"), 7)
            for t in range(TT):
                o = proj2[:, t, C_QA:C_QA + 1024]
                nc.vector.tensor_scalar(o, o, small[:, 4 + t:5 + t], None, ALU.mult).then_inc(ev("mixed2"), 1)
            dve.wait_ge(ev("rstd"), 8)
            r = hstat[:, 2, :].rearrange("p (h t o) -> p h t o", t=TT, o=1)
            for t in range(TT):
                g = proj2[:, t, C_GR:C_GR + 1024].rearrange("p (h d) -> p h d", h=HR)
                me(nc.vector.tensor_tensor(g, g, r[:, :, t, :].broadcast_to((P, HR, P)), ALU.mult))
                nc.vector.tensor_tensor(proj2[:, t, C_IR:C_IR + 1024], proj2[:, t, C_FR:C_FR + 1024],
                                        proj2[:, t, C_GR:C_GR + 1024], ALU.mult).then_inc(ev("mixed2"), 1)
            split_turned("mix2")
            tok("out2", False)
            residual(7, 9, 3)
            normed_x(8, 10)
            split_turned("n4")
            last_up = feat("up2a", False)
            tok("down2a", False, before=last_up)
            last_up = feat("up2b", False)
            dve.wait_ge(ev("acc_free"), 2 + G["down2b"].acc)
            tok("down2b", True, before=last_up)
            residual(9, 11, 4)

        @block.tensor
        def _(pe):
            def tok(name, lhs, up=None):
                g, pairs = G[name], PAIRS[name]
                T = g.tiles

                def one(i, b, base):
                    _, nb, bank, wd = place(name, i, b)
                    pe.wait_ge(ev("acc_free"), nb + (g.acc + 1))
                    for j in range(T):
                        if up is not None and b == 0 and j == T - (2 if up.startswith("up2") else 1):
                            pe.wait_ge(ev("g_lo"), 1 + G[up].acc + G[up].blocks)
                        s = (b * T + j) % SPLITS
                        pe.wait_ge(ev("lo_done"), base + (j + 1 + STAGES))
                        for c in range(TC):
                            k = TC * j + c
                            h, l = whi[:, s, c * wd:(c + 1) * wd], wlo[:, s, c * wd:(c + 1) * wd]
                            for t in range(TT):
                                o = PS[:, 4 * g.turned + 2 * bank + t, 0:wd]
                                ah, al = lhs[:, k, t * P:(t + 1) * P], lhs[:, k, S + t * P:S + (t + 1) * P]
                                nc.tensor.matmul(o, ah, h, start=k == 0, stop=False)
                                nc.tensor.matmul(o, ah, l, start=False, stop=False)
                                last = nc.tensor.matmul(o, al, h, start=False, stop=k == TC * T - 1)
                        last.then_inc(ev("tile_used"), 1)
                if up is not None:
                    pe.wait_ge(ev("pre_done"), 1 + G[up].acc + G[up].blocks)
                    pe.wait_ge(ev("g_lo"), G[up].acc + G[up].blocks)
                if pairs:
                    with pe.Fori(0, pairs) as i:
                        for b in range(2):
                            one(i, b, i * (2 * T) + (g.first + b * T))
                for b in range(2 * pairs, g.blocks):
                    one(None, b, g.first + b * T)

            def feat(name, down=None):
                g = G[name]
                with pe.Fori(0, g.blocks // 2) as r:
                    for s in range(2):
                        i = r * 2 + s
                        pe.wait_ge(ev("pre_done"), i + (g.acc + 1))
                        if s == 1 and down is not None:
                            pe.wait_ge(ev("acc_free"), 2 + G[down].acc + G[down].blocks)
                        for j in range(FT):
                            pe.wait_ge(ev("lo_done"), i * FT + (g.first + j + 1 + STAGES))
                            for c in range(FC):
                                k = j % (FT // 2) * FC + c
                                for f in range(2):
                                    o = PS[:, 4 * (s ^ g.turned) + 2 * (j // (FT // 2)) + f, :]
                                    at = slice(c * FW + f * P, c * FW + (f + 1) * P)
                                    nc.tensor.matmul(o, whi[:, j % SPLITS, at], actT[:, k, :], start=k == 0, stop=False)
                                    last = nc.tensor.matmul(o[:, S:2 * S], wlo[:, j % SPLITS, at], actT[:, k, 0:S],
                                                            start=False, stop=k == KC - 1)
                            last.then_inc(ev("tile_used"), 1)

            def turn(name, ready, n):
                pe.wait_ge(ev(ready), n)
                for c in range(KC):
                    for t in range(TT):
                        at = (c % 2) * S + t * P
                        last = nc.tensor.transpose(PS[:, c // 2, at:at + P], src_of(name, t, c), ident[:, :])
                    if c % 2:
                        last.then_inc(ev("turned_" + name), 1)

            def acts(name):
                pe.wait_ge(ev("actlo_" + name), KC)

            pe.sem_inc(ev("tile_used"), SPLITS)
            pe.wait_ge(ev("tab_in"), 32)
            nc.tensor.matmul(PS[0:16, 5, 0:SK], tab, hot, start=True, stop=True).then_inc(ev("urow_mm"), 1)
            pe.wait_ge(ev("ident_in"), 32)
            pe.wait_ge(ev("vecs_in"), 16 * 14)
            nc.tensor.transpose(PS[:, 7, 0:90], vecs[0:90, 0, :], ident[0:90, 0:90])
            nc.tensor.transpose(PS[:, 7, 128:192], vecs[0:64, 1, :], ident[0:64, 0:64])
            for j in range(4):
                last = nc.tensor.transpose(PS[:, 6, j * P:j * P + 88], vecs[0:88, 2 + j, :], ident[0:88, 0:88])
            last.then_inc(ev("vecs_mm"), 1)
            pe.wait_ge(ev("hankel_in"), 16)
            pe.wait_ge(ev("urow"), 2)
            pe.wait_ge(ev("cols"), 1)
            pe.wait_ge(ev("ssq"), 1)
            for n in range(8):
                nc.tensor.matmul(PS[:, n, :], flip, hankel[:, 2 * n:2 * n + 2, :].rearrange("p h j -> p (h j)"),
                                 start=True, stop=True).then_inc(ev("bias_mm"), 1)
            pe.wait_ge(ev("bias_done"), 8)
            turn("n1", "normed", 2)
            acts("n1")
            tok("in1", actT)
            pe.wait_ge(ev("acc_free"), 2 + G["in1"].blocks)
            COLS = ([C_DQ + c * P for c in range(8)] + [C_DK + c * P for c in range(8)] + [C_NQ + c * P for c in range(8)]
                    + [c0 + g * P for c0 in (C_KC, C_VC, C_KS, C_KW) for g in range(NKV)])
            for m, n in enumerate(TURN1):
                if m >= 8:
                    pe.wait_ge(ev("qt_d" if m % 2 else "qt_a"), (m - 8) // 2 + 1)
                for c in range(2):
                    for t in range(TT):
                        at = COLS[2 * n + c]
                        last = nc.tensor.transpose(PS[:, m % 8, c * S + t * P:c * S + (t + 1) * P],
                                                   proj[:, t, at:at + P], ident[:, :])
                last.then_inc(ev("qt_mm"), 1)
            pe.wait_ge(ev("qt_a"), 8)
            pe.wait_ge(ev("qt_d"), 8)

            def compress(s):
                g = G["cmp"]
                if 1 <= s <= g.tiles // 2:
                    pe.wait_ge(ev("tile_used"), used(g.first + 2 * s))
                    pe.sem_inc(ev("lo_done"), 2)
                if s < g.tiles // 2:
                    v = s // 4
                    pe.wait_ge(ev("blocks_done"), 4 * (v + 1))
                    if v:
                        pe.wait_ge(ev("hid_done"), 1)
                    for j in (2 * s, 2 * s + 1):
                        pe.wait_ge(ev(f"landed{j % STAGES}"), 16 * ((g.first + j) // STAGES + 1))
                        for l in range(FC):
                            k = FC * (j % STAGES) + l
                            for a in range(2):
                                at = stage[:, j % STAGES, l * HID + a * P:l * HID + (a + 1) * P]
                                last = nc.tensor.matmul(PS[:, 6 + a, 0:2 * NC], at,
                                                        blocks[:, v, k, :, :].rearrange("p g c -> p (g c)"),
                                                        start=k == 0, stop=k == CMP_LEN - 1)
                        last.then_inc(ev("tile_used"), 1)
                if s == 8:
                    pe.wait_ge(ev("w2_in"), 32)
                    pe.wait_ge(ev("hid_done"), 2)
                    for a in range(2):
                        nc.tensor.matmul(PS[:, 7, 0:2 * NC], w2[:, 0, a, :], hid[:, 0, a, :], start=a == 0, stop=a == 1)
                    for g in range(NKV):
                        for a in range(2):
                            last = nc.tensor.matmul(PS[0:NC, 7, (2 + g) * P:(3 + g) * P], hid[:, 1, a, g * NC:(g + 1) * NC],
                                                    w2[:, 1, a, :], start=a == 0, stop=a == 1)
                    last.then_inc(ev("kc_mm"), 1)
                if s == 9:
                    pe.wait_ge(ev("kc_out"), 1)
                    for n in range(HN * TT):
                        h, t = n // TT, n % TT
                        g = h // (HN // NKV)
                        last = nc.tensor.matmul(PS[:, 7, n * 16:n * 16 + NC], QT[:, 16 + h, t * P:(t + 1) * P],
                                                kcT[:, g * NC:(g + 1) * NC], start=True, stop=True)
                    last.then_inc(ev("cmp_mm"), 1)
                if s == 10:
                    pe.wait_ge(ev("cmp_probs"), 1)

            def branch(s):
                if s < HD:
                    return [(QT[64 * m:64 * m + 64, s, :], QT[64 * m:64 * m + 64, 8 + s, :]) for m in range(2)], C_DV + s * P
                h, kind = (s - HD) // 2, (s - HD) % 2
                g = h // (HN // NKV)
                return [(QT[:, 16 + h, :], QT[:, 28 + 2 * kind + g, :])], (C_VS, C_VW)[kind] + g * P

            for s in range(NBR + 3):
                if s < NBR:
                    if s >= 2:
                        pe.wait_ge(ev("max1"), s - 1)
                    for m, (q, k) in enumerate(branch(s)[0]):
                        nc.tensor.matmul(PS[:, 2 * (s % 2) + m, 0:P], q[:, 0:P], k[:, 0:P], start=True, stop=True)
                        last = nc.tensor.matmul(PS[:, 2 * (s % 2) + m, P:SK], q[:, P:S], k[:, 0:S], start=True, stop=True)
                    last.then_inc(ev("log_mm1"), 1)
                compress(s)
                if 2 <= s < NBR + 2:
                    r = s - 2
                    pe.wait_ge(ev("probs1"), r + 1)
                    if r >= 1:
                        pe.wait_ge(ev("pt_out1"), r if r <= HD else r - 1)
                    src = probs[:, r % 2, :] if r < HD else scores[:, r % 2, 0, :]
                    for b in range(3):
                        last = nc.tensor.transpose(PS[:, bank_of(4, r), b * P:(b + 1) * P], src[:, b * P:(b + 1) * P], ident[:, :])
                    if r >= HD:
                        last = nc.tensor.transpose(PS[0:NC, bank_of(4, r), SK:SK + P], pcs[:, (r - HD) // 2, (r - HD) % 2, :], ident[:, :])
                    last.then_inc(ev("pt_mm1"), 1)
                if s >= 3:
                    r = s - 3
                    pe.wait_ge(ev("pt_out1"), r + 1)
                    if r >= 1:
                        pe.wait_ge(ev("o_out1"), r if r <= HD else r - 1)
                    v = branch(r)[1]
                    pt, o = probsT[:, r % 2, :], PS[:, bank_of(5, r), :]
                    if r >= HD:
                        nc.tensor.matmul(o[:, 2 * P:3 * P], pcT[:, r % 2, :], vc[:, (r - HD) // HN, :], start=True, stop=True)
                    nc.tensor.matmul(o[:, 0:P], pt[:, 0:P], proj[:, 0, v:v + P], start=True, stop=True)
                    nc.tensor.matmul(o[:, P:2 * P], pt[:, P:2 * P], proj[:, 0, v:v + P], start=True, stop=False)
                    nc.tensor.matmul(o[:, P:2 * P], pt[:, 2 * P:3 * P], proj[:, 1, v:v + P], start=False, stop=True)\
                        .then_inc(ev("pv_mm1"), 1)
            pe.wait_ge(ev("o_out1"), NBR)
            turn("mix1", "mixed1", 2)
            acts("mix1")
            tok("out1", actT)
            turn("n2", "normed", 4)
            acts("n2")
            feat("up1a")
            tok("down1a", gT1, "up1a")
            feat("up1b", "down1a")
            tok("down1b", gT1, "up1b")
            turn("n3", "normed", 6)
            acts("n3")
            tok("in2", actT)
            pe.wait_ge(ev("acc_free"), 2 + G["in2"].acc + G["in2"].blocks)
            pe.wait_ge(ev("kdup"), 1)
            for m, n in enumerate(TURN2):
                if m >= 8:
                    pe.wait_ge(ev("qt2_d" if m % 2 else "qt2_a"), (m - 8) // 2 + 1)
                for c in range(2):
                    for t in range(TT):
                        if n == 4:
                            src = kdup[:, t, c, :, :].rearrange("p u d -> p (u d)")
                        else:
                            at = C_QA + (2 * n + c) * P if n < 4 else C_QR + (2 * n + c - 16) * P
                            src = proj2[:, t, at:at + P]
                        last = nc.tensor.transpose(PS[:, m % 8, c * S + t * P:c * S + (t + 1) * P], src, ident[:, :])
                last.then_inc(ev("qt2_mm"), 1)
            pe.wait_ge(ev("qt2_a"), 7)
            pe.wait_ge(ev("qt2_d"), 6)
            pe.wait_ge(ev("ln_done"), 1)
            pe.wait_ge(ev("f_done"), 1)
            for n in range(4):
                for k in range(4):
                    h, t = 4 * (n % 2) + k, n // 2
                    last = nc.tensor.transpose(PS[:, n, k * P:(k + 1) * P], lnf[:, h, t * P:(t + 1) * P], ident[:, :])
                last.then_inc(ev("logf_mm"), 1)
            pe.wait_ge(ev("logf_out"), 4)
            for s in range(HA + 3):
                if s < HA:
                    if s >= 2:
                        pe.wait_ge(ev("max2"), s - 1)
                    rows = slice(64 * (s % 2), 64 * (s % 2) + 64)
                    q, k = QT2[rows, s // 2, :], QT2[rows, 8 + s // (HA // NKV), :]
                    nc.tensor.matmul(PS[:, s % 2, 0:P], q[:, 0:P], k[:, 0:P], start=True, stop=True)
                    nc.tensor.matmul(PS[:, s % 2, P:SK], q[:, P:S], k[:, 0:S], start=True, stop=True).then_inc(ev("log_mm2"), 1)
                if 2 <= s < HA + 2:
                    r = s - 2
                    pe.wait_ge(ev("exp2"), r + 1)
                    if r >= 2:
                        pe.wait_ge(ev("pt_out2"), r - 1)
                    for b in range(3):
                        last = nc.tensor.transpose(PS[:, 2 + r % 2, b * P:(b + 1) * P], scores2[:, r % 2, b * P:(b + 1) * P], ident[:, :])
                    last.then_inc(ev("pt_mm2"), 1)
                if s >= 3:
                    r = s - 3
                    pe.wait_ge(ev("pt_out2"), r + 1)
                    if r >= 2:
                        pe.wait_ge(ev("o_out2"), r - 1)
                    v = C_VA + r // (HA // NKV) * 64
                    pt, o = probsT2[:, r % 2, :], PS[:, 6 + r % 2, :]
                    nc.tensor.matmul(o[:, 0:64], pt[:, 0:P], proj2[:, 0, v:v + 64], start=True, stop=True)
                    nc.tensor.matmul(o[:, 64:P], pt[:, P:2 * P], proj2[:, 0, v:v + 64], start=True, stop=False)
                    nc.tensor.matmul(o[:, 64:P], pt[:, 2 * P:3 * P], proj2[:, 1, v:v + 64], start=False, stop=True)\
                        .then_inc(ev("pv_mm2"), 1)
            NR = HR * TT
            pe.wait_ge(ev("key_done"), 1)
            for n in range(NR + 2):
                if n < NR:
                    h, t = n // TT, n % TT
                    if n >= 1:
                        pe.wait_ge(ev("fac"), n)
                    lf = logf[:, t, h, :]
                    nc.tensor.matmul(PS[:, 0, :], lf, sums[:, 0:4, :].rearrange("p l t -> p (l t)"), start=True, stop=True)
                    nc.tensor.matmul(PS[:, 1, 0:3 * P], lf, sums[:, 4:7, :].rearrange("p l t -> p (l t)"), start=True, stop=True)
                    nc.tensor.matmul(PS[:, 1, 3 * P:4 * P], lf, sums[:, 7 + t, :], start=True, stop=True).then_inc(ev("exps_mm"), 1)
                if 1 <= n <= NR:
                    r = n - 1
                    h, t = r // TT, r % TT
                    pe.wait_ge(ev("qf"), r + 1)
                    pe.wait_ge(ev("kf"), r + 1)
                    if r >= 1:
                        pe.wait_ge(ev("att_out"), r)
                    if t == 1:
                        pe.wait_ge(ev("kcross_done"), h + 1)
                        if h >= 1:
                            pe.wait_ge(ev("cross_out"), h)
                        nc.tensor.matmul(PS[:, 4, 0:P], kcross[:, :], qf[:, 7, :], start=True, stop=True).then_inc(ev("cross_mm"), 1)
                    for l in range(8):
                        lhs = kf[:, l, :] if l < 7 else QT2[:, 24 + h, t * P:(t + 1) * P]
                        rhs = qf[:, l, :] if l < 7 else QT2[:, 16 + h, t * P:(t + 1) * P]
                        last = nc.tensor.matmul(PS[:, 2 + l // 4, (l % 4) * P:(l % 4 + 1) * P], lhs, rhs, start=True, stop=True)
                    last.then_inc(ev("att_mm"), 1)
                if n >= 2:
                    r = n - 2
                    h, t = r // TT, r % TT
                    pe.wait_ge(ev("att_out"), r + 1)
                    if r >= 1:
                        pe.wait_ge(ev("o_out"), r)
                    v = C_IR + h * P
                    if t == 0:
                        nc.tensor.matmul(PS[:, 5, 0:P], attT[:, :], proj2[:, 0, v:v + P], start=True, stop=True).then_inc(ev("o_mm"), 1)
                    else:
                        nc.tensor.matmul(PS[:, 5, 0:P], attT[:, :], proj2[:, 1, v:v + P], start=True, stop=False)
                        pe.wait_ge(ev("cross_out"), h + 1)
                        nc.tensor.matmul(PS[:, 5, 0:P], crossT[:, :], proj2[:, 0, v:v + P], start=False, stop=True).then_inc(ev("o_mm"), 1)
            pe.wait_ge(ev("o_out"), NR)
            pe.wait_ge(ev("ssq"), 6)
            turn("mix2", "mixed2", 4)
            acts("mix2")
            tok("out2", actT)
            turn("n4", "normed", 8)
            acts("n4")
            feat("up2a")
            tok("down2a", gT2, "up2a")
            feat("up2b", "down2a")
            tok("down2b", gT2, "up2b")


_INS = ["x", "pre_mix_norm", "w_in", "lambda_q1", "lambda_k1", "lambda_q2", "lambda_k2", "diff_subln", "cmp_pos_k",
        "cmp_pos_v", "cmp_k_w1", "cmp_k_w2", "cmp_v_w1", "cmp_v_w2", "rel_bias", "w_out", "post_mix_norm",
        "pre_ffn_norm", "w_up", "conv_w", "conv_b", "w_down", "post_ffn_norm", "w_in_2", "attn_sinks_2",
        "attn_out_gain_2", "rnn_lb_logits_2", "rnn_norm_gain_2", "w_out_2", "mix_pre_gain_2", "mix_post_gain_2",
        "mlp_pre_gain_2", "mlp_post_gain_2", "w_up_2", "w_down_2"]


def kernel(**inputs):
    import concourse.bacc as bacc
    from concourse.bass_utils import run_bass_kernel_spmd

    nc = bacc.Bacc("TRN2", target_bir_lowering=False, num_devices=1)
    arrays, w = {}, {}
    for name in _INS:
        a = np.ascontiguousarray(inputs[name])
        arrays[f"in_{name}"] = a
        w[name] = nc.dram_tensor(f"in_{name}", a.shape, F32, kind="ExternalInput").ap()
    for name, a in shape_constants().items():
        arrays[f"const_{name}"] = a
        w[name] = nc.dram_tensor(f"const_{name}", a.shape, F32, kind="ExternalInput").ap()
    out = nc.dram_tensor("out", (1, S, D), F32, kind="ExternalOutput").ap()
    scratch = nc.dram_tensor("bias_by_distance", (16, SK), F32, kind="Internal").ap()
    build(nc, w, out, scratch)
    r = run_bass_kernel_spmd(nc, [arrays], core_ids=[0])
    return r.results[0]["out"]
```

```python
import math

import numpy as np

import concourse.bass as bass
from concourse import mybir
from contextlib import ExitStack

F32 = mybir.dt.float32
F32R = mybir.dt.float32r
ALU = mybir.AluOpType
ACT = mybir.ActivationFunctionType
AX = mybir.AxisListType

P = 128
D = 2048
S = 256
TT = S // P
KC = D // P
EPS = 1e-6
NEG = -1e30
TINY = 1e-30

HD = 8
HN = 8
NKV = 2
GATES = HN * 3
NB_BUCKETS = 32
CMP_LEN, CMP_STRIDE, HID = 32, 16, 256
NC = (S - CMP_LEN) // CMP_STRIDE + 1
LAM_INIT = 0.8 - 0.6 * math.exp(0.0)
C_DQ, C_DK, C_DV, C_NQ = 0, 1024, 2048, 3072
C_KC, C_VC, C_KS, C_VS, C_KW, C_VW, C_G = 4096, 4352, 4608, 4864, 5120, 5376, 5632
IN1 = C_G + GATES
F1 = 5632
F2 = 8192
HA, HR = 16, 8
C_QA, C_KA, C_VA, C_QR, C_FR, C_IR, C_GR = 0, 1024, 1152, 1280, 2304, 3328, 4352
IN2 = 5376
SK = 384
LEVELS = (64, 32, 16, 8, 4, 2, 1)

STAGES = 8
SPLITS = 4
AHEAD = 3
TILE = 1024
NW = 512
TC = TILE // NW
FW = 256
FC = TILE // FW
FT = 2 * KC // FC


class Gemm:

    def __init__(self, kind, first, blocks, tiles, acc=0, turned=0):
        self.kind, self.first, self.blocks, self.tiles, self.acc = kind, first, blocks, tiles, acc
        self.turned = turned


def plan():
    out, n, acc, up = {}, 0, 0, 0
    order = [("in1", "tok", 12, 8), ("cmp", "raw", 1, 16), ("out1", "tok", 4, 8),
             ("up1a", "feat", 12, FT), ("down1a", "tok", 4, 12), ("up1b", "feat", 10, FT), ("down1b", "tok", 4, 10),
             ("in2", "tok", 11, 8), ("out2", "tok", 4, 8),
             ("up2a", "feat", 8, FT), ("down2a", "tok", 4, 16), ("up2b", "feat", 8, FT), ("down2b", "tok", 4, 16)]
    for name, kind, blocks, tiles in order:
        out[name] = Gemm(kind, n, blocks, tiles, up if kind == "feat" else acc, int(name in ("up1b", "down1b", "up2b", "down2b")))
        assert n % STAGES == 0
        n += blocks * tiles
        if kind == "tok":
            acc += blocks
        if kind == "feat":
            up += blocks
    return out


def buckets(d):
    half = NB_BUCKETS // 2
    if d < half:
        return d
    return min(half + int(math.log(d / half) / math.log(128 / half) * half), NB_BUCKETS - 1)


def shape_constants():
    i = np.arange(P)
    c = {}
    c["ident"] = np.eye(P, dtype=np.float32)
    c["flip"] = np.eye(P, dtype=np.float32)[::-1].copy()
    onehot = np.zeros((NB_BUCKETS, SK), np.float32)
    for m in range(S):
        onehot[buckets(S - 1 - m), m] = 1.0
    c["onehot"] = onehot
    far = np.full((P, SK), 1e34, np.float32)
    for q in range(P):
        for lo, hi, off in ((0, 128, 0), (128, 256, 256), (256, 384, 256)):
            for col in range(lo, hi):
                d = off + q - col if lo != 0 else q - col
                if 0 <= d < P:
                    far[q, col] = d
    c["far"] = far
    ends = np.zeros((P, TT, NC), np.float32)
    for t in range(TT):
        for n in range(NC):
            ends[:, t, n] = (n * CMP_STRIDE + CMP_LEN - 1 <= t * P + i)
    c["cmp_keep"] = ends
    c["cmp_drop"] = ((1.0 - ends) * NEG).astype(np.float32)
    sums = np.zeros((P, 9, P), np.float32)
    keep = np.zeros((P, 8, P), np.float32)
    u, t = i[:, None], i[None, :]
    for n, ln in enumerate(LEVELS):
        mid = t // (2 * ln) * (2 * ln) + ln
        sums[:, n, :] = np.where(t >= mid, (u >= mid) & (u <= t), (u > t) & (u < mid))
        same = u // (2 * ln) == t // (2 * ln)
        keep[:, n, :] = same & (u % (2 * ln) < ln) & (t % (2 * ln) >= ln)
    sums[:, 7, :] = u > t
    sums[:, 8, :] = u <= t
    keep[:, 7, :] = u == t
    c["sums"] = sums
    c["keep"] = keep
    return c


def layout(a):
    return a


def build(nc, w, out, scratch):
    G = plan()
    ctx = ExitStack()
    sems = {}

    def ev(name):
        if name not in sems:
            sems[name] = ctx.enter_context(nc.semaphore(name))
        return sems[name]

    with ctx:
        def sb(name, shape, dt=F32, on=ctx):
            return on.enter_context(nc.sbuf_tensor(name, shape, dt))

        stage = sb("stage", [P, STAGES, TILE])
        whi = sb("whi", [P, SPLITS, TILE], F32R)
        wlo = sb("wlo", [P, SPLITS, TILE], F32R)
        x = sb("x", [P, TT, D])
        ident = sb("ident", [P, P])
        grow = sb("grow", [P, D])
        cols = sb("cols", [P, 96])
        posT = sb("posT", [P, 2, CMP_LEN])
        convT = sb("convT", [P, 4, 2 * F1 // P])
        small = sb("small", [P, 24])
        hstat = sb("hstat", [P, 3, 16])
        lbs = sb("lbs", [P, 48])
        half = sb("half", [P, 1])
        parts = sb("parts", [P, TT, 8])
        stat = sb("stat", [P, 2, 16])
        here = ExitStack()
        actT = sb("actT", [P, KC, 2 * S], F32R, here)
        here.close()
        mixer1 = ExitStack()
        QT = sb("QT", [P, 32, S], F32, mixer1)
        proj = sb("proj", [P, TT, IN1], F32, mixer1)
        bias = sb("bias", [P, 16, SK], F32, mixer1)
        work = sb("work", [P, 3072], F32, mixer1)
        gates = sb("gates", [P, TT, GATES], F32, mixer1)
        mixer1.close()
        scores = work[:, 0:4 * SK].rearrange("p (a m k) -> p a m k", a=2, m=2)
        probs = work[:, 4 * SK:6 * SK].rearrange("p (a k) -> p a k", a=2)
        probsT = work[:, 6 * SK:8 * SK].rearrange("p (a k) -> p a k", a=2)
        flat = proj[:, :, :].rearrange("p t n -> p (t n)")
        hankel = grow[:, :].rearrange("p (h j) -> p h j", h=8)
        vecs = flat[:, 8192:8192 + 6 * P].rearrange("p (r j) -> p r j", r=6)
        lamv = work[:, 0:256].rearrange("p (a c) -> p a c", a=4)
        tab = work[0:NB_BUCKETS, 512:528]
        hot = work[0:NB_BUCKETS, 1024:1024 + SK]
        flip = work[:, 1536:1664]
        urow = work[0:16, 2048:2048 + SK]
        blocks = grow[:, 0:2 * CMP_LEN * NKV * NC].rearrange("p (v l g c) -> p v l g c", v=2, l=CMP_LEN, g=NKV)
        w2 = proj[:, 0, C_KC:C_KC + 512].rearrange("p (v a n) -> p v a n", v=2, a=2)
        hid = proj[:, 1, C_KC:C_KC + 4 * 2 * NC].rearrange("p (v a c) -> p v a c", v=2, a=2)
        kcT = proj[:, 1, C_KC + 128:C_KC + 128 + 2 * NC]
        vc = proj[0:NC, 1, C_KC + 192:C_KC + 192 + NKV * P].rearrange("p (g d) -> p g d", g=NKV)
        pcs = proj[:, 0, C_DK:C_DK + HN * TT * NC].rearrange("p (h t c) -> p h t c", h=HN, t=TT)
        keepc = proj[:, 0, C_DK + 256:C_DK + 256 + 2 * TT * NC].rearrange("p (a t c) -> p a t c", a=2, t=TT)
        cst = proj[:, 0, C_DK + 384:C_DK + 384 + 3 * HN * TT].rearrange("p (a h t) -> p a h t", a=3, h=HN)
        pcT = probs[0:NC, :, 0:P]
        mixer2 = ExitStack()
        QT2 = sb("QT2", [P, 32, S], F32, mixer2)
        proj2 = sb("proj2", [P, TT, IN2], F32, mixer2)
        far = sb("far", [P, SK], F32, mixer2)
        scores2 = sb("scores2", [P, 2, SK], F32, mixer2)
        probsT2 = sb("probsT2", [P, 2, SK], F32, mixer2)
        sinks = sb("sinks", [P, 2, HA], F32, mixer2)
        sums = sb("sums", [P, 9, P], F32, mixer2)
        keep = sb("keep", [P, 8, P], F32, mixer2)
        logf = sb("logf", [P, TT, HR, P], F32, mixer2)
        fackf = sb("fackf", [P, 2, 8, P], F32, mixer2)
        kcross = sb("kcross", [P, P], F32, mixer2)
        attT = sb("attT", [P, 2, P], F32, mixer2)
        crossT = sb("crossT", [P, P], F32, mixer2)
        mixer2.close()
        kdup = QT2[:, 10:12, :].rearrange("p t (v u d) -> p t v u d", v=NKV, u=2)
        fac = fackf[:, 0, :, :]
        kf = fackf[:, 1, :, :]
        attm = proj2[:, 0, C_QR:C_QR + 1024].rearrange("p (l t) -> p l t", l=8)
        qf = proj2[:, 1, C_QR:C_QR + 1024].rearrange("p (l t) -> p l t", l=8)
        sig_q = logf[:, :, :, :].rearrange("p t h k -> p (t h k)").rearrange("p (h s) -> p h s", h=HR)
        lnf = fackf[:, :, :, :].rearrange("p a l t -> p (a l t)").rearrange("p (h s) -> p h s", h=HR)
        sig_g = fackf[:, :, :, :].rearrange("p a l t -> p a (l t)")
        ffn = ExitStack()
        sb("actT_place", [P, KC, 2 * S], F32R, ffn)
        yacc = sb("yacc", [P, TT, D], F32, ffn)
        both = ExitStack()
        gT1 = sb("gT1", [P, 24, 2 * S], F32R, both)
        pre = sb("pre", [P, 4, S + 2], F32, both)
        both.close()
        gT2 = sb("gT2", [P, 32, 2 * S], F32R, ffn)
        ffn.close()
        diag = yacc[:, 0, 0:TT * P].rearrange("p (t q) -> p t q", t=TT)
        lowsum = grow[:, 0:4 * S].rearrange("p (a s) -> p a s", a=4)
        post = grow[:, 4 * S:8 * S].rearrange("p (a s) -> p a s", a=4)

        PS = ctx.enter_context(nc.psum_tensor("PS", [P, 8, 512], F32))

        ln = {"dve": 0, "act": 0, "pool": 0}

        def then(eng, name, ins):
            ln[name] += 1
            ins.then_inc(ev("self_" + name), 1)
            eng.wait_ge(ev("self_" + name), ln[name])

        GAIN = {"n1": 0, "n2": 16, "n3": 32, "n4": 48, "attn": 64, "subln": 72, "rnn": 73, "one": 74}
        C_LB = 76

        def gain_of(turn, c):
            if turn == "mix1":
                at = GAIN["subln"] if c < HD else GAIN["one"]
            elif turn == "mix2":
                at = GAIN["attn"] + c if c < 8 else GAIN["rnn"]
            else:
                at = GAIN[turn] + c
            return cols[:, at:at + 1]

        def src_of(turn, t, c):
            if turn == "mix1":
                at = C_DQ + c * P if c < HD else C_NQ + (c - HD) * P
                return proj[:, t, at:at + P]
            if turn == "mix2":
                at = C_QA + c * P if c < 8 else C_IR + (c - 8) * P
                return proj2[:, t, at:at + P]
            return x[:, t, c * P:(c + 1) * P]

        WT = {"in1": (w["w_in"][0], 0), "out1": (w["w_out"][0], 0),
              "down1a": (w["w_down"][0], 0), "down1b": (w["w_down"][0], 24),
              "in2": (w["w_in_2"][0], 0), "out2": (w["w_out_2"][0], 0),
              "down2a": (w["w_down_2"][0], 0), "down2b": (w["w_down_2"][0], 32)}
        UP = {"up1a": (w["w_up"][0], 0, F1, 256), "up1b": (w["w_up"][0], 12 * 256, F1, 256),
              "up2a": (w["w_up_2"][0], 0, 256, 512), "up2b": (w["w_up_2"][0], 8 * 512, 256, 512)}
        PAIRS = {"in1": 5, "out1": 2, "down1a": 2, "down1b": 0, "in2": 5, "out2": 2, "down2a": 2, "down2b": 2}
        WIDTH = {("in1", 11): GATES, ("in2", 10): 256}

        def width(name, b):
            return WIDTH.get((name, b), NW)

        def used(n):
            return n + SPLITS

        def tok_order(eng, name, tile, take, before, defer, extra, ahead):
            g, pairs = G[name], PAIRS[name]
            T = g.tiles

            def one(i, b, base, prev):
                for j in range(T):
                    if not (b == 0 and j < AHEAD and prev is None and before is None):
                        tile(i, b, j, base + j)
                    if j == SPLITS - 1:
                        if prev is not None and take is not None:
                            take(*prev)
                        if prev is None and before is not None:
                            before()
            if pairs:
                for b in range(2):
                    one(0, b, g.first + b * T, (0, 0) if b else None)
                with eng.Fori(1, pairs) as i:
                    for b in range(2):
                        one(i, b, i * (2 * T) + (g.first + b * T), (i, 0) if b else (i - 1, 1))
            for b in range(2 * pairs, g.blocks):
                one(None, b, g.first + b * T, (None, b - 1) if b else None)
                if extra is not None:
                    extra(b)
            if defer:
                return lambda: take(None, g.blocks - 1)
            if ahead is not None:
                ahead()
            if take is not None:
                take(None, g.blocks - 1)

        def place(name, i, b):
            if i is None:
                return b * NW, b, b % 2, width(name, b)
            return i * (2 * NW) + b * NW, i * 2 + b, b, NW

        def span(start, size):
            return slice(start, start + size) if isinstance(start, int) else bass.ds(start, size)

        def turn_at(name, i, s):
            g = G[name]
            k = (g.first + s) // STAGES + 1
            return 16 * k if i is None else i * (2 * g.tiles // STAGES * 16) + 16 * k

        block = ctx.enter_context(nc.Block())

        @block.sync
        def _(sp):
            def tile_in(slot, n, src, dst):
                sp.wait_ge(ev("lo_done"), n + 1)
                sp.dma_start(dst, src).then_inc(ev(f"landed{slot}"), 16)

            def tok_block(name, i, b, base):
                m, k0 = WT[name]
                col, _, _, wd = place(name, i, b)
                for j in range(G[name].tiles):
                    k = k0 + TC * j
                    slot = (b * G[name].tiles + j) % STAGES
                    tile_in(slot, base + j, m[k * P:(k + TC) * P, span(col, wd)].rearrange("(c p) n -> p c n", p=P),
                            stage[:, slot, 0:TC * wd].rearrange("p (c n) -> p c n", c=TC))

            def tok(name):
                g = G[name]
                if PAIRS[name]:
                    with sp.Fori(0, PAIRS[name]) as i:
                        for b in range(2):
                            tok_block(name, i, b, i * (2 * g.tiles) + (g.first + b * g.tiles))
                for b in range(2 * PAIRS[name], g.blocks):
                    tok_block(name, None, b, g.first + b * g.tiles)

            def feat(name):
                m, c0, other, step = UP[name]
                with sp.Fori(0, G[name].blocks) as i:
                    for j in range(FT):
                        q, kh = j // (FT // 2), j % (FT // 2)
                        src = m[kh * FC * P:(kh + 1) * FC * P, bass.ds(i * step + (c0 + q * other), FW)]
                        tile_in(j, i * FT + (G[name].first + j), src.rearrange("(c p) n -> p c n", p=P),
                                stage[:, j, :].rearrange("p (c n) -> p c n", c=FC))

            tok("in1")
            for j in range(G["cmp"].tiles):
                m = (w["cmp_k_w1"], w["cmp_v_w1"])[j // 8][0]
                r = (j % 8) * FC * P
                tile_in(j % STAGES, G["cmp"].first + j, m[r:r + FC * P, :].rearrange("(c p) n -> p c n", p=P),
                        stage[:, j % STAGES, :].rearrange("p (c n) -> p c n", c=FC))
            tok("out1")
            feat("up1a")
            tok("down1a")
            feat("up1b")
            tok("down1b")
            tok("in2")
            tok("out2")
            feat("up2a")
            tok("down2a")
            feat("up2b")
            tok("down2b")
            for k in range(2 * TT):
                sp.wait_ge(ev("resid"), 3 * 2 * TT + k + 1)
                t, half_ = k // 2, slice((k % 2) * 1024, (k % 2 + 1) * 1024)
                sp.dma_start(out[0, t * P:(t + 1) * P, half_], x[:, t, half_]).then_inc(ev("stored"), 16)
            sp.wait_ge(ev("stored"), 16 * 2 * TT)

        @block.gpsimd
        def _(pool):
            pool.dma_start(tab, w["rel_bias"]).then_inc(ev("tab_in"), 16)
            pool.dma_start(hot, w["onehot"]).then_inc(ev("tab_in"), 16)
            pool.dma_start(flip, w["flip"]).then_inc(ev("flip_in"), 16)
            pool.dma_start(vecs[74:90, 0, :], w["rnn_lb_logits_2"].rearrange("l (r f) -> (l r) f", f=P)).then_inc(ev("more_vecs_in"), 16)
            pool.dma_start(vecs[0:CMP_LEN, 1, :], w["cmp_pos_k"][0]).then_inc(ev("more_vecs_in"), 16)
            pool.dma_start(vecs[CMP_LEN:2 * CMP_LEN, 1, :], w["cmp_pos_v"][0]).then_inc(ev("more_vecs_in"), 16)
            for j in range(3):
                pool.dma_start(vecs[0:88, 2 + j, :], w["conv_w"][0, j].rearrange("(r f) -> r f", f=P)).then_inc(ev("more_vecs_in"), 16)
            pool.dma_start(vecs[0:88, 5, :], w["conv_b"][0].rearrange("(r f) -> r f", f=P)).then_inc(ev("more_vecs_in"), 16)
            for j, nm in enumerate(("lambda_q1", "lambda_q2", "lambda_k1", "lambda_k2")):
                pool.dma_start(lamv[:, j, :], w[nm][0:1, :].broadcast_to((P, 64))).then_inc(ev("lam_in"), 16)
            pool.memset(half[:, :], -0.5).then_inc(ev("half_set"), 1)
            pool.wait_ge(ev("urow"), 2)
            pool.dma_start(scratch, urow).then_inc(ev("scratch_out"), 16)
            pool.wait_ge(ev("scratch_out"), 16)

            def hankel_rows(k):
                pool.dma_start(hankel, bass.AP(scratch.tensor, 8 * k * SK, [[1, P], [SK, 8], [1, S]])).then_inc(ev("hankel_in"), 16)
            hankel_rows(0)
            pool.wait_ge(ev("half_set"), 1)

            def inv_sqrt(n, dst, src, k):
                pool.wait_ge(ev("var"), n)
                pool.tensor_tensor(dst, src, half[:, 0:1].broadcast_to((P, k)), ALU.pow).then_inc(ev("rstd"), 1)

            inv_sqrt(1, small[:, 4:6], small[:, 2:4], 2)
            pool.wait_ge(ev("bias_mm"), 4)
            hankel_rows(1)
            pool.wait_ge(ev("qt_a"), 1)
            pool.wait_ge(ev("qt_d"), 1)
            for j, nm in enumerate(("cmp_k_w2", "cmp_v_w2")):
                pool.dma_start(w2[:, j, :, :], w[nm][0].rearrange("(a p) n -> p a n", p=P)).then_inc(ev("w2_in"), 16)
            pool.wait_ge(ev("cols"), 1)
            for v in range(2):
                for g in range(NKV):
                    for a in range(2):
                        src = QT[:, 24 + 2 * v + g, 16 * a:16 * a + 16 * NC].rearrange("p (c b) -> p b c", b=16)
                        add = posT[:, v, 16 * a:16 * a + 16].rearrange("p (b o) -> p b o", o=1).broadcast_to((P, 16, NC))
                        pool.tensor_tensor(blocks[:, v, 16 * a:16 * a + 16, g, :], src, add, ALU.add).then_inc(ev("blocks_done"), 1)
            pool.wait_ge(ev("qt_a"), 8)
            pool.wait_ge(ev("qt_d"), 8)
            pool.dma_start(keepc[:, 0, :, :], w["cmp_keep"]).then_inc(ev("keep_in"), 16)
            pool.dma_start(keepc[:, 1, :, :], w["cmp_drop"]).then_inc(ev("keep_in"), 16)
            pool.wait_ge(ev("tile_used"), used(G["cmp"].first + G["cmp"].tiles))
            pool.dma_start(grow[:, :], w["post_mix_norm"][0:1, :].broadcast_to((P, D))).then_inc(ev("grow_in"), 16)
            inv_sqrt(2, hstat[:, 2, :], hstat[:, 1, :], 16)
            inv_sqrt(3, small[:, 4:6], small[:, 2:4], 2)
            inv_sqrt(4, small[:, 4:6], small[:, 2:4], 2)
            pool.wait_ge(ev("g_lo"), 1 + 22)
            pool.dma_start(grow[:, :], w["post_ffn_norm"][0:1, :].broadcast_to((P, D))).then_inc(ev("grow_in"), 16)
            inv_sqrt(5, small[:, 4:6], small[:, 2:4], 2)
            pool.wait_ge(ev("resid"), 4 * TT)
            pool.dma_start(grow[:, :], w["mix_post_gain_2"][0:1, :].broadcast_to((P, D))).then_inc(ev("grow_in"), 16)
            pool.dma_start(far[:, :], w["far"]).then_inc(ev("mix2_in"), 16)
            pool.dma_start(sinks[:, 0, :], w["attn_sinks_2"][0:1, :].broadcast_to((P, HA))).then_inc(ev("mix2_in"), 16)
            pool.dma_start(sums[:, :, :], w["sums"]).then_inc(ev("mix2_in"), 16)
            pool.dma_start(keep[:, :, :], w["keep"]).then_inc(ev("mix2_in"), 16)
            inv_sqrt(6, small[:, 4:6], small[:, 2:4], 2)
            pool.wait_ge(ev("key_done"), 1)
            for n in range(HR * TT):
                h, t = n // TT, n % TT
                key = QT2[:, 24 + h, t * P:(t + 1) * P]
                pool.wait_ge(ev("fac"), n + 1)
                if t == 0:
                    if h >= 1:
                        pool.wait_ge(ev("cross_mm"), h)
                    pool.tensor_tensor(kcross[:, :], fac[:, 7, :], key, ALU.mult).then_inc(ev("kcross_done"), 1)
                if n >= 1:
                    pool.wait_ge(ev("att_mm"), n)
                many = key.rearrange("p (o t) -> p o t", o=1).broadcast_to((P, 7, P))
                pool.tensor_tensor(kf[:, 0:7, :], fac[:, 0:7, :], many, ALU.mult).then_inc(ev("kf"), 1)
            inv_sqrt(7, small[:, 4:6], small[:, 2:4], 2)
            inv_sqrt(8, hstat[:, 2, :], hstat[:, 1, :], 16)
            inv_sqrt(9, small[:, 4:6], small[:, 2:4], 2)
            inv_sqrt(10, small[:, 4:6], small[:, 2:4], 2)
            pool.wait_ge(ev("g_lo"), 1 + 22 + 16)
            pool.dma_start(grow[:, :], w["mlp_post_gain_2"][0:1, :].broadcast_to((P, D))).then_inc(ev("grow_in"), 16)
            inv_sqrt(11, small[:, 4:6], small[:, 2:4], 2)

        NBR = HD + 2 * HN

        def bank_of(first, r):
            return first if r <= HD else first + 2 * (r % 2)
        NORMED = {"out1": 0, "down1b": 1, "out2": 2, "down2b": 3}
        TURN1 = [12, 13] + list(range(12)) + [14, 15]
        TURN2 = [0, 1, 2, 3, 4, 8, 9, 10, 11, 12, 13, 14, 15]

        @block.scalar
        def _(act):
            squares = [PS[:, 4 * t:4 * t + 4, :].rearrange("p b n -> p (b n)") for t in range(TT)]

            def first_tiles(name):
                n = G[name].first
                for j in range(AHEAD):
                    act.wait_ge(ev("tile_used"), used(n + j - SPLITS + 1))
                    act.wait_ge(ev(f"landed{j}"), 16 * (n // STAGES + 1))
                    nc.scalar.activation(whi[:, j, :], stage[:, j, :], ACT.Copy).then_inc(ev("hi_done"), 1)

            def tok(name, dst, before=None, defer=False, then_first=None):
                g = G[name]
                junk = PS[:, 4 * (1 - g.turned):4 * (1 - g.turned) + 4, :]

                def tile(i, b, j, n):
                    s = b * g.tiles + j
                    wd = TC * (width(name, b) if i is None else NW)
                    act.wait_ge(ev("tile_used"), used(n - SPLITS + 1))
                    act.wait_ge(ev(f"landed{s % STAGES}"), turn_at(name, i, s))
                    nc.scalar.activation(whi[:, s % SPLITS, 0:wd], stage[:, s % STAGES, 0:wd], ACT.Copy)\
                        .then_inc(ev("hi_done"), 1)

                def take(i, b):
                    col, nb, bank, wd = place(name, i, b)
                    if dst == "squares of sums":
                        act.wait_ge(ev("acc_free"), nb + (g.acc + 3))
                    else:
                        act.wait_ge(ev("tile_used"), used((nb + 1) * g.tiles + g.first))
                    act.wait_ge(ev("begun"), 1)
                    if name in NORMED:
                        for t in range(TT):
                            src = yacc[:, t, span(col, wd)] if dst == "squares of sums" else PS[:, 2 * bank + t, 0:wd]
                            last = nc.scalar.activation(junk[:, 2 * bank + t, :], src, ACT.Square, accum_out=parts[:, t, span(nb, 1)])
                        last.then_inc(ev("part"), 1)
                        return
                    for t in range(TT):
                        last = nc.scalar.activation(dst[:, t, span(col, wd)], PS[:, 4 * g.turned + 2 * bank + t, 0:wd], ACT.Copy)
                    last.then_inc(ev("acc_free"), 1)
                tail = tok_order(act, name, tile, take, before, defer, None,
                                 None if then_first is None else lambda: first_tiles(then_first))
                if tail is not None:
                    return tail
                if name not in NORMED:
                    act.wait_ge(ev("acc_free"), 2 + g.acc + g.blocks)

            def squares_of_x(n):
                for k in range(2 * TT):
                    if n:
                        act.wait_ge(ev("resid"), 2 * TT * (n - 1) + k + 1)
                    half_ = slice((k % 2) * 1024, (k % 2 + 1) * 1024)
                    junk = PS[:, 2 * k:2 * k + 2, :].rearrange("p b n -> p (b n)") if n else yacc[:, k // 2, half_]
                    last = nc.scalar.activation(junk, x[:, k // 2, half_], ACT.Square, accum_out=parts[:, k // 2, 4 + k % 2:5 + k % 2])
                last.then_inc(ev("ssq"), 1)

            def split_turned(turn):
                for c in range(KC):
                    act.wait_ge(ev("turned_" + turn), c // 2 + 1)
                    nc.scalar.activation(actT[:, c, 0:S], PS[:, c // 2, (c % 2) * S:(c % 2 + 1) * S], ACT.Copy,
                                         scale=gain_of(turn, c)).then_inc(ev("acthi_" + turn), 1)

            def feat(name, conv, before=None):
                g = G[name]
                gT = gT1 if conv else gT2

                def tiles(i, js):
                    for j in js:
                        act.wait_ge(ev("tile_used"), used(i * FT + (g.first + j - SPLITS + 1)))
                        act.wait_ge(ev(f"landed{j}"), i * 16 + (g.first // STAGES + 1) * 16)
                        nc.scalar.activation(whi[:, j % SPLITS, :], stage[:, j, :], ACT.Copy).then_inc(ev("hi_done"), 1)

                def low_sums(i, s):
                    act.wait_ge(ev("tile_used"), used(i * FT + (g.first + FT)))
                    nc.scalar.activation(lowsum, PS[:, 4 * (s ^ g.turned):4 * (s ^ g.turned) + 4, S:2 * S], ACT.Copy).then_inc(ev("low_out"), 1)

                def first_tap(i):
                    act.wait_ge(ev("g_lo"), i + (g.acc + 1))
                    act.wait_ge(ev("pre_done"), i + (g.acc + 3))
                    act.wait_ge(ev("begun"), 1)
                    for a in range(4):
                        f = i * 2 + (2 * (g.acc if name == "up1b" else 0) + a % 2 + F1 // P * (a // 2))
                        nc.scalar.activation(post[:, a, :], pre[:, a, 2:2 + S], ACT.Identity,
                                             scale=convT[:, 2, span(f, 1)], bias=convT[:, 3, span(f, 1)])\
                            .then_inc(ev("tap"), 1)

                def high_parts(i):
                    if conv:
                        act.wait_ge(ev("conv_done"), i + (g.acc + 1))
                        nc.scalar.activation(lowsum[:, 0:2, :], post[:, 0:2, :], ACT.Gelu_apprx_tanh).then_inc(ev("gelu"), 1)
                    k = 2 if conv else 4
                    act.wait_ge(ev("prod"), i + (g.acc + 1))
                    act.wait_ge(ev("begun"), 1)
                    nc.scalar.activation(gT[:, span(i * k, k), 0:S], post[:, 0:k, :], ACT.Copy).then_inc(ev("g_hi"), 1)

                def one(i, s, prev):
                    tiles(i, (3,) if prev is None and before is None else (0, 1, 2, 3))
                    if prev is None and before is not None:
                        before()
                    if prev is not None:
                        low_sums(prev, 1 - s)
                        if conv:
                            first_tap(prev)
                    tiles(i, (4, 5))
                    if prev is not None:
                        high_parts(prev)
                    tiles(i, (6, 7))
                one(0, 0, None)
                one(1, 1, 0)
                with act.Fori(1, g.blocks // 2) as r:
                    one(r * 2, 0, r * 2 - 1)
                    one(r * 2 + 1, 1, r * 2)

                def tail():
                    low_sums(g.blocks - 1, 1)
                    if conv:
                        first_tap(g.blocks - 1)
                    high_parts(g.blocks - 1)
                return tail

            act.sem_inc(ev("begun"), 1)
            for t in range(TT):
                act.dma_start(x[:, t, :], w["x"][0, t * P:(t + 1) * P, :]).then_inc(ev("x_in"), 16)
            act.dma_start(ident[:, :], w["ident"]).then_inc(ev("ident_in"), 16)
            for r0, nm, k in ((0, "pre_mix_norm", 16), (16, "pre_ffn_norm", 16), (32, "mix_pre_gain_2", 16),
                              (48, "mlp_pre_gain_2", 16), (64, "attn_out_gain_2", 8), (72, "diff_subln", 1),
                              (73, "rnn_norm_gain_2", 1)):
                act.dma_start(vecs[r0:r0 + k, 0, :], w[nm][0].rearrange("(r f) -> r f", f=P)).then_inc(ev("vecs_in"), 16)
            first_tiles("in1")
            act.wait_ge(ev("x_in"), 32)
            squares_of_x(0)
            split_turned("n1")
            act.wait_ge(ev("lam_dot"), 1)
            nc.scalar.activation(small[:, 10:12], small[:, 8:10], ACT.Exp)
            nc.scalar.activation(lbs[:, 16:32], lbs[:, 0:16], ACT.Exp).then_inc(ev("early_exp"), 1)
            tok("in1", proj)
            for m in range(0, 16, 2):
                n = TURN1[m]
                act.wait_ge(ev("qt_mm"), m + 1)
                root = 64 ** -0.5 if n < 4 else P ** -0.5 if 8 <= n < 12 else 1.0
                nc.scalar.activation(QT[:, 2 * n:2 * n + 2, :].rearrange("p c s -> p (c s)"), PS[:, m % 8, :], ACT.Copy,
                                     scale=root).then_inc(ev("qt_a"), 1)
            nc.scalar.activation(gates[:, :, :], proj[:, :, C_G:C_G + GATES], ACT.Sigmoid).then_inc(ev("gates_done"), 1)

            def compress(s):
                if s in (4, 8):
                    v = s // 4 - 1
                    act.wait_ge(ev("tile_used"), used(G["cmp"].first + STAGES * (v + 1)))
                    nc.scalar.activation(hid[:, v, :, :], PS[:, 6:8, 0:2 * NC], ACT.Gelu_apprx_tanh).then_inc(ev("hid_done"), 1)
                if s == 8:
                    act.sem_inc(ev("hi_done"), G["cmp"].tiles)

            for s in range(NBR + 2):
                compress(s)
                if s < NBR:
                    act.wait_ge(ev("max1"), s + 1)
                    for m in range(2 if s < HD else 1):
                        for q, (lo, hi) in enumerate(((0, P), (P, SK))):
                            last = nc.scalar.activation(scores[:, s % 2, m, lo:hi], scores[:, s % 2, m, lo:hi], ACT.Exp,
                                                        bias=stat[:, s % 2, 2 * m + q:2 * m + q + 1],
                                                        accum_out=stat[:, s % 2, 4 + 2 * m + q:5 + 2 * m + q])
                    last.then_inc(ev("exp1"), 1)
                if s >= 2:
                    act.wait_ge(ev("pt_mm1"), s - 1)
                    if s >= 4:
                        act.wait_ge(ev("pv_mm1"), s - 3)
                    last = nc.scalar.activation(probsT[:, s % 2, :], PS[:, bank_of(4, s - 2), 0:SK], ACT.Copy)
                    if s - 2 >= HD:
                        last = nc.scalar.activation(pcT[:, s % 2, :], PS[0:NC, bank_of(4, s - 2), SK:SK + P], ACT.Copy)
                    last.then_inc(ev("pt_out1"), 1)
                if s == 9:
                    act.wait_ge(ev("cmp_shift"), 1)
                    nc.scalar.activation(pcs, pcs, ACT.Exp).then_inc(ev("cmp_exp"), 1)
            first_tiles("out1")
            act.wait_ge(ev("o_out1"), NBR)
            for n in range(HD * TT):
                h, t = n // TT, n % TT
                last = nc.scalar.activation(work[:, n * P:(n + 1) * P], proj[:, t, C_DQ + h * P:C_DQ + (h + 1) * P], ACT.Square,
                                            accum_out=hstat[:, 0, n:n + 1])
            last.then_inc(ev("hssq"), 1)
            split_turned("mix1")
            tok("out1", "squares", then_first="up1a")
            squares_of_x(1)
            split_turned("n2")
            last_up = feat("up1a", True)
            last_down = tok("down1a", yacc, before=last_up, defer=True)
            last_up = feat("up1b", True, before=last_down)
            tok("down1b", "squares of sums", before=last_up, then_first="in2")
            squares_of_x(2)
            split_turned("n3")
            tok("in2", proj2)
            for m, n in enumerate(TURN2):
                if m % 2 == 0:
                    act.wait_ge(ev("qt2_mm"), m + 1)
                    nc.scalar.activation(QT2[:, 2 * n:2 * n + 2, :].rearrange("p c s -> p (c s)"), PS[:, m % 8, :], ACT.Copy,
                                         scale=64 ** -0.5 if n < 4 else 1.0).then_inc(ev("qt2_a"), 1)
            act.wait_ge(ev("qt2_a"), 7)
            act.wait_ge(ev("qt2_d"), 6)
            nc.scalar.activation(sig_q, QT2[:, 16:24, :], ACT.Sigmoid).then_inc(ev("sig"), 1)
            nc.scalar.activation(QT2[:, 24:32, :], QT2[:, 24:32, :], ACT.Sigmoid).then_inc(ev("sig"), 1)
            nc.scalar.activation(sig_g, proj2[:, :, C_GR:C_GR + 1024], ACT.Sigmoid).then_inc(ev("sig"), 1)
            act.wait_ge(ev("f_done"), 1)
            nc.scalar.activation(lnf, QT2[:, 24:32, :], ACT.Ln).then_inc(ev("ln_done"), 1)
            for n in range(4):
                act.wait_ge(ev("logf_mm"), n + 1)
                nc.scalar.activation(logf[:, n // 2, 4 * (n % 2):4 * (n % 2) + 4, :].rearrange("p a b -> p (a b)"),
                                     PS[:, n, :], ACT.Copy).then_inc(ev("logf_out"), 1)
            def window_exp(s):
                if s < HA:
                    act.wait_ge(ev("max2"), s + 1)
                    for q, (lo, hi) in enumerate(((0, P), (P, SK))):
                        nc.scalar.activation(scores2[:, s % 2, lo:hi], scores2[:, s % 2, lo:hi], ACT.Exp,
                                             bias=stat[:, s % 2, q:q + 1], accum_out=stat[:, s % 2, 4 + q:5 + q])
                    nc.scalar.activation(stat[:, s % 2, 6:8], stat[:, s % 2, 0:2], ACT.Exp,
                                         bias=sinks[:, 0, s:s + 1]).then_inc(ev("exp2"), 1)

            def window_turned(s):
                if 2 <= s < HA + 2:
                    act.wait_ge(ev("pt_mm2"), s - 1)
                    if s >= 4:
                        act.wait_ge(ev("pv_mm2"), s - 3)
                    nc.scalar.activation(probsT2[:, s % 2, :], PS[:, 7, 0:SK], ACT.Copy).then_inc(ev("pt_out2"), 1)

            def cross_out(h):
                act.wait_ge(ev("cross_mm"), h + 1)
                if h >= 1:
                    act.wait_ge(ev("o_mm"), 2 * h)
                nc.scalar.activation(crossT[:, :], PS[:, 4, 0:P], ACT.Copy).then_inc(ev("cross_out"), 1)

            def o_out(n):
                h, t = n // TT, n % TT
                act.wait_ge(ev("o_mm"), n + 1)
                nc.scalar.activation(proj2[:, t, C_FR + h * P:C_FR + (h + 1) * P], PS[:, 5, 0:P], ACT.Copy)
                nc.scalar.activation(PS[:, 5, P:2 * P], PS[:, 5, 0:P], ACT.Square, accum_out=hstat[:, 0, n:n + 1])\
                    .then_inc(ev("o_out"), 1)

            NR = HR * TT

            def decays(n):
                act.wait_ge(ev("exps_mm"), n + 1)
                if n >= 1:
                    act.wait_ge(ev("qf"), n)
                    act.wait_ge(ev("kf"), n)
                nc.scalar.activation(fac.rearrange("p a b -> p (a b)"), PS[:, 0:2, :].rearrange("p a b -> p (a b)"),
                                     ACT.Exp).then_inc(ev("fac"), 1)
            decays(0)
            for n in range(NR + 3):
                window_turned(n)
                if 1 <= n <= NR and (n - 1) % TT == 1:
                    cross_out((n - 1) // TT)
                if n >= 3:
                    o_out(n - 3)
                if n + 1 < NR:
                    decays(n + 1)
                window_exp(n)
            first_tiles("out2")
            act.wait_ge(ev("o_out2"), HA)
            act.wait_ge(ev("o_out"), NR)
            for t in range(TT):
                last = nc.scalar.activation(squares[t][:, 0:1024], proj2[:, t, C_QA:C_QA + 1024],
                                            ACT.Square, accum_out=small[:, t:t + 1])
            last.then_inc(ev("ssq"), 1)
            split_turned("mix2")
            tok("out2", "squares", then_first="up2a")
            squares_of_x(3)
            split_turned("n4")
            last_up = feat("up2a", False)
            last_down = tok("down2a", yacc, before=last_up, defer=True)
            last_up = feat("up2b", False, before=last_down)
            tok("down2b", "squares of sums", before=last_up)

        @block.vector
        def _(dve):
            def first_tiles(name):
                n = G[name].first
                for j in range(AHEAD):
                    dve.wait_ge(ev("hi_done"), n + j + 1)
                    nc.vector.tensor_tensor(wlo[:, j, :], stage[:, j, :], whi[:, j, :].bitcast(F32), ALU.subtract)\
                        .then_inc(ev("lo_done"), 1)

            def tok(name, add, before=None, extra=None, then_first=None):
                g = G[name]

                def tile(i, b, j, n):
                    s = b * g.tiles + j
                    wd = TC * (width(name, b) if i is None else NW)
                    dve.wait_ge(ev("hi_done"), n + 1)
                    nc.vector.tensor_tensor(wlo[:, s % SPLITS, 0:wd], stage[:, s % STAGES, 0:wd],
                                            whi[:, s % SPLITS, 0:wd].bitcast(F32), ALU.subtract).then_inc(ev("lo_done"), 1)

                def take(i, b):
                    col, nb, bank, wd = place(name, i, b)
                    if add:
                        dve.wait_ge(ev("tile_used"), used((nb + 1) * g.tiles + g.first))
                        for t in range(TT):
                            last = nc.vector.tensor_tensor(yacc[:, t, span(col, wd)], PS[:, 4 * g.turned + 2 * bank + t, 0:wd],
                                                           yacc[:, t, span(col, wd)], ALU.add)
                        last.then_inc(ev("acc_free"), 1)
                    dve.wait_ge(ev("grow_in"), 16 * (NORMED[name] + 1))
                    dve.wait_ge(ev("part"), nb + (4 * NORMED[name] + 1))
                    for t in range(TT):
                        src = yacc[:, t, span(col, wd)] if add else PS[:, 2 * bank + t, 0:wd]
                        last = nc.vector.tensor_tensor(yacc[:, t, span(col, wd)], src, grow[:, span(col, wd)], ALU.mult)
                    if not add:
                        last.then_inc(ev("acc_free"), 1)
                tok_order(dve, name, tile, take if name in NORMED else None, before, False, extra,
                          None if then_first is None else lambda: first_tiles(then_first))

            def feat(name, conv, before=None):
                g = G[name]
                gT = gT1 if conv else gT2

                def tiles(i, js):
                    for j in js:
                        dve.wait_ge(ev("hi_done"), i * FT + (g.first + j + 1))
                        nc.vector.tensor_tensor(wlo[:, j % SPLITS, :], stage[:, j, :], whi[:, j % SPLITS, :].bitcast(F32),
                                                ALU.subtract).then_inc(ev("lo_done"), 1)

                def join(i, s):
                    dve.wait_ge(ev("low_out"), i + (g.acc + 1))
                    to = pre[:, :, 2:2 + S] if conv else lowsum
                    nc.vector.tensor_tensor(to, PS[:, 4 * (s ^ g.turned):4 * (s ^ g.turned) + 4, 0:S], lowsum, ALU.add).then_inc(ev("pre_done"), 1)

                def taps(i):
                    for tap, name_ in ((1, "tap_mid"), (0, "conv_done")):
                        if tap:
                            dve.wait_ge(ev("tap"), i * 4 + 4 * (g.acc + 1))
                        else:
                            dve.wait_ge(ev("tap_mid"), i + (g.acc + 1))
                        for a in range(4):
                            f = i * 2 + (2 * (g.acc if name == "up1b" else 0) + a % 2 + F1 // P * (a // 2))
                            last = nc.vector.scalar_tensor_tensor(post[:, a, :], pre[:, a, tap:tap + S],
                                                                  convT[:, tap, span(f, 1)], post[:, a, :],
                                                                  ALU.mult, ALU.add)
                        last.then_inc(ev(name_), 1)

                def product(i):
                    if conv:
                        dve.wait_ge(ev("gelu"), i + (g.acc + 1))
                        nc.vector.tensor_tensor(post[:, 0:2, :], lowsum[:, 0:2, :], post[:, 2:4, :], ALU.mult)\
                            .then_inc(ev("prod"), 1)
                    else:
                        dve.wait_ge(ev("pre_done"), i + (g.acc + 3))
                        nc.vector.scalar_tensor_tensor(post[:, :, :], lowsum, 0.0, lowsum, ALU.max, ALU.mult)\
                            .then_inc(ev("prod"), 1)

                def low_parts(i):
                    k = 2 if conv else 4
                    dve.wait_ge(ev("g_hi"), i + (g.acc + 1))
                    nc.vector.tensor_tensor(gT[:, span(i * k, k), S:2 * S], post[:, 0:k, :],
                                            gT[:, span(i * k, k), 0:S].bitcast(F32), ALU.subtract).then_inc(ev("g_lo"), 1)

                def one(i, s, prev):
                    tiles(i, (3,) if prev is None and before is None else (0, 1, 2, 3))
                    if prev is None and before is not None:
                        before()
                    if prev is not None:
                        join(prev, 1 - s)
                        if conv:
                            taps(prev)
                    tiles(i, (4, 5))
                    if prev is not None:
                        product(prev)
                        low_parts(prev)
                    tiles(i, (6, 7))
                one(0, 0, None)
                one(1, 1, 0)
                with dve.Fori(1, g.blocks // 2) as r:
                    one(r * 2, 0, r * 2 - 1)
                    one(r * 2 + 1, 1, r * 2)

                def tail():
                    join(g.blocks - 1, 1)
                    if conv:
                        taps(g.blocks - 1)
                    product(g.blocks - 1)
                    low_parts(g.blocks - 1)
                return tail

            def mean_square(k, src, dst, count, ready, n):
                dve.wait_ge(ev(ready), n)
                nc.vector.tensor_scalar(dst, src, 1.0 / count, EPS, ALU.mult, ALU.add).then_inc(ev("var"), 1)

            def root_of_x(k, n):
                dve.wait_ge(ev("ssq"), k)
                me(nc.vector.tensor_reduce(small[:, 0:2], parts[:, :, 4:6], AX.X, ALU.add))
                nc.vector.tensor_scalar(small[:, 2:4], small[:, 0:2], 1.0 / D, EPS, ALU.mult, ALU.add).then_inc(ev("var"), 1)
                dve.wait_ge(ev("rstd"), n)
                for t in range(TT):
                    nc.vector.tensor_scalar(diag[:, t, :], ident[:, :], small[:, 4 + t:5 + t], None, ALU.mult)\
                        .then_inc(ev("diag"), 1)

            def split_turned(turn):
                for c in range(KC):
                    dve.wait_ge(ev("acthi_" + turn), c // 2 * 2 + 2)
                    nc.vector.scalar_tensor_tensor(actT[:, c, S:2 * S], PS[:, c // 2, (c % 2) * S:(c % 2 + 1) * S],
                                                   gain_of(turn, c), actT[:, c, 0:S].bitcast(F32),
                                                   ALU.mult, ALU.subtract).then_inc(ev("actlo_" + turn), 1)

            def residual(name, n):
                dve.wait_ge(ev("part"), 4 * NORMED[name] + 4)
                me(nc.vector.tensor_reduce(small[:, 0:2], parts[:, :, 0:4], AX.X, ALU.add))
                nc.vector.tensor_scalar(small[:, 2:4], small[:, 0:2], 1.0 / D, EPS, ALU.mult, ALU.add).then_inc(ev("var"), 1)
                dve.wait_ge(ev("rstd"), n)
                for k in range(2 * TT):
                    t, half_ = k // 2, slice((k % 2) * 1024, (k % 2 + 1) * 1024)
                    nc.vector.scalar_tensor_tensor(x[:, t, half_], yacc[:, t, half_], small[:, 4 + t:5 + t], x[:, t, half_],
                                                   ALU.mult, ALU.add).then_inc(ev("resid"), 1)

            def me(ins):
                then(dve, "dve", ins)

            def nothing():
                pass

            dve.sem_inc(ev("lo_done"), STAGES)
            dve.sem_inc(ev("acc_free"), 2)
            dve.sem_inc(ev("pre_done"), 2)
            dve.sem_inc(ev("g_lo"), 1)
            dve.wait_ge(ev("urow_mm"), 1)
            nc.vector.memset(urow[:, S:SK], NEG).then_inc(ev("urow"), 1)
            nc.vector.tensor_copy(urow[:, 0:S], PS[0:16, 5, 0:S]).then_inc(ev("urow"), 1)
            dve.wait_ge(ev("vecs_mm"), 1)
            me(nc.vector.tensor_copy(cols[:, 0:74], PS[:, 7, 0:74]))
            me(nc.vector.tensor_scalar(cols[:, 72:73], cols[:, 72:73], 1.0 - LAM_INIT, None, ALU.mult))
            me(nc.vector.memset(cols[:, 74:75], 1.0))
            me(nc.vector.tensor_copy(cols[:, C_LB:C_LB + 16], PS[:, 7, 74:90]))
            nc.vector.tensor_copy(convT[:, :, :], PS[:, 6, :].rearrange("p (j f) -> p j f", j=4)[:, :, 0:88])
            nc.vector.tensor_copy(posT[:, :, :], PS[:, 7, 128:192].rearrange("p (v l) -> p v l", v=2)).then_inc(ev("cols"), 1)
            dve.wait_ge(ev("lam_in"), 64)
            me(nc.vector.tensor_tensor(lamv[:, 0:2, :], lamv[:, 0:2, :], lamv[:, 2:4, :], ALU.mult))
            me(nc.vector.tensor_tensor(lbs[:, 32:40], cols[:, C_LB:C_LB + 8], cols[:, C_LB + 8:C_LB + 16], ALU.max))
            nc.vector.tensor_tensor(lbs[:, 0:8], cols[:, C_LB:C_LB + 8], lbs[:, 32:40], ALU.subtract)
            nc.vector.tensor_tensor(lbs[:, 8:16], cols[:, C_LB + 8:C_LB + 16], lbs[:, 32:40], ALU.subtract)
            nc.vector.tensor_reduce(small[:, 8:10], lamv[:, 0:2, :], AX.X, ALU.add).then_inc(ev("lam_dot"), 1)
            first_tiles("in1")
            dve.wait_ge(ev("ident_in"), 16)
            root_of_x(1, 1)
            split_turned("n1")
            dve.wait_ge(ev("early_exp"), 1)
            me(nc.vector.tensor_tensor(small[:, 12:13], small[:, 11:12], small[:, 10:11], ALU.subtract))
            me(nc.vector.tensor_scalar(small[:, 12:13], small[:, 12:13], LAM_INIT, None, ALU.subtract))
            me(nc.vector.tensor_tensor(lbs[:, 32:40], lbs[:, 16:24], lbs[:, 24:32], ALU.add))
            me(nc.vector.reciprocal(lbs[:, 32:40], lbs[:, 32:40]))
            me(nc.vector.tensor_tensor(lbs[:, 32:40], lbs[:, 16:24], lbs[:, 32:40], ALU.mult))
            me(nc.vector.tensor_scalar(lbs[:, 40:48], lbs[:, 32:40], -1.0, 1.0, ALU.mult, ALU.add))

            def bias_rows(b):
                if b < G["in1"].blocks - 2:
                    return
                for n in range(4 * (b - G["in1"].blocks + 2), 4 * (b - G["in1"].blocks + 3)):
                    dve.wait_ge(ev("bias_mm"), n + 1)
                    rows = PS[:, 4 + n % 4, :].rearrange("p (h j) -> p h j", h=2)
                    nc.vector.tensor_copy(bias[:, 2 * n:2 * n + 2, P:SK], rows)
                    nc.vector.tensor_copy(bias[:, 2 * n:2 * n + 2, 0:P], rows[:, :, P:2 * P]).then_inc(ev("bias_done"), 1)
            tok("in1", False, extra=bias_rows)
            for m in range(1, 16, 2):
                n = TURN1[m]
                dve.wait_ge(ev("qt_mm"), m + 1)
                root = 64 ** -0.5 if n < 4 else P ** -0.5 if 8 <= n < 12 else 1.0
                nc.vector.tensor_scalar(QT[:, 2 * n:2 * n + 2, :].rearrange("p c s -> p (c s)"), PS[:, m % 8, :], root, None,
                                        ALU.mult).then_inc(ev("qt_d"), 1)
            flat_h = cst.rearrange("p a h t -> p a (h t)")
            flat_p = pcs.rearrange("p h t c -> p (h t) c")

            def wide(k):
                return flat_h[:, k, :].rearrange("p (n o) -> p n o", o=1).broadcast_to((P, HN * TT, NC))

            def masked(src, k, op):
                for t in range(TT):
                    mask = keepc[:, k, t, :].rearrange("p (o c) -> p o c", o=1).broadcast_to((P, HN, NC))
                    last = nc.vector.tensor_tensor(pcs[:, :, t, :], src[:, :, t, :], mask, op)
                me(last)

            def compressed(s):
                if s == 9:
                    dve.wait_ge(ev("kc_mm"), 1)
                    nc.vector.tensor_copy(kcT, PS[:, 7, 0:2 * NC])
                    nc.vector.tensor_copy(vc, PS[0:NC, 7, 2 * P:4 * P].rearrange("p (g d) -> p g d", g=NKV)).then_inc(ev("kc_out"), 1)

            def compressed_scores(s):
                if s == 9:
                    dve.wait_ge(ev("keep_in"), 32)
                    dve.wait_ge(ev("cmp_mm"), 1)
                    masked(PS[:, 7, 0:256].rearrange("p (h t c) -> p h t c", h=HN, t=TT)[:, :, :, 0:NC], 0, ALU.mult)
                    masked(pcs, 1, ALU.add)
                    me(nc.vector.tensor_reduce(flat_h[:, 0, :], flat_p, AX.X, ALU.max))
                    nc.vector.tensor_tensor(flat_p, flat_p, wide(0), ALU.subtract).then_inc(ev("cmp_shift"), 1)

            def compressed_probs(s):
                if s == 10:
                    dve.wait_ge(ev("cmp_exp"), 1)
                    dve.wait_ge(ev("gates_done"), 1)
                    masked(pcs, 0, ALU.mult)
                    me(nc.vector.tensor_reduce(flat_h[:, 1, :], flat_p, AX.X, ALU.add))
                    me(nc.vector.tensor_scalar(flat_h[:, 1, :], flat_h[:, 1, :], TINY, None, ALU.max))
                    me(nc.vector.reciprocal(flat_h[:, 1, :], flat_h[:, 1, :]))
                    gate0 = gates[:, :, :].rearrange("p t (h b) -> p h t b", b=3)[:, :, :, 0]
                    me(nc.vector.tensor_tensor(cst[:, 2, :, :], cst[:, 1, :, :], gate0, ALU.mult))
                    nc.vector.tensor_tensor(flat_p, flat_p, wide(2), ALU.mult).then_inc(ev("cmp_probs"), 1)

            def front(s):
                dve.wait_ge(ev("log_mm1"), s + 1)
                if s >= 2:
                    dve.wait_ge(ev("pt_mm1"), s - 1)
                head = s if s < HD else HD + (s - HD) // 2
                maps = 2 if s < HD else 1
                b = bias[:, head:head + 1, :].broadcast_to((P, maps, SK))
                me(nc.vector.tensor_tensor(scores[:, s % 2, 0:maps, :], PS[:, 2 * (s % 2):2 * (s % 2) + maps, 0:SK], b, ALU.add))
                nm = stat[:, s % 2, 0:4].rearrange("p (m q) -> p m q", q=2)
                nc.vector.tensor_reduce(nm[:, 0:maps, 0], scores[:, s % 2, 0:maps, 0:P], AX.X, ALU.max, negate=True)
                nc.vector.tensor_reduce(nm[:, 0:maps, 1], scores[:, s % 2, 0:maps, P:SK], AX.X, ALU.max, negate=True)\
                    .then_inc(ev("max1"), 1)

            def weigh(s):
                dve.wait_ge(ev("exp1"), s + 1)
                st = stat[:, s % 2, :]
                k = 4 if s < HD else 2
                me(nc.vector.reciprocal(st[:, 8:8 + k], st[:, 4:4 + k]))
                if s < HD:
                    me(nc.vector.tensor_scalar(st[:, 10:12], st[:, 10:12], small[:, 12:13], None, ALU.mult))
                    if s >= 2:
                        dve.wait_ge(ev("pt_mm1"), s - 1)
                    for q, (lo, hi) in enumerate(((0, P), (P, SK))):
                        last = nc.vector.tensor_scalar(probs[:, s % 2, lo:hi], scores[:, s % 2, 0, lo:hi], st[:, 8 + q:9 + q],
                                                       None, ALU.mult)
                    me(last)
                    for q, (lo, hi) in enumerate(((0, P), (P, SK))):
                        last = nc.vector.scalar_tensor_tensor(probs[:, s % 2, lo:hi], scores[:, s % 2, 1, lo:hi],
                                                              st[:, 10 + q:11 + q], probs[:, s % 2, lo:hi],
                                                              ALU.mult, ALU.add)
                    last.then_inc(ev("probs1"), 1)
                else:
                    r = s - HD
                    g = gates[:, :, :].rearrange("p t (h b) -> p h t b", b=3)[:, r // 2, :, 1 + r % 2]
                    nc.vector.tensor_tensor(weights[:, s % 4, :], st[:, 8:10], g, ALU.mult).then_inc(ev("probs1"), 1)

            def take_out(s):
                dve.wait_ge(ev("pv_mm1"), s + 1)
                o = PS[:, bank_of(5, s), 0:3 * P].rearrange("p (t d) -> p t d", t=3)
                if s < HD:
                    nc.vector.tensor_copy(proj[:, :, C_DQ + s * P:C_DQ + (s + 1) * P], o[:, 0:TT, :]).then_inc(ev("o_out1"), 1)
                    return
                h, mine = (s - HD) // 2, (s - HD) % 2
                at = [proj[:, t, C_NQ + h * P:C_NQ + (h + 1) * P] for t in range(TT)]
                wt = weights[:, s % 4, :]
                ln["dve"] += 1
                if mine == 0:
                    nc.vector.tensor_copy(at[0], o[:, 2, :]).then_inc(ev("self_dve"), 1)
                    nc.vector.tensor_scalar(at[1], o[:, 1, :], wt[:, 1:2], None, ALU.mult)
                else:
                    nc.vector.tensor_tensor(at[1], o[:, 2, :], at[1], ALU.add).then_inc(ev("self_dve"), 1)
                    nc.vector.scalar_tensor_tensor(at[0], o[:, 0, :], wt[:, 0:1], at[0], ALU.mult, ALU.add)
                dve.wait_ge(ev("self_dve"), ln["dve"])
                nc.vector.scalar_tensor_tensor(at[mine], o[:, mine, :], wt[:, mine:mine + 1], at[mine], ALU.mult, ALU.add)\
                    .then_inc(ev("o_out1"), 1)
                dve.wait_ge(ev("o_out1"), s + 1)
            weights = small[:, 16:24].rearrange("p (s t) -> p s t", s=4)
            for s in range(NBR + 3):
                compressed(s)
                compressed_probs(s)
                if s < NBR:
                    front(s)
                if 1 <= s <= NBR:
                    weigh(s - 1)
                if s >= 3:
                    take_out(s - 3)
                compressed_scores(s)
            first_tiles("out1")
            mean_square(0, hstat[:, 0, :], hstat[:, 1, :], P, "hssq", 1)
            dve.wait_ge(ev("rstd"), 2)
            r = hstat[:, 2, :].rearrange("p (h t o) -> p h t o", t=TT, o=1)
            for t in range(TT):
                o = proj[:, t, C_DQ:C_DQ + HD * P].rearrange("p (h d) -> p h d", h=HD)
                nc.vector.tensor_tensor(o, o, r[:, :, t, :].broadcast_to((P, HD, P)), ALU.mult).then_inc(ev("mixed1"), 1)
            split_turned("mix1")
            tok("out1", False, then_first="up1a")
            residual("out1", 3)
            me(nc.vector.memset(pre[:, :, 0:2], 0.0))
            root_of_x(2, 4)
            split_turned("n2")
            last_up = feat("up1a", True)
            tok("down1a", False, before=last_up)
            last_up = feat("up1b", True, before=nothing)
            dve.wait_ge(ev("acc_free"), 2 + G["down1b"].acc)
            tok("down1b", True, before=last_up, then_first="in2")
            residual("down1b", 5)
            root_of_x(3, 6)
            split_turned("n3")
            tok("in2", False)
            dve.wait_ge(ev("acc_free"), 2 + G["in2"].acc + G["in2"].blocks)
            for v in range(NKV):
                src = proj2[:, :, C_KA + v * 64:C_KA + (v + 1) * 64]
                for u in range(2):
                    last = nc.vector.tensor_copy(kdup[:, :, v, u, :], src)
            last.then_inc(ev("kdup"), 1)
            for m, n in enumerate(TURN2):
                if m % 2:
                    dve.wait_ge(ev("qt2_mm"), m + 1)
                    nc.vector.tensor_scalar(QT2[:, 2 * n:2 * n + 2, :].rearrange("p c s -> p (c s)"), PS[:, m % 8, :],
                                            64 ** -0.5 if n < 4 else 1.0, None, ALU.mult).then_inc(ev("qt2_d"), 1)
            dve.wait_ge(ev("sig"), 1)
            me(nc.vector.tensor_tensor(QT2[:, 16:24, :], QT2[:, 16:24, :], sig_q, ALU.mult))
            dve.wait_ge(ev("sig"), 2)
            for h in range(HR):
                f = QT2[:, 24 + h, :]
                nc.vector.tensor_scalar(f, f, lbs[:, 40 + h:41 + h], lbs[:, 32 + h:33 + h], ALU.mult, ALU.add)
            dve.wait_ge(ev("sig"), 3)
            gr = proj2[:, :, C_GR:C_GR + 1024]
            nc.vector.tensor_tensor(gr, gr, sig_g, ALU.mult).then_inc(ev("f_done"), 1)
            dve.wait_ge(ev("ln_done"), 1)
            nc.vector.tensor_scalar(QT2[:, 24:32, :], QT2[:, 24:32, :], -1.0, 1.0, ALU.mult, ALU.add).then_inc(ev("key_done"), 1)
            dve.wait_ge(ev("mix2_in"), 64)
            me(nc.vector.tensor_scalar(sinks[:, 1, :], sinks[:, 0, :], -1.0, None, ALU.mult))

            def front2(s):
                dve.wait_ge(ev("log_mm2"), s + 1)
                if s >= 2:
                    dve.wait_ge(ev("pt_mm2"), s - 1)
                slope = -(2.0 ** (-8.0 * (s + 1) / HA))
                me(nc.vector.scalar_tensor_tensor(scores2[:, s % 2, :], far[:, :], slope, PS[:, 6, 0:SK], ALU.mult, ALU.add))
                st = stat[:, s % 2, :]
                nc.vector.tensor_reduce(st[:, 0:1], scores2[:, s % 2, 0:P], AX.X, ALU.max, negate=True)
                me(nc.vector.tensor_reduce(st[:, 1:2], scores2[:, s % 2, P:SK], AX.X, ALU.max, negate=True))
                nc.vector.tensor_scalar(st[:, 0:2], st[:, 0:2], sinks[:, 1, s:s + 1], None, ALU.min).then_inc(ev("max2"), 1)

            def weigh2(s):
                dve.wait_ge(ev("exp2"), s + 1)
                st = stat[:, s % 2, :]
                me(nc.vector.tensor_tensor(st[:, 4:6], st[:, 4:6], st[:, 6:8], ALU.add))
                me(nc.vector.reciprocal(wsum[:, s % 4, :], st[:, 4:6]))

            def take_out2(s):
                dve.wait_ge(ev("pv_mm2"), s + 1)
                for t in range(TT):
                    last = nc.vector.tensor_scalar(proj2[:, t, C_QA + s * 64:C_QA + (s + 1) * 64],
                                                   PS[:, 7, SK + t * 64:SK + (t + 1) * 64], wsum[:, s % 4, t:t + 1], None, ALU.mult)
                last.then_inc(ev("o_out2"), 1)
            wsum = lbs[:, 0:8].rearrange("p (s t) -> p s t", s=4)
            NR = HR * TT
            for n in range(NR + 2):
                if n < NR:
                    h, t = n // TT, n % TT
                    dve.wait_ge(ev("fac"), n + 1)
                    if n >= 1:
                        dve.wait_ge(ev("att_mm"), n)
                    q = QT2[:, 16 + h, t * P:(t + 1) * P].rearrange("p (o t) -> p o t", o=1).broadcast_to((P, 8, P))
                    nc.vector.tensor_tensor(qf, fac, q, ALU.mult).then_inc(ev("qf"), 1)
                if 1 <= n <= NR:
                    dve.wait_ge(ev("att_mm"), n)
                    me(nc.vector.tensor_tensor(attm, PS[:, 2:4, :].rearrange("p a (l t) -> p (a l) t", t=P), keep[:, :, :], ALU.mult))
                    if n >= 3:
                        dve.wait_ge(ev("o_mm"), n - 2)
                    nc.vector.tensor_reduce(attT[:, (n - 1) % 2, :], attm.rearrange("p l t -> p t l"), AX.X, ALU.add).then_inc(ev("att_out"), 1)
                if n < HA:
                    front2(n)
                if 1 <= n <= HA:
                    weigh2(n - 1)
                if n >= 2:
                    take_out2(n - 2)
            first_tiles("out2")
            mean_square(0, small[:, 0:2], small[:, 2:4], 1024, "ssq", 4)
            dve.wait_ge(ev("o_out"), NR)
            mean_square(0, hstat[:, 0, :], hstat[:, 1, :], P, "o_out", NR)
            dve.wait_ge(ev("rstd"), 7)
            for t in range(TT):
                o = proj2[:, t, C_QA:C_QA + 1024]
                nc.vector.tensor_scalar(o, o, small[:, 4 + t:5 + t], None, ALU.mult).then_inc(ev("mixed2"), 1)
            dve.wait_ge(ev("rstd"), 8)
            r = hstat[:, 2, :].rearrange("p (h t o) -> p h t o", t=TT, o=1)
            for t in range(TT):
                g = proj2[:, t, C_GR:C_GR + 1024].rearrange("p (h d) -> p h d", h=HR)
                me(nc.vector.tensor_tensor(g, g, r[:, :, t, :].broadcast_to((P, HR, P)), ALU.mult))
                nc.vector.tensor_tensor(proj2[:, t, C_IR:C_IR + 1024], proj2[:, t, C_FR:C_FR + 1024],
                                        proj2[:, t, C_GR:C_GR + 1024], ALU.mult).then_inc(ev("mixed2"), 1)
            split_turned("mix2")
            tok("out2", False, then_first="up2a")
            residual("out2", 9)
            root_of_x(5, 10)
            split_turned("n4")
            last_up = feat("up2a", False)
            tok("down2a", False, before=last_up)
            last_up = feat("up2b", False, before=nothing)
            dve.wait_ge(ev("acc_free"), 2 + G["down2b"].acc)
            tok("down2b", True, before=last_up)
            residual("down2b", 11)

        @block.tensor
        def _(pe):
            def tok(name, lhs, up=None, turned=None, extra=None):
                g, pairs = G[name], PAIRS[name]
                T = g.tiles

                def one(i, b, base):
                    _, nb, bank, wd = place(name, i, b)
                    pe.wait_ge(ev("acc_free"), nb + (g.acc + 1))
                    for j in range(T):
                        if turned is not None and b == 0:
                            pe.wait_ge(ev("actlo_" + turned), max(4, TC * (j + 1)))
                        if up is not None and b == 0 and j == T - (2 if up.startswith("up2") else 1):
                            pe.wait_ge(ev("g_lo"), 1 + G[up].acc + G[up].blocks)
                        s = (b * T + j) % SPLITS
                        pe.wait_ge(ev("lo_done"), base + (j + 1 + STAGES))
                        for c in range(TC):
                            k = TC * j + c
                            h, l = whi[:, s, c * wd:(c + 1) * wd], wlo[:, s, c * wd:(c + 1) * wd]
                            for t in range(TT):
                                o = PS[:, 4 * g.turned + 2 * bank + t, 0:wd]
                                ah, al = lhs[:, k, t * P:(t + 1) * P], lhs[:, k, S + t * P:S + (t + 1) * P]
                                nc.tensor.matmul(o, ah, h, start=k == 0, stop=False)
                                nc.tensor.matmul(o, ah, l, start=False, stop=False)
                                last = nc.tensor.matmul(o, al, h, start=False, stop=k == TC * T - 1)
                        last.then_inc(ev("tile_used"), 1)
                if up is not None:
                    pe.wait_ge(ev("pre_done"), 1 + G[up].acc + G[up].blocks)
                    pe.wait_ge(ev("g_lo"), G[up].acc + G[up].blocks)
                if pairs:
                    with pe.Fori(0, pairs) as i:
                        for b in range(2):
                            one(i, b, i * (2 * T) + (g.first + b * T))
                for b in range(2 * pairs, g.blocks):
                    if extra is not None:
                        extra(b)
                    one(None, b, g.first + b * T)

            def feat(name, down=None, turned=None):
                g = G[name]
                with pe.Fori(0, g.blocks // 2) as r:
                    for s in range(2):
                        i = r * 2 + s
                        pe.wait_ge(ev("pre_done"), i + (g.acc + 1))
                        if s == 1 and down is not None:
                            pe.wait_ge(ev("acc_free"), 2 + G[down].acc + G[down].blocks)
                        for j in range(FT):
                            if turned is not None and s == 0:
                                pe.wait_ge(ev("actlo_" + turned), min(FC * (j + 1), KC))
                            pe.wait_ge(ev("lo_done"), i * FT + (g.first + j + 1 + STAGES))
                            for c in range(FC):
                                k = j % (FT // 2) * FC + c
                                for f in range(2):
                                    o = PS[:, 4 * (s ^ g.turned) + 2 * (j // (FT // 2)) + f, :]
                                    at = slice(c * FW + f * P, c * FW + (f + 1) * P)
                                    nc.tensor.matmul(o, whi[:, j % SPLITS, at], actT[:, k, :], start=k == 0, stop=False)
                                    last = nc.tensor.matmul(o[:, S:2 * S], wlo[:, j % SPLITS, at], actT[:, k, 0:S],
                                                            start=False, stop=k == KC - 1)
                            last.then_inc(ev("tile_used"), 1)

            def turn(name, ready, n):
                pe.wait_ge(ev(ready), n)
                for c in range(KC):
                    for t in range(TT):
                        at = (c % 2) * S + t * P
                        if ready == "diag":
                            last = nc.tensor.matmul(PS[:, c // 2, at:at + P], src_of(name, t, c), diag[:, t, :], start=True, stop=True)
                        else:
                            last = nc.tensor.transpose(PS[:, c // 2, at:at + P], src_of(name, t, c), ident[:, :])
                    if c % 2:
                        last.then_inc(ev("turned_" + name), 1)

            pe.sem_inc(ev("tile_used"), SPLITS)
            pe.wait_ge(ev("tab_in"), 32)
            nc.tensor.matmul(PS[0:16, 5, 0:SK], tab, hot, start=True, stop=True).then_inc(ev("urow_mm"), 1)
            pe.wait_ge(ev("ident_in"), 16)
            pe.wait_ge(ev("vecs_in"), 16 * 7)
            pe.wait_ge(ev("more_vecs_in"), 16 * 7)
            nc.tensor.transpose(PS[:, 7, 0:90], vecs[0:90, 0, :], ident[0:90, 0:90])
            nc.tensor.transpose(PS[:, 7, 128:192], vecs[0:64, 1, :], ident[0:64, 0:64])
            for j in range(4):
                last = nc.tensor.transpose(PS[:, 6, j * P:j * P + 88], vecs[0:88, 2 + j, :], ident[0:88, 0:88])
            last.then_inc(ev("vecs_mm"), 1)
            pe.wait_ge(ev("cols"), 1)

            def bias_rows(b):
                k = b - G["in1"].blocks + 2
                if k >= 0:
                    pe.wait_ge(ev("flip_in"), 16)
                    pe.wait_ge(ev("hankel_in"), 16 * (k + 1))
                    pe.wait_ge(ev("actlo_n1"), KC)
                    if k:
                        pe.wait_ge(ev("bias_done"), 4)
                    for n in range(4):
                        nc.tensor.matmul(PS[:, 4 + n, :], flip, hankel[:, 2 * n:2 * n + 2, :].rearrange("p h j -> p (h j)"),
                                         start=True, stop=True).then_inc(ev("bias_mm"), 1)
            turn("n1", "diag", 2)
            tok("in1", actT, turned="n1", extra=bias_rows)
            pe.wait_ge(ev("acc_free"), 2 + G["in1"].blocks)
            pe.wait_ge(ev("bias_done"), 8)
            COLS = ([C_DQ + c * P for c in range(8)] + [C_DK + c * P for c in range(8)] + [C_NQ + c * P for c in range(8)]
                    + [c0 + g * P for c0 in (C_KC, C_VC, C_KS, C_KW) for g in range(NKV)])
            for m, n in enumerate(TURN1):
                if m >= 8:
                    pe.wait_ge(ev("qt_d" if m % 2 else "qt_a"), (m - 8) // 2 + 1)
                for c in range(2):
                    for t in range(TT):
                        at = COLS[2 * n + c]
                        last = nc.tensor.transpose(PS[:, m % 8, c * S + t * P:c * S + (t + 1) * P],
                                                   proj[:, t, at:at + P], ident[:, :])
                last.then_inc(ev("qt_mm"), 1)
            pe.wait_ge(ev("qt_a"), 8)
            pe.wait_ge(ev("qt_d"), 8)

            def compress(s):
                g = G["cmp"]
                if 1 <= s <= g.tiles // 2:
                    pe.wait_ge(ev("tile_used"), used(g.first + 2 * s))
                    pe.sem_inc(ev("lo_done"), 2)
                if s < g.tiles // 2:
                    v = s // 4
                    pe.wait_ge(ev("blocks_done"), 4 * (v + 1))
                    if v:
                        pe.wait_ge(ev("hid_done"), 1)
                    for j in (2 * s, 2 * s + 1):
                        pe.wait_ge(ev(f"landed{j % STAGES}"), 16 * ((g.first + j) // STAGES + 1))
                        for l in range(FC):
                            k = FC * (j % STAGES) + l
                            for a in range(2):
                                at = stage[:, j % STAGES, l * HID + a * P:l * HID + (a + 1) * P]
                                last = nc.tensor.matmul(PS[:, 6 + a, 0:2 * NC], at,
                                                        blocks[:, v, k, :, :].rearrange("p g c -> p (g c)"),
                                                        start=k == 0, stop=k == CMP_LEN - 1)
                        last.then_inc(ev("tile_used"), 1)
                if s == 8:
                    pe.wait_ge(ev("w2_in"), 32)
                    pe.wait_ge(ev("hid_done"), 2)
                    for a in range(2):
                        nc.tensor.matmul(PS[:, 7, 0:2 * NC], w2[:, 0, a, :], hid[:, 0, a, :], start=a == 0, stop=a == 1)
                    for g in range(NKV):
                        for a in range(2):
                            last = nc.tensor.matmul(PS[0:NC, 7, (2 + g) * P:(3 + g) * P], hid[:, 1, a, g * NC:(g + 1) * NC],
                                                    w2[:, 1, a, :], start=a == 0, stop=a == 1)
                    last.then_inc(ev("kc_mm"), 1)
                if s == 9:
                    pe.wait_ge(ev("kc_out"), 1)
                    for n in range(HN * TT):
                        h, t = n // TT, n % TT
                        g = h // (HN // NKV)
                        last = nc.tensor.matmul(PS[:, 7, n * 16:n * 16 + NC], QT[:, 16 + h, t * P:(t + 1) * P],
                                                kcT[:, g * NC:(g + 1) * NC], start=True, stop=True)
                    last.then_inc(ev("cmp_mm"), 1)
                if s == 10:
                    pe.wait_ge(ev("cmp_probs"), 1)

            def branch(s):
                if s < HD:
                    return [(QT[64 * m:64 * m + 64, s, :], QT[64 * m:64 * m + 64, 8 + s, :]) for m in range(2)], C_DV + s * P
                h, kind = (s - HD) // 2, (s - HD) % 2
                g = h // (HN // NKV)
                return [(QT[:, 16 + h, :], QT[:, 28 + 2 * kind + g, :])], (C_VS, C_VW)[kind] + g * P

            for s in range(NBR + 3):
                if s < NBR:
                    if s >= 2:
                        pe.wait_ge(ev("max1"), s - 1)
                    for m, (q, k) in enumerate(branch(s)[0]):
                        nc.tensor.matmul(PS[:, 2 * (s % 2) + m, 0:P], q[:, 0:P], k[:, 0:P], start=True, stop=True)
                        last = nc.tensor.matmul(PS[:, 2 * (s % 2) + m, P:SK], q[:, P:S], k[:, 0:S], start=True, stop=True)
                    last.then_inc(ev("log_mm1"), 1)
                compress(s)
                if 2 <= s < NBR + 2:
                    r = s - 2
                    pe.wait_ge(ev("probs1"), r + 1)
                    if r >= 1:
                        pe.wait_ge(ev("pt_out1"), r if r <= HD else r - 1)
                    src = probs[:, r % 2, :] if r < HD else scores[:, r % 2, 0, :]
                    for b in range(3):
                        last = nc.tensor.transpose(PS[:, bank_of(4, r), b * P:(b + 1) * P], src[:, b * P:(b + 1) * P], ident[:, :])
                    if r >= HD:
                        last = nc.tensor.transpose(PS[0:NC, bank_of(4, r), SK:SK + P], pcs[:, (r - HD) // 2, (r - HD) % 2, :], ident[:, :])
                    last.then_inc(ev("pt_mm1"), 1)
                if s >= 3:
                    r = s - 3
                    pe.wait_ge(ev("pt_out1"), r + 1)
                    if r >= 1:
                        pe.wait_ge(ev("o_out1"), r if r <= HD else r - 1)
                    v = branch(r)[1]
                    pt, o = probsT[:, r % 2, :], PS[:, bank_of(5, r), :]
                    if r >= HD:
                        nc.tensor.matmul(o[:, 2 * P:3 * P], pcT[:, r % 2, :], vc[:, (r - HD) // HN, :], start=True, stop=True)
                    nc.tensor.matmul(o[:, 0:P], pt[:, 0:P], proj[:, 0, v:v + P], start=True, stop=True)
                    nc.tensor.matmul(o[:, P:2 * P], pt[:, P:2 * P], proj[:, 0, v:v + P], start=True, stop=False)
                    nc.tensor.matmul(o[:, P:2 * P], pt[:, 2 * P:3 * P], proj[:, 1, v:v + P], start=False, stop=True)\
                        .then_inc(ev("pv_mm1"), 1)
            pe.wait_ge(ev("o_out1"), NBR)
            turn("mix1", "mixed1", 2)
            tok("out1", actT, turned="mix1")
            pe.wait_ge(ev("acc_free"), 2 + G["out1"].acc + G["out1"].blocks)
            turn("n2", "diag", 4)
            feat("up1a", turned="n2")
            tok("down1a", gT1, "up1a")
            feat("up1b", "down1a")
            tok("down1b", gT1, "up1b")
            turn("n3", "diag", 6)
            tok("in2", actT, turned="n3")
            pe.wait_ge(ev("acc_free"), 2 + G["in2"].acc + G["in2"].blocks)
            pe.wait_ge(ev("kdup"), 1)
            for m, n in enumerate(TURN2):
                if m >= 8:
                    pe.wait_ge(ev("qt2_d" if m % 2 else "qt2_a"), (m - 8) // 2 + 1)
                for c in range(2):
                    for t in range(TT):
                        if n == 4:
                            src = kdup[:, t, c, :, :].rearrange("p u d -> p (u d)")
                        else:
                            at = C_QA + (2 * n + c) * P if n < 4 else C_QR + (2 * n + c - 16) * P
                            src = proj2[:, t, at:at + P]
                        last = nc.tensor.transpose(PS[:, m % 8, c * S + t * P:c * S + (t + 1) * P], src, ident[:, :])
                last.then_inc(ev("qt2_mm"), 1)
            pe.wait_ge(ev("qt2_a"), 7)
            pe.wait_ge(ev("qt2_d"), 6)
            pe.wait_ge(ev("ln_done"), 1)
            pe.wait_ge(ev("f_done"), 1)
            for n in range(4):
                for k in range(4):
                    h, t = 4 * (n % 2) + k, n // 2
                    last = nc.tensor.transpose(PS[:, n, k * P:(k + 1) * P], lnf[:, h, t * P:(t + 1) * P], ident[:, :])
                last.then_inc(ev("logf_mm"), 1)
            pe.wait_ge(ev("logf_out"), 4)
            def window_scores(s):
                if s >= 1:
                    pe.wait_ge(ev("max2"), s)
                rows = slice(64 * (s % 2), 64 * (s % 2) + 64)
                q, k = QT2[rows, s // 2, :], QT2[rows, 8 + s // (HA // NKV), :]
                nc.tensor.matmul(PS[:, 6, 0:P], q[:, 0:P], k[:, 0:P], start=True, stop=True)
                nc.tensor.matmul(PS[:, 6, P:SK], q[:, P:S], k[:, 0:S], start=True, stop=True).then_inc(ev("log_mm2"), 1)

            def window_turn(r):
                pe.wait_ge(ev("exp2"), r + 1)
                if r >= 1:
                    pe.wait_ge(ev("o_out2"), r)
                for b in range(3):
                    last = nc.tensor.transpose(PS[:, 7, b * P:(b + 1) * P], scores2[:, r % 2, b * P:(b + 1) * P], ident[:, :])
                last.then_inc(ev("pt_mm2"), 1)

            def window_values(r):
                pe.wait_ge(ev("pt_out2"), r + 1)
                v = C_VA + r // (HA // NKV) * 64
                pt, o = probsT2[:, r % 2, :], PS[:, 7, SK:SK + P]
                nc.tensor.matmul(o[:, 0:64], pt[:, 0:P], proj2[:, 0, v:v + 64], start=True, stop=True)
                nc.tensor.matmul(o[:, 64:P], pt[:, P:2 * P], proj2[:, 0, v:v + 64], start=True, stop=False)
                nc.tensor.matmul(o[:, 64:P], pt[:, 2 * P:3 * P], proj2[:, 1, v:v + 64], start=False, stop=True)\
                    .then_inc(ev("pv_mm2"), 1)

            NR = HR * TT
            pe.wait_ge(ev("key_done"), 1)
            pe.wait_ge(ev("mix2_in"), 64)

            def exponents(n):
                h, t = n // TT, n % TT
                if n >= 1:
                    pe.wait_ge(ev("fac"), n)
                lf = logf[:, t, h, :]
                nc.tensor.matmul(PS[:, 0, :], lf, sums[:, 0:4, :].rearrange("p l t -> p (l t)"), start=True, stop=True)
                nc.tensor.matmul(PS[:, 1, 0:3 * P], lf, sums[:, 4:7, :].rearrange("p l t -> p (l t)"), start=True, stop=True)
                nc.tensor.matmul(PS[:, 1, 3 * P:4 * P], lf, sums[:, 7 + t, :], start=True, stop=True).then_inc(ev("exps_mm"), 1)
            exponents(0)
            for n in range(NR + 3):
                if 1 <= n <= NR:
                    r = n - 1
                    h, t = r // TT, r % TT
                    pe.wait_ge(ev("qf"), r + 1)
                    pe.wait_ge(ev("kf"), r + 1)
                    if r >= 1:
                        pe.wait_ge(ev("att_out"), r)
                    if t == 1:
                        pe.wait_ge(ev("kcross_done"), h + 1)
                        if h >= 1:
                            pe.wait_ge(ev("cross_out"), h)
                        nc.tensor.matmul(PS[:, 4, 0:P], kcross[:, :], qf[:, 7, :], start=True, stop=True).then_inc(ev("cross_mm"), 1)
                    for l in range(8):
                        lhs = kf[:, l, :] if l < 7 else QT2[:, 24 + h, t * P:(t + 1) * P]
                        rhs = qf[:, l, :] if l < 7 else QT2[:, 16 + h, t * P:(t + 1) * P]
                        last = nc.tensor.matmul(PS[:, 2 + l // 4, (l % 4) * P:(l % 4 + 1) * P], lhs, rhs, start=True, stop=True)
                    last.then_inc(ev("att_mm"), 1)
                if n < HA:
                    window_scores(n)
                if n >= 3:
                    r = n - 3
                    h, t = r // TT, r % TT
                    pe.wait_ge(ev("att_out"), r + 1)
                    if r >= 1:
                        pe.wait_ge(ev("o_out"), r)
                    v = C_IR + h * P
                    if t == 0:
                        nc.tensor.matmul(PS[:, 5, 0:P], attT[:, r % 2, :], proj2[:, 0, v:v + P], start=True, stop=True).then_inc(ev("o_mm"), 1)
                    else:
                        nc.tensor.matmul(PS[:, 5, 0:P], attT[:, r % 2, :], proj2[:, 1, v:v + P], start=True, stop=False)
                        pe.wait_ge(ev("cross_out"), h + 1)
                        nc.tensor.matmul(PS[:, 5, 0:P], crossT[:, :], proj2[:, 0, v:v + P], start=False, stop=True).then_inc(ev("o_mm"), 1)
                if 2 <= n < HA + 2:
                    window_turn(n - 2)
                if n + 1 < NR:
                    exponents(n + 1)
                if 2 <= n < HA + 2:
                    window_values(n - 2)
            pe.wait_ge(ev("o_out"), NR)
            pe.wait_ge(ev("ssq"), 4)
            turn("mix2", "mixed2", 4)
            tok("out2", actT, turned="mix2")
            pe.wait_ge(ev("acc_free"), 2 + G["out2"].acc + G["out2"].blocks)
            turn("n4", "diag", 8)
            feat("up2a", turned="n4")
            tok("down2a", gT2, "up2a")
            feat("up2b", "down2a")
            tok("down2b", gT2, "up2b")


_INS = ["x", "pre_mix_norm", "w_in", "lambda_q1", "lambda_k1", "lambda_q2", "lambda_k2", "diff_subln", "cmp_pos_k",
        "cmp_pos_v", "cmp_k_w1", "cmp_k_w2", "cmp_v_w1", "cmp_v_w2", "rel_bias", "w_out", "post_mix_norm",
        "pre_ffn_norm", "w_up", "conv_w", "conv_b", "w_down", "post_ffn_norm", "w_in_2", "attn_sinks_2",
        "attn_out_gain_2", "rnn_lb_logits_2", "rnn_norm_gain_2", "w_out_2", "mix_pre_gain_2", "mix_post_gain_2",
        "mlp_pre_gain_2", "mlp_post_gain_2", "w_up_2", "w_down_2"]


def kernel(**inputs):
    import concourse.bacc as bacc
    from concourse.bass_utils import run_bass_kernel_spmd

    nc = bacc.Bacc("TRN2", target_bir_lowering=False, num_devices=1)
    arrays, w = {}, {}
    for name in _INS:
        a = np.ascontiguousarray(inputs[name])
        arrays[f"in_{name}"] = a
        w[name] = nc.dram_tensor(f"in_{name}", a.shape, F32, kind="ExternalInput").ap()
    for name, a in shape_constants().items():
        arrays[f"const_{name}"] = a
        w[name] = nc.dram_tensor(f"const_{name}", a.shape, F32, kind="ExternalInput").ap()
    out = nc.dram_tensor("out", (1, S, D), F32, kind="ExternalOutput").ap()
    scratch = nc.dram_tensor("bias_by_distance", (16, SK), F32, kind="Internal").ap()
    build(nc, w, out, scratch)
    r = run_bass_kernel_spmd(nc, [arrays], core_ids=[0])
    return r.results[0]["out"]
```
